# Optimizing a Trainium2 kernel written in Bass

```python
import jax
import jax.numpy as jnp
from jax import lax
import numpy as np

D_MODEL = 1024
BATCH = 1
SEQ = 256
DEPTH = 1
DEC_BATCH = 1
DEC_SEQ = 64
PAST_LEN = 512

CHUNK = 64
N_META = 16
N_HEADS = 8
N_KV = 2
Q_PER_KV = N_HEADS // N_KV
HEAD_DIM = 64
D_ATTN = N_HEADS * HEAD_DIM
D_KV = N_KV * HEAD_DIM
WINDOW = 128
WIN_CHUNKS = WINDOW // CHUNK
ROPE_DIM = HEAD_DIM // 4
ROPE_THETA = 500000.0
D_RNN = D_MODEL
N_RNN_BLOCKS = 8
RNN_BLOCK = D_RNN // N_RNN_BLOCKS
CONV_W = 4
LRU_C = 8.0
N_GROUPS = 4
EXPERTS_PER_GROUP = 4
N_EXPERTS = N_GROUPS * EXPERTS_PER_GROUP
TOP_K_INNER = 2
D_EXPERT = 512
ALPHA = (2 * DEPTH) ** 0.25
BETA = (8 * DEPTH) ** -0.25
LN_EPS = 1e-5
D_IN = D_ATTN + 2 * D_KV + 2 * D_RNN + 2 * D_MODEL
IN_SPLITS = (D_ATTN, D_ATTN + D_KV, D_ATTN + 2 * D_KV, D_ATTN + 2 * D_KV + D_RNN, D_ATTN + 2 * D_KV + 2 * D_RNN)

kernel_name = 'hybrid_swa_sink_rglru_hmoe_stream_step'

def layer_norm(x, g, b):
    xf = x.astype(jnp.float32)
    mu = jnp.mean(xf, axis=-1, keepdims=True)
    var = jnp.mean(jnp.square(xf - mu), axis=-1, keepdims=True)
    y = (xf - mu) * lax.rsqrt(var + LN_EPS) * g.astype(jnp.float32) + b.astype(jnp.float32)
    return y.astype(x.dtype)

def partial_rope(x, pos):
    half = ROPE_DIM // 2
    inv_freq = ROPE_THETA ** (-jnp.arange(half, dtype=jnp.float32) / half)
    ang = pos.astype(jnp.float32)[:, None] * inv_freq[None, :]
    cos = jnp.cos(ang)[:, None, :]
    sin = jnp.sin(ang)[:, None, :]
    xr = x[..., :ROPE_DIM].astype(jnp.float32)
    x1, x2 = xr[..., :half], xr[..., half:]
    rot = jnp.concatenate([x1 * cos - x2 * sin, x2 * cos + x1 * sin], axis=-1)
    return jnp.concatenate([rot.astype(x.dtype), x[..., ROPE_DIM:]], axis=-1)

def project_in(h, w_in, b_gate, pos):
    B, T, _ = h.shape
    z = h @ w_in
    q, k, v, xr, gr, gl = jnp.split(z, IN_SPLITS, axis=-1)
    q = partial_rope(q.reshape(B, T, N_HEADS, HEAD_DIM), pos)
    k = partial_rope(k.reshape(B, T, N_KV, HEAD_DIM), pos)
    v = v.reshape(B, T, N_KV, HEAD_DIM)
    return q, k, v, xr, gr, gl + b_gate

def sink_attention(q, k, v, mask, sinks):
    B, N, Q = q.shape[:3]
    qg = q.reshape(B, N, Q, N_KV, Q_PER_KV, HEAD_DIM)
    s = jnp.einsum('bnqkgd,bnlkd->bnkgql', qg, k, preferred_element_type=jnp.float32) * (HEAD_DIM ** -0.5)
    s = jnp.where(mask[None, :, None, None], s, -jnp.inf)
    sink = sinks.astype(jnp.float32).reshape(1, 1, N_KV, Q_PER_KV, 1, 1)
    m = jnp.maximum(jnp.max(s, axis=-1, keepdims=True), sink)
    p = jnp.exp(s - m)
    p = p / (jnp.sum(p, axis=-1, keepdims=True) + jnp.exp(sink - m))
    o = jnp.einsum('bnkgql,bnlkd->bnqkgd', p.astype(v.dtype), v)
    return o.reshape(B, N * Q, D_ATTN)

def prompt_attention(q, k, v, sinks):
    B, T = q.shape[:2]
    S = T - N_META
    NC = S // CHUNK
    band = (WIN_CHUNKS + 1) * CHUNK
    o_meta = sink_attention(q[:, None, :N_META], k[:, None, :N_META], v[:, None, :N_META],
                            jnp.ones((1, N_META, N_META), bool), sinks)
    qc = q[:, N_META:].reshape(B, NC, CHUNK, N_HEADS, HEAD_DIM)

    def band_rows(x):
        xc = x[:, N_META:].reshape(B, NC, CHUNK, N_KV, HEAD_DIM)
        xp = jnp.pad(xc, ((0, 0), (WIN_CHUNKS, 0), (0, 0), (0, 0), (0, 0)))
        rows = jnp.concatenate([xp[:, j:j + NC] for j in range(WIN_CHUNKS + 1)], axis=2)
        meta = jnp.broadcast_to(x[:, None, :N_META], (B, NC, N_META, N_KV, HEAD_DIM))
        return jnp.concatenate([meta, rows], axis=2)

    kb, vb = band_rows(k), band_rows(v)
    key_chunk = jnp.arange(NC)[:, None] - WIN_CHUNKS + jnp.arange(band)[None, :] // CHUNK
    mask = jnp.concatenate([jnp.ones((NC, N_META), bool), key_chunk >= 0], axis=1)
    mask = jnp.broadcast_to(mask[:, None, :], (NC, CHUNK, N_META + band))
    o_real = sink_attention(qc, kb, vb, mask, sinks)
    return jnp.concatenate([o_meta, o_real], axis=1)

def rglru_branch(xr, gr, conv_buf, h0, conv_w, conv_b, w_a, b_a, w_x, b_x, lam):
    B, T, _ = xr.shape
    xpad = jnp.concatenate([conv_buf.astype(xr.dtype), xr], axis=1)
    xc = sum(xpad[:, j:j + T] * conv_w[j] for j in range(CONV_W)) + conv_b
    new_buf = xpad[:, -(CONV_W - 1):]
    xb = xc.reshape(B, T, N_RNN_BLOCKS, RNN_BLOCK)
    r = jax.nn.sigmoid((jnp.einsum('btnc,nce->btne', xb, w_a).reshape(B, T, D_RNN) + b_a).astype(jnp.float32))
    i = jax.nn.sigmoid((jnp.einsum('btnc,nce->btne', xb, w_x).reshape(B, T, D_RNN) + b_x).astype(jnp.float32))
    log_a = -LRU_C * r * jax.nn.softplus(-lam.astype(jnp.float32))
    a = jnp.exp(log_a)
    u = jnp.sqrt(-jnp.expm1(2.0 * log_a)) * i * xc.astype(jnp.float32)

    def step(h, au):
        a_t, u_t = au
        h = a_t * h + u_t
        return h, h

    h_last, hs = lax.scan(step, h0.astype(jnp.float32), (jnp.swapaxes(a, 0, 1), jnp.swapaxes(u, 0, 1)))
    y = jnp.swapaxes(hs, 0, 1) * jax.nn.gelu(gr.astype(jnp.float32))
    return y.astype(xr.dtype), new_buf, h_last.astype(xr.dtype)

def merge_branches(attn, rnn, gl, w_pa, w_pr, w_o):
    g = jax.nn.sigmoid(gl)
    g_attn, g_rnn = g[..., :D_MODEL], g[..., D_MODEL:]
    return (g_attn * (attn @ w_pa) + g_rnn * (rnn @ w_pr)) @ w_o

def hier_moe(x, w_group, b_group, w_router, b_router, w_gate, w_up, w_down):
    shp = x.shape
    xt = x.reshape(-1, D_MODEL)
    n = xt.shape[0]
    rows = jnp.arange(n)
    g_logits = (xt @ w_group).astype(jnp.float32) + b_group.astype(jnp.float32)
    g_prob = jax.nn.softmax(g_logits, axis=-1)
    g_idx = jnp.argmax(g_logits, axis=-1)
    g_w = g_prob[rows, g_idx][:, None]
    e_logits = jnp.einsum('nd,dge->nge', xt, w_router).astype(jnp.float32) + b_router.astype(jnp.float32)
    e_sel = e_logits[rows, g_idx]
    top_v, top_i = lax.top_k(e_sel, TOP_K_INNER)
    top_w = jax.nn.softmax(top_v, axis=-1) * g_w
    e_idx = g_idx[:, None] * EXPERTS_PER_GROUP + top_i
    combine = jnp.sum(jax.nn.one_hot(e_idx, N_EXPERTS, dtype=jnp.float32) * top_w[..., None], axis=1)
    y = jnp.zeros((n, D_MODEL), jnp.float32)
    for e in range(N_EXPERTS):
        h = jax.nn.silu(xt @ w_gate[e]) * (xt @ w_up[e])
        y = y + combine[:, e:e + 1] * (h @ w_down[e]).astype(jnp.float32)
    return y.astype(x.dtype).reshape(shp)

def setup_inputs(seed: int = 0) -> dict:
    key = jax.random.key(seed)
    keys = jax.random.split(key, 40)

    def nrm(i, shape, scale):
        return scale * jax.random.normal(keys[i], shape, jnp.float32)

    win_rows = min(WINDOW, PAST_LEN)
    a0 = jax.random.uniform(keys[20], (DEPTH, D_RNN), jnp.float32, 0.9, 0.999)
    s0 = a0 ** (1.0 / LRU_C)
    return {
        'x_prompt': nrm(0, (BATCH, SEQ, D_MODEL), 1.0),
        'x_sample': nrm(1, (DEC_BATCH, DEC_SEQ, D_MODEL), 1.0),
        'cache_meta_k': nrm(2, (DEPTH, DEC_BATCH, N_META, N_KV, HEAD_DIM), 1.0),
        'cache_meta_v': nrm(3, (DEPTH, DEC_BATCH, N_META, N_KV, HEAD_DIM), 1.0),
        'cache_win_k': nrm(4, (DEPTH, DEC_BATCH, win_rows, N_KV, HEAD_DIM), 1.0),
        'cache_win_v': nrm(5, (DEPTH, DEC_BATCH, win_rows, N_KV, HEAD_DIM), 1.0),
        'state_conv': nrm(6, (DEPTH, DEC_BATCH, CONV_W - 1, D_RNN), 1.0),
        'state_h': nrm(7, (DEPTH, DEC_BATCH, D_RNN), 0.5),
        'meta_tokens': nrm(8, (N_META, D_MODEL), 1.0),
        'ln_in_g': 1.0 + nrm(9, (D_MODEL,), 0.02),
        'ln_in_b': nrm(10, (D_MODEL,), 0.02),
        'w_in': nrm(11, (DEPTH, D_MODEL, D_IN), D_MODEL ** -0.5),
        'b_gate': nrm(12, (DEPTH, 2 * D_MODEL), 0.02),
        'attn_sinks': nrm(13, (DEPTH, N_HEADS), 0.5),
        'conv_w': nrm(14, (DEPTH, CONV_W, D_RNN), CONV_W ** -0.5),
        'conv_b': nrm(15, (DEPTH, D_RNN), 0.02),
        'w_rg_a': nrm(16, (DEPTH, N_RNN_BLOCKS, RNN_BLOCK, RNN_BLOCK), RNN_BLOCK ** -0.5),
        'b_rg_a': nrm(17, (DEPTH, D_RNN), 0.02),
        'w_rg_x': nrm(18, (DEPTH, N_RNN_BLOCKS, RNN_BLOCK, RNN_BLOCK), RNN_BLOCK ** -0.5),
        'b_rg_x': nrm(19, (DEPTH, D_RNN), 0.02),
        'lru_lambda': jnp.log(s0) - jnp.log1p(-s0),
        'w_branch_attn': nrm(21, (DEPTH, D_ATTN, D_MODEL), BETA * D_ATTN ** -0.5),
        'w_branch_rnn': nrm(22, (DEPTH, D_RNN, D_MODEL), BETA * D_RNN ** -0.5),
        'w_out': nrm(23, (DEPTH, D_MODEL, D_MODEL), BETA * D_MODEL ** -0.5),
        'ln1_g': 1.0 + nrm(24, (DEPTH, D_MODEL), 0.02),
        'ln1_b': nrm(25, (DEPTH, D_MODEL), 0.02),
        'w_group': nrm(26, (DEPTH, D_MODEL, N_GROUPS), D_MODEL ** -0.5),
        'b_group': nrm(27, (DEPTH, N_GROUPS), 0.01),
        'w_router': nrm(28, (DEPTH, D_MODEL, N_GROUPS, EXPERTS_PER_GROUP), D_MODEL ** -0.5),
        'b_router': nrm(29, (DEPTH, N_GROUPS, EXPERTS_PER_GROUP), 0.01),
        'w_gate': nrm(30, (DEPTH, N_EXPERTS, D_MODEL, D_EXPERT), D_MODEL ** -0.5),
        'w_up': nrm(31, (DEPTH, N_EXPERTS, D_MODEL, D_EXPERT), D_MODEL ** -0.5),
        'w_down': nrm(32, (DEPTH, N_EXPERTS, D_EXPERT, D_MODEL), BETA * D_EXPERT ** -0.5),
        'ln2_g': 1.0 + nrm(33, (DEPTH, D_MODEL), 0.02),
        'ln2_b': nrm(34, (DEPTH, D_MODEL), 0.02),
    }

def reference(x_prompt, x_sample, cache_meta_k, cache_meta_v, cache_win_k, cache_win_v, state_conv, state_h,
              meta_tokens, ln_in_g, ln_in_b, w_in, b_gate, attn_sinks, conv_w, conv_b, w_rg_a, b_rg_a,
              w_rg_x, b_rg_x, lru_lambda, w_branch_attn, w_branch_rnn, w_out, ln1_g, ln1_b, w_group, b_group,
              w_router, b_router, w_gate, w_up, w_down, ln2_g, ln2_b):
    B, S, _ = x_prompt.shape
    DB, TS, _ = x_sample.shape
    T = N_META + S
    meta = jnp.broadcast_to(meta_tokens.astype(x_prompt.dtype)[None], (B, N_META, D_MODEL))
    z_p = layer_norm(jnp.concatenate([meta, x_prompt], axis=1), ln_in_g, ln_in_b)
    z_s = layer_norm(x_sample, ln_in_g, ln_in_b)
    pos_p = jnp.arange(T)
    pos_s = N_META + PAST_LEN + jnp.arange(TS)
    win_p = min(WINDOW, S)
    mk_p, mv_p, wk_p, wv_p, cv_p, hh_p = [], [], [], [], [], []
    nk_s, nv_s, cv_s, hh_s = [], [], [], []
    for l in range(DEPTH):
        q, k, v, xr, gr, gl = project_in(z_p, w_in[l], b_gate[l], pos_p)
        attn = prompt_attention(q, k, v, attn_sinks[l])
        rnn, conv_new, h_new = rglru_branch(
            xr, gr, jnp.zeros((B, CONV_W - 1, D_RNN), xr.dtype), jnp.zeros((B, D_RNN), jnp.float32),
            conv_w[l], conv_b[l], w_rg_a[l], b_rg_a[l], w_rg_x[l], b_rg_x[l], lru_lambda[l])
        mix = merge_branches(attn, rnn, gl, w_branch_attn[l], w_branch_rnn[l], w_out[l])
        z_p = layer_norm(ALPHA * z_p + mix, ln1_g[l], ln1_b[l])
        z_p = layer_norm(ALPHA * z_p + hier_moe(z_p, w_group[l], b_group[l], w_router[l], b_router[l],
                                                w_gate[l], w_up[l], w_down[l]), ln2_g[l], ln2_b[l])
        mk_p.append(k[:, :N_META])
        mv_p.append(v[:, :N_META])
        wk_p.append(k[:, T - win_p:])
        wv_p.append(v[:, T - win_p:])
        cv_p.append(conv_new)
        hh_p.append(h_new)
        q, k, v, xr, gr, gl = project_in(z_s, w_in[l], b_gate[l], pos_s)
        k_all = jnp.concatenate([cache_meta_k[l].astype(k.dtype), cache_win_k[l].astype(k.dtype), k], axis=1)
        v_all = jnp.concatenate([cache_meta_v[l].astype(v.dtype), cache_win_v[l].astype(v.dtype), v], axis=1)
        attn = sink_attention(q[:, None], k_all[:, None], v_all[:, None],
                              jnp.ones((1, TS, k_all.shape[1]), bool), attn_sinks[l])
        rnn, conv_new, h_new = rglru_branch(
            xr, gr, state_conv[l], state_h[l],
            conv_w[l], conv_b[l], w_rg_a[l], b_rg_a[l], w_rg_x[l], b_rg_x[l], lru_lambda[l])
        mix = merge_branches(attn, rnn, gl, w_branch_attn[l], w_branch_rnn[l], w_out[l])
        z_s = layer_norm(ALPHA * z_s + mix, ln1_g[l], ln1_b[l])
        z_s = layer_norm(ALPHA * z_s + hier_moe(z_s, w_group[l], b_group[l], w_router[l], b_router[l],
                                                w_gate[l], w_up[l], w_down[l]), ln2_g[l], ln2_b[l])
        nk_s.append(k)
        nv_s.append(v)
        cv_s.append(conv_new)
        hh_s.append(h_new.astype(state_h.dtype))
    y_prompt = z_p[:, N_META:]
    y_sample = z_s
    meta_k_p = jnp.stack(mk_p, axis=0)
    meta_v_p = jnp.stack(mv_p, axis=0)
    win_k_p = jnp.stack(wk_p, axis=0)
    win_v_p = jnp.stack(wv_p, axis=0)
    conv_p = jnp.stack(cv_p, axis=0)
    h_p = jnp.stack(hh_p, axis=0)
    new_k_s = jnp.stack(nk_s, axis=0)
    new_v_s = jnp.stack(nv_s, axis=0)
    conv_s = jnp.stack(cv_s, axis=0)
    h_s = jnp.stack(hh_s, axis=0)
    return (y_prompt, y_sample, meta_k_p, meta_v_p, win_k_p, win_v_p, conv_p, h_p, new_k_s, new_v_s, conv_s, h_s)


_drawn_inputs = setup_inputs


def setup_inputs(seed=0):
    import zlib

    import numpy as np

    out = dict(_drawn_inputs(seed))
    spreads = {}
    factors = {'cache_meta_k': 5.906,
     'cache_meta_v': 8.0,
     'cache_win_k': 4.802,
     'cache_win_v': 3.869,
     'b_gate': 8.0,
     'attn_sinks': 64.0,
     'b_rg_a': 8.0,
     'b_rg_x': 7.805,
     'b_group': 18.352,
     'b_router': 25.609,
     'ln2_g': 8.007,
     'ln2_b': 8.066}
    for name, (base, spread) in spreads.items():
        noise = np.random.default_rng([zlib.crc32(name.encode()), seed]).standard_normal(out[name].shape)
        drawn = base * np.exp(spread * noise) if base else spread * noise
        out[name] = jnp.asarray(drawn.astype(out[name].dtype))
    for name, factor in factors.items():
        out[name] = (out[name] * factor).astype(out[name].dtype)
    return out
```

```python
from contextlib import ExitStack

import numpy as np

import concourse.bass as bass
from concourse import mybir

F32 = mybir.dt.float32
I32 = mybir.dt.int32
ALU = mybir.AluOpType
ACT = mybir.ActivationFunctionType
AX_X = mybir.AxisListType.X

P = 128
D = 1024
KD = D // P
SEQ, DEC, META = 256, 64, 16
NTOK = SEQ + DEC
NALL = NTOK + META
CHUNK, WIN = 64, 128
NH, NKV, HD = 8, 2, 64
HPK = NH // NKV
ROT = HD // 4
HALF = ROT // 2
THETA = 500000.0
LRU_C = 8.0
PAST = 512
CONVW = 4
QKV = (NH + 2 * NKV) * HD
ALPHA = 2.0 ** 0.25
EPS = 1e-5
NG, EPG = 4, 4
NE = NG * EPG
FE = 512
KF = FE // P
TILE_ROWS = (128, 128, DEC + META)
OUT_ROWS = (128, 128, DEC)
TP = META + SEQ
GAP = CONVW - 1
TW = TP + GAP + DEC
XPAD = TW + GAP
CAP = 80
LEVELS = NTOK // CAP
NOV = 2 * NTOK // (CAP + 1) if CAP else 0
NOV = min(NOV, 8)
NITEM = NE + NOV
UNIT = KD * 256
RING = 6
U_QKV, U_XR, U_RG, U_GR, U_MERGE, U_OUT = 0, 3, 7, 8, 12, 28
NUNIT = 32
C_XR = QKV
C_GR = C_XR + D
C_GL = C_GR + D


def const_layout():
    cols, at = {}, 0
    for name, n in (("ident", P), ("before", P), ("ones", P), ("cos", 3 * HALF), ("sin", 3 * HALF),
                    ("iota_cap", CAP), ("iota_item", NITEM), ("iota_ov", NOV), ("expert", NE),
                    ("level", LEVELS), ("tie", 4), ("token", 3), ("valid", 3), ("eps", 1)):
        cols[name] = (at, at + n)
        at += n
    return cols, at


CC, NCONST = const_layout()


def constants():
    c = np.zeros((P, NCONST), np.float32)

    def put(name, v):
        c[:, CC[name][0]:CC[name][1]] = v

    row = np.arange(P)
    put("ident", np.eye(P))
    put("before", (row[:, None] < row[None, :]).astype(np.float32))
    put("ones", 1.0)
    pos = np.zeros((P, 3), np.float32)
    pos[:, 0] = META + row
    pos[:, 1] = META + P + row
    pos[:DEC, 2] = META + PAST + row[:DEC]
    pos[DEC:DEC + META, 2] = row[:META]
    inv = np.float32(THETA) ** (-np.arange(HALF, dtype=np.float32) / np.float32(HALF))
    ang = pos[:, :, None] * inv.astype(np.float32)[None, None, :]
    put("cos", np.cos(ang).reshape(P, -1))
    put("sin", np.sin(ang).reshape(P, -1))
    put("iota_cap", np.arange(CAP))
    put("iota_item", np.arange(NITEM))
    put("iota_ov", np.arange(NOV))
    put("expert", np.arange(NE))
    put("level", CAP * (1 + np.arange(LEVELS)))
    put("tie", [4, 3, 2, 1])
    valid = np.array([[float(p < OUT_ROWS[j]) for j in range(3)] for p in range(P)])
    put("valid", valid)
    put("token", valid * (row[:, None] + P * np.arange(3)[None, :]))
    put("eps", EPS)
    return c


VEC = {}
_at = 0
for _n, _k in (("conv_w", CONVW * KD), ("conv_b", KD), ("b_a", KD), ("b_x", KD), ("lam", KD),
               ("state_h", KD), ("state_conv", GAP * KD), ("b_gate", 2 * KD)):
    VEC[_n] = (_at, _at + _k)
    _at += _k
NVEC = _at


class Ring:

    def __init__(self, banks, full, free, names):
        self.banks, self.full, self.free = banks, full, free
        self.index = {n: i for i, n in enumerate(names)}

    def bank(self, name):
        return self.banks[self.index[name] % len(self.banks)]

    def sems(self, name):
        i = self.index[name]
        n = len(self.banks)
        return self.full[i % n], self.free[i % n], i // n

    def claim(self, eng, name):
        _, free, n = self.sems(name)
        if n >= 1:
            eng.wait_ge(free, n)
        return self.bank(name)

    def arrived(self, eng, name):
        full, _, n = self.sems(name)
        eng.wait_ge(full, n + 1)
        return self.bank(name)

    def emptied(self, eng, name):
        _, free, n = self.sems(name)
        eng.wait_ge(free, n + 1)

    def f_full(self, name):
        return self.sems(name)[0]

    def f_free(self, name):
        return self.sems(name)[1]


class Steps:

    def __init__(self, eng, sem):
        self.eng, self.sem, self.n = eng, sem, 0

    def __call__(self, inst):
        inst.then_inc(self.sem, 1)
        self.n += 1
        return self.n

    def settle(self):
        self.eng.wait_ge(self.sem, self.n)


def wait_past(eng, sem, n):
    if not (isinstance(n, int) and n == 0):
        eng.wait_ge(sem, n)


CHUNKS = 5


def chunk_keys(c):
    lo = max(0, (c - 2) * CHUNK)
    hi = (c + 1) * CHUNK
    return lo, hi, lo % P


def chunk_blocks(c):
    if c == 4:
        return [(0, P), (P, DEC + META)]
    lo, hi, off = chunk_keys(c)
    out, at, end = [], 0, off + hi - lo
    while at < end:
        out.append((at, min(P, end - at)))
        at += P
    return out + [(end, META)]


def pe_fills():
    m, s = [], []
    s.append("vec")
    for j in range(3):
        s += [("zT", j, h) for h in range(2)]
        m += [("qkv", j, u) for u in range(3)]
    m += [("xr", c) for c in range(KD)]
    m += [("QT", j) for j in range(3)] + ["KT", "KS"]
    for c in range(KD):
        m += [("r", c), ("i", c)]
    gr = iter(range(KD))
    for c in range(CHUNKS + 1):
        if c < CHUNKS:
            s += [("S", c, g) for g in range(4)]
        if c >= 1:
            m += [("PT", c - 1, b) for b in range(len(chunk_blocks(c - 1)))] + [("PV", c - 1)]
        for _ in range(GR_AFTER[c]):
            m.append(("gr", next(gr)))
    for mm in range(KD):
        m += [("ga", mm), ("gr_gate", mm), ("pa", mm), ("pr", mm)]
    s.append("tail")
    for kind, j in OUT_ORDER:
        s += [(kind, j, h) for h in range(2)]
    s += ["logits", "ranks", "index"]
    return m, s


OUT_ORDER = (("out", 0), ("out", 1), ("z1T", 0), ("out", 2), ("z1T", 1), ("z1T", 2))
GR_AFTER = [2, 2, 1, 1, 2, 0]


def build(nc, t, outs):
    (y_prompt, y_sample, meta_k, meta_v, win_k, win_v, conv_p, h_p, new_k, new_v, conv_s, h_s) = outs
    with ExitStack() as ctx:
        def sb(name, shape, dt=F32):
            return ctx.enter_context(nc.sbuf_tensor(name, shape, dt))

        def sem(name):
            return ctx.enter_context(nc.semaphore(name))

        EXP = KD * FE + KD * FE + KF * D
        slots = sb("expert_slots", [P, 3 * EXP])
        NWORK = 3 * D + KD * (NALL + META) + 2 * KD * NTOK + 4 * NTOK + 160
        work = sb("work", [P, NWORK])
        const = sb("const", [P, NCONST])
        small = sb("small", [P, 900])
        index_i = sb("index_i", [P, NITEM], I32)
        slot_i = sb("slot_i", [P, 2, 3], I32)
        ctrl_i = sb("ctrl_i", [P, NOV + 1], I32)

        class Area:
            def __init__(self, tensor, base, end):
                self.t, self.at, self.end = tensor, base, end

            def take(self, *dims):
                n = int(np.prod(dims))
                ap = self.t[:, self.at:self.at + n]
                self.at += n
                assert self.at <= self.end, (self.at, self.end)
                if len(dims) == 2:
                    ap = ap.rearrange("p (a b) -> p a b", b=dims[1])
                if len(dims) == 3:
                    ap = ap.rearrange("p (a b c) -> p a b c", b=dims[1], c=dims[2])
                return ap

        def cst(name):
            return const[:, CC[name][0]:CC[name][1]]

        ident, before, ones = cst("ident"), cst("before"), cst("ones")

        scr = Area(slots, 0, 2 * EXP)
        qkv = scr.take(3, QKV)
        qT = scr.take(CHUNKS, 4 * CHUNK)
        kT = scr.take(NALL)
        kTs = scr.take(WIN + DEC + META)
        vM, vS, vW = scr.take(P), scr.take(P), scr.take(P)
        kW, kS = scr.take(P), scr.take(P)
        prob = [scr.take(4, 272), scr.take(4, 272)]
        pT = scr.take(3, 512)
        xpad = scr.take(KD, XPAD)
        xc = scr.take(KD, TW)
        dec = scr.take(KD, TW)
        inp = scr.take(KD, TW)
        gate_i = scr.take(KD, TW)
        th_r = scr.take(2, TW)
        den = scr.take(2, TW)
        gel = [scr.take(NTOK) for _ in range(2)]
        ring = [slots[:, 2 * EXP + i * UNIT:2 * EXP + (i + 1) * UNIT] for i in range(RING)]
        w_gate = [slots[:, i * EXP:i * EXP + KD * FE].rearrange("p (k f) -> p k f", f=FE) for i in range(3)]
        w_up = [slots[:, i * EXP + KD * FE:i * EXP + 2 * KD * FE].rearrange("p (k f) -> p k f", f=FE)
                for i in range(3)]
        w_down = [slots[:, i * EXP + 2 * KD * FE:(i + 1) * EXP].rearrange("p (k f) -> p k f", f=D)
                  for i in range(3)]

        area = Area(work, 0, NWORK)
        rows = area.take(3, D)
        zT = area.take(KD, NALL + META)
        rnnT = area.take(KD, NTOK)
        attnT = area.take(4, NTOK)
        merged = area.take(KD, NTOK)
        z1T = rnnT
        ea = Area(work, 3 * D, NWORK)
        xg = [ea.take(D) for _ in range(3)]
        xT = [ea.take(KD, CAP) for _ in range(3)]
        hT = [ea.take(KF, CAP) for _ in range(3)]
        yo = [ea.take(D) for _ in range(3)]
        htmp = [ea.take(CAP) for _ in range(KF)]
        gb = sb("norm_rows", [P, 2, D])
        mtmp = [[gb[:, i, NTOK * w:NTOK * w + NTOK] for w in range(2)] for i in range(2)]
        fin = Area(slots, 0, 3 * EXP)
        yg = [[fin.take(D) for _ in range(2)] for _ in range(3)]

        sm = Area(small, 0, 900)
        vrow = sm.take(P)
        vcol = sm.take(NVEC)
        stage = sm.take(64)
        stage_rows = sm.take(P)
        sink = sm.take(4)
        stats = sm.take(3, 12)
        mv = sm.take(3, 2)
        rstd = sm.take(3)
        hba, hbx = sm.take(KD), sm.take(KD)
        hbg = sm.take(2 * KD)
        sp4, nsp4 = sm.take(KD), sm.take(KD)
        sp_t = [sm.take(KD) for _ in range(6)]
        mx, m_c, nm, es, rs, dn, rd = [sm.take(2, 4) for _ in range(7)]
        wr = sb("router", [P, KD, 20])
        br = sb("router_bias", [1, 20])
        rt = Area(work, 3 * D + KD * (NALL + META) + KD * NTOK + 4 * NTOK, NWORK)
        logit = rt.take(3, 20)
        e_sum = rt.take(3, NE)
        rank_hot = rt.take(2, 3 * CAP)
        item_hot = rt.take(2, 3 * NITEM)
        weight = [sm.take(3) for _ in range(2)]
        exi, exo = rt.take(15), rt.take(15)
        g_top, tie_top, slot_f = rt.take(3), rt.take(3), rt.take(3)
        top, item_of, rank_of = ([rt.take(3) for _ in range(2)] for _ in range(3))
        g_hot, e_sel = rt.take(3, 4), rt.take(3, 4)
        hot = [rt.take(3, 4) for _ in range(2)]
        cross = rt.take(3, 4, 4)
        e_hot = [rt.take(3, NE) for _ in range(2)]
        e_sum2, rank, level, where = (rt.take(3, NE) for _ in range(4))
        count_e, ov, ov_end, base = (rt.take(NE) for _ in range(4))
        ov_cmp, ov_exp = rt.take(NOV, NE), rt.take(NOV)
        eps = cst("eps")

        def vc(name, i, n=1):
            return vcol[:, VEC[name][0] + i:VEC[name][0] + i + n]

        banks = [ctx.enter_context(nc.psum_tensor(f"bank{i}", [P, 512], F32)) for i in range(8)]
        names_m, names_s = pe_fills()
        M = Ring(banks[0:4], [sem(f"m_full{i}") for i in range(4)], [sem(f"m_free{i}") for i in range(4)], names_m)
        S = Ring(banks[4:8], [sem(f"s_full{i}") for i in range(4)], [sem(f"s_free{i}") for i in range(4)], names_s)

        TB, HB, YB = banks[0:2], banks[2:4] + banks[6:8], banks[4:6]
        z1_dram = nc.dram_tensor("z1_rows", [NTOK, D], F32, kind="Internal")
        y_dram = nc.dram_tensor("expert_rows", [NITEM * CAP, D], F32, kind="Internal")

        const_in = sem("const_in")
        lam_ready, lam_exp, cols_ready = sem("lam_ready"), sem("lam_exp"), sem("cols_ready")
        x_in = [sem(f"x_in{j}") for j in range(3)]
        norm_in = sem("norm_in")
        vec_in = sem("vec_in")
        sink_in = sem("sink_in")
        cache_in = sem("cache_in")
        vm_in = sem("vm_in")
        router_in = sem("router_in")
        unit_in = [sem(f"unit_in{i}") for i in range(RING)]
        dve_step, act_step, pool_step = sem("dve_step"), sem("act_step"), sem("pool_step")
        var_ready = sem("var_ready")
        std_ready = sem("std_ready")
        rows_ready = sem("rows_ready")
        scaled = sem("scaled")
        roped = sem("roped")
        side_keys = sem("side_keys")
        conv_made = sem("conv_made")
        gate_prod = sem("gate_prod")
        sqrt_made = sem("sqrt_made")
        max_ready = sem("max_ready")
        exp_made = sem("exp_made")
        prob_ready = sem("prob_ready")
        gelu_sq, gelu_cube, gelu_tanh = [sem(f"gelu_{n}") for n in ("sq", "cube", "tanh")]
        rnn_made = sem("rnn_made")
        tail_staged = sem("tail_staged")
        merge_made = sem("merge_made")
        kv_out = sem("kv_out")
        tail_out = sem("tail_out")
        z1_out = sem("z1_out")
        lg_exp_in, lg_exp = sem("lg_exp_in"), sem("lg_exp")
        chosen = sem("chosen")
        selected = sem("selected")
        route_done = sem("route_done")
        zeroed, zero_out = sem("zeroed"), sem("zero_out")
        ctrl_done = sem("ctrl_done")
        rows_scaled2 = sem("rows_scaled2")
        g_in = [sem(f"gate_in{i}") for i in range(3)]
        u_in = [sem(f"up_in{i}") for i in range(3)]
        d_in = [sem(f"down_in{i}") for i in range(3)]
        xg_in = [sem(f"xg_in{i}") for i in range(3)]
        xt_half = sem("xt_half")
        hid_full = sem("hid_full")
        hid_tanh = sem("hid_tanh")
        hid_mul = sem("hid_mul")
        hid_made = sem("hid_made")
        y_full = sem("y_full")
        y_made = sem("y_made")
        y_out = [sem(f"y_out{i}") for i in range(3)]
        xt_full = sem("xt_full")
        yg_in = [sem(f"yg_in{j}") for j in range(3)]
        out_done = sem("out_done")

        def unit_consumed(eng, u):
            if u < U_XR:
                M.arrived(eng, ("qkv", 2, u))
            elif u < U_RG:
                M.arrived(eng, ("xr", 2 * (u - U_XR) + 1))
            elif u == U_RG:
                M.arrived(eng, ("i", KD - 1))
            elif u < U_MERGE:
                M.arrived(eng, ("gr", 2 * (u - U_GR) + 1))
            elif u < U_OUT:
                M.arrived(eng, (("ga", "gr_gate", "pa", "pr")[(u - U_MERGE) % 4], 2 * ((u - U_MERGE) // 4) + 1))
            else:
                S.arrived(eng, ("out", 2, (u - U_OUT) // 2))

        def unit_loaded(eng, u):
            n = 0
            for v in range(u % RING, u + 1, RING):
                n += 32 if v == U_RG or (U_MERGE <= v < U_OUT and (v - U_MERGE) % 4 == 2) else 16
            eng.wait_ge(unit_in[u % RING], n)

        block = ctx.enter_context(nc.Block())

        @block.sync
        def _(sp):
            w_in = t["w_in"][0].rearrange("(k p) n -> p k n", p=P)
            w_pa, w_pr, w_o = t["w_branch_attn"][0], t["w_branch_rnn"][0], t["w_out"][0]
            xp, xs = t["x_prompt"][0], t["x_sample"][0]
            sp.dma_start(rows[:, 0, :], xp[0:P, :]).then_inc(x_in[0], 16)
            sp.dma_start(rows[:, 1, :], xp[P:2 * P, :]).then_inc(x_in[1], 16)
            sp.dma_start(rows[0:DEC, 2, :], xs).then_inc(x_in[2], 16)
            sp.dma_start(rows[DEC:DEC + META, 2, :], t["meta_tokens"]).then_inc(x_in[2], 16)

            def unit(u):
                if u >= RING:
                    unit_consumed(sp, u - RING)
                dst, done = ring[u % RING], unit_in[u % RING]
                wide = dst.rearrange("p (k n) -> p k n", n=256)
                if u == U_RG:
                    half = dst.rearrange("p (w n e) -> p w n e", w=2, e=P)
                    sp.dma_start(half[:, 0], t["w_rg_a"][0].rearrange("n c e -> c n e")).then_inc(done, 16)
                    sp.dma_start(half[:, 1], t["w_rg_x"][0].rearrange("n c e -> c n e")).then_inc(done, 16)
                elif u < U_MERGE:
                    col = 256 * u if u < U_RG else C_GR + 256 * (u - U_GR)
                    sp.dma_start(wide, w_in[:, :, col:col + 256]).then_inc(done, 16)
                elif u < U_OUT:
                    mp, kind = divmod(u - U_MERGE, 4)
                    cols = slice(256 * mp, 256 * mp + 256)
                    if kind < 2:
                        col = C_GL + D * kind + 256 * mp
                        sp.dma_start(wide, w_in[:, :, col:col + 256]).then_inc(done, 16)
                    elif kind == 2:
                        for g in range(NKV):
                            src = w_pa[256 * g:256 * g + 256, cols].rearrange("(c d) n -> d c n", d=HD)
                            sp.dma_start(wide[HD * g:HD * g + HD, 0:4], src).then_inc(done, 16)
                    else:
                        sp.dma_start(wide, w_pr[:, cols].rearrange("(k p) n -> p k n", p=P)).then_inc(done, 16)
                else:
                    c = 256 * (u - U_OUT)
                    sp.dma_start(wide, w_o[:, c:c + 256].rearrange("(k p) n -> p k n", p=P)).then_inc(done, 16)

            def expert(e, s):
                sp.dma_start(w_gate[s], t["w_gate"][0, e].rearrange("(k p) f -> p k f", p=P)).then_inc(g_in[s], 16)
                sp.dma_start(w_up[s], t["w_up"][0, e].rearrange("(k p) f -> p k f", p=P)).then_inc(u_in[s], 16)
                sp.dma_start(w_down[s], t["w_down"][0, e].rearrange("(k p) f -> p k f", p=P)).then_inc(d_in[s], 16)

            def expert_dyn(e, s):
                sp.dma_start(w_gate[s], t["w_gate"][0, bass.ds(e, 1)].rearrange("o (k p) f -> p (o k) f", p=P))\
                    .then_inc(g_in[s], 16)
                sp.dma_start(w_up[s], t["w_up"][0, bass.ds(e, 1)].rearrange("o (k p) f -> p (o k) f", p=P))\
                    .then_inc(u_in[s], 16)
                sp.dma_start(w_down[s], t["w_down"][0, bass.ds(e, 1)].rearrange("o (k p) f -> p (o k) f", p=P))\
                    .then_inc(d_in[s], 16)

            for u in range(U_MERGE + 8):
                unit(u)
            sp.wait_ge(rnn_made, 4)
            M.emptied(sp, ("PV", CHUNKS - 1))
            sp.wait_ge(tail_staged, 1)
            sp.wait_ge(kv_out, 16 * 6)
            expert(0, 0)
            for u in range(U_MERGE + 8, U_MERGE + 12):
                unit(u)
            expert(1, 1)
            for u in range(U_MERGE + 12, NUNIT):
                unit(u)
            for u in range(NUNIT - RING, NUNIT):
                unit_consumed(sp, u)
            expert(2, 2)
            with sp.Fori(1, NE // 3) as n:
                for s in range(3):
                    sp.wait_ge(y_full, 3 * n + (s - 2))
                    expert_dyn(3 * n + s, s)
            sp.wait_ge(y_full, NE - 3)
            expert(NE - 1, 0)
            sp.wait_ge(ctrl_done, 1)
            count = sp.value_load(ctrl_i[0:1, NOV:NOV + 1], min_val=0, max_val=NOV)
            with sp.If(count > 0):
                with sp.Fori(0, count) as v:
                    sp.wait_ge(y_full, v + NE)
                    e = sp.value_load(ctrl_i[0:1, bass.ds(v, 1)], min_val=0, max_val=NE - 1)
                    expert_dyn(e, 1)
            for j, dst in enumerate((y_prompt[0, 0:P, :], y_prompt[0, P:SEQ, :], y_sample[0])):
                sp.wait_ge(rows_ready, 7 + j)
                sp.dma_start(dst, rows[0:OUT_ROWS[j], j, :]).then_inc(out_done, 16)
            sp.wait_ge(out_done, 48)
            sp.wait_ge(kv_out, 96)
            sp.wait_ge(tail_out, 64)

        @block.gpsimd
        def _(pool):
            pool.dma_start(const[:], t["const"]).then_inc(const_in, 16)
            for name, key, spec in (("conv_w", "conv_w", "j (c p) -> (j c) p"), ("state_conv", "state_conv", "j (c p) -> (j c) p")):
                a, b = VEC[name]
                src = t[key][0] if name == "conv_w" else t[key][0, 0]
                pool.dma_start(vrow[a:b, :], src.rearrange(spec, p=P)).then_inc(vec_in, 16)
            for name, key in (("conv_b", "conv_b"), ("b_a", "b_rg_a"), ("b_x", "b_rg_x"), ("lam", "lru_lambda"),
                              ("b_gate", "b_gate")):
                a, b = VEC[name]
                pool.dma_start(vrow[a:b, :], t[key][0].rearrange("(c p) -> c p", p=P)).then_inc(vec_in, 16)
            a, b = VEC["state_h"]
            pool.dma_start(vrow[a:b, :], t["state_h"][0, 0].rearrange("(c p) -> c p", p=P)).then_inc(vec_in, 16)
            for h in range(2):
                src = t["attn_sinks"][0].rearrange("(c h) -> h c", h=2)[h:h + 1, :].to_broadcast([HD, 4])
                pool.dma_start(sink[HD * h:HD * h + HD, :], src, allow_slow_non_contiguous=True).then_inc(sink_in, 16)
            flat = "r h d -> r (h d)"
            pool.dma_start(kW, t["cache_win_k"][0, 0].rearrange(flat)).then_inc(cache_in, 16)
            pool.dma_start(vW, t["cache_win_v"][0, 0].rearrange(flat)).then_inc(cache_in, 16)
            pool.dma_start(kS[DEC:DEC + META, :], t["cache_meta_k"][0, 0].rearrange(flat)).then_inc(cache_in, 16)
            pool.dma_start(vS[DEC:DEC + META, :], t["cache_meta_v"][0, 0].rearrange(flat)).then_inc(cache_in, 16)
            nc.gpsimd.memset(merged[:, 0:4, :].rearrange("p k n -> p (k n)")[:, 0:D], 0.0).then_inc(zeroed, 1)
            pool.wait_ge(zeroed, 1)
            left = NOV * CAP
            while left:
                n = min(left, 112)
                at = NITEM * CAP - left
                pool.dma_start(y_dram[at:at + n, :], merged[0:n, 0:4, :].rearrange("p k n -> p (k n)")[:, 0:D])\
                    .then_inc(zero_out, 16)
                left -= n
            for j in range(3):
                for h in range(2):
                    S.emptied(pool, ("zT", j, h))
            for j in range(3):
                n = TILE_ROWS[j]
                nc.gpsimd.tensor_scalar(rows[0:n, j, :], rows[0:n, j, :], ALPHA, None, ALU.mult).then_inc(scaled, 1)
            M.emptied(pool, ("qkv", 2, 2))
            pool.dma_start(vM[0:META, :], qkv[DEC:DEC + META, 2, QKV - P:QKV]).then_inc(vm_in, 16)
            pool.wait_ge(roped, 3)
            nc.gpsimd.tensor_copy(kS[0:DEC, :], qkv[0:DEC, 2, NH * HD:NH * HD + P]).then_inc(side_keys, 1)
            nc.gpsimd.tensor_copy(vS[0:DEC, :], qkv[0:DEC, 2, QKV - P:QKV]).then_inc(side_keys, 1)
            for ko, vo, j, lo, n in ((meta_k, meta_v, 2, DEC, META), (win_k, win_v, 1, 0, P), (new_k, new_v, 2, 0, DEC)):
                pool.dma_start(ko[0, 0].rearrange(flat), qkv[lo:lo + n, j, NH * HD:NH * HD + P]).then_inc(kv_out, 16)
                pool.dma_start(vo[0, 0].rearrange(flat), qkv[lo:lo + n, j, QKV - P:QKV]).then_inc(kv_out, 16)
            pool.dma_start(wr[:, :, 0:NG], t["w_group"][0].rearrange("(k p) g -> p k g", p=P),
                           allow_slow_non_contiguous=True).then_inc(router_in, 16)
            pool.dma_start(wr[:, :, NG:20], t["w_router"][0].rearrange("(k p) g e -> p k (g e)", p=P),
                           allow_slow_non_contiguous=True).then_inc(router_in, 16)
            pool.dma_start(br[:, 0:NG], t["b_group"]).then_inc(router_in, 16)
            pool.dma_start(br[:, NG:20], t["b_router"].rearrange("a g e -> a (g e)")).then_inc(router_in, 16)
            S.emptied(pool, "tail")
            pool.dma_start(conv_p[0, 0].rearrange("j (c p) -> (j c) p", p=P), stage_rows[0:24, :]).then_inc(tail_out, 16)
            pool.dma_start(conv_s[0, 0].rearrange("j (c p) -> (j c) p", p=P), stage_rows[24:48, :]).then_inc(tail_out, 16)
            pool.dma_start(h_p[0, 0].rearrange("(c p) -> c p", p=P), stage_rows[48:56, :]).then_inc(tail_out, 16)
            pool.dma_start(h_s[0, 0].rearrange("(c p) -> c p", p=P), stage_rows[56:64, :]).then_inc(tail_out, 16)
            for j in range(3):
                for h in range(2):
                    S.emptied(pool, ("z1T", j, h))
            pool.wait_ge(z1_out, 48)
            for j in range(3):
                n = OUT_ROWS[j]
                nc.gpsimd.tensor_scalar(rows[0:n, j, :], rows[0:n, j, :], ALPHA, None, ALU.mult).then_inc(rows_scaled2, 1)

            def gather(i, s):
                nc.gpsimd.indirect_dma_start(
                    out=xg[s][0:CAP, :], out_offset=None, in_=z1_dram[:, :],
                    in_offset=bass.IndirectOffsetOnAxis(ap=index_i[0:CAP, i:i + 1], axis=0)).then_inc(xg_in[s], 16)

            pool.wait_ge(route_done, 1)
            for i in range(NE):
                if i >= 3:
                    pool.wait_ge(xt_full, i - 2)
                gather(i, i % 3)
            pool.wait_ge(ctrl_done, 1)
            count = pool.value_load(ctrl_i[0:1, NOV:NOV + 1], min_val=0, max_val=NOV)
            for v in range(NOV):
                with pool.If(count > v):
                    pool.wait_ge(xt_full, NE + v)
                    gather(NE + v, 1)
            pool.wait_ge(zero_out, 16 * -(-NOV * CAP // 112))
            for s in range(3):
                pool.wait_ge(y_out[s], 16 * len(range(s, NE, 3)))
            for v in range(NOV):
                with pool.If(count > v):
                    pool.wait_ge(y_out[1], 16 * (len(range(1, NE, 3)) + v + 1))
            for j in range(3):
                for k in range(2):
                    nc.gpsimd.indirect_dma_start(
                        out=yg[j][k][0:OUT_ROWS[j], :], out_offset=None, in_=y_dram[:, :],
                        in_offset=bass.IndirectOffsetOnAxis(ap=slot_i[0:OUT_ROWS[j], k, j:j + 1], axis=0))\
                        .then_inc(yg_in[j], 16)

        @block.tensor
        def _(pe):
            pe.wait_ge(const_in, 16)
            pe.wait_ge(vec_in, 128)
            b = S.claim(pe, "vec")
            nc.tensor.transpose(b[:, 0:NVEC], vrow[0:NVEC, :], ident[0:NVEC, 0:NVEC]).then_inc(S.f_full("vec"), 1)

            def transpose_rows(kind, j, n):
                for h in range(2):
                    b = S.claim(pe, (kind, j, h))
                    for k in range(4):
                        kk = 4 * h + k
                        mm = nc.tensor.transpose(b[:, k * P:k * P + n], rows[0:n, j, kk * P:kk * P + P], ident[0:n, 0:n])
                    mm.then_inc(S.f_full((kind, j, h)), 1)

            for j in range(3):
                n = TILE_ROWS[j]
                pe.wait_ge(rows_ready, j + 1)
                transpose_rows("zT", j, n)
            for j in range(3):
                n = TILE_ROWS[j]
                for h in range(2):
                    S.emptied(pe, ("zT", j, h))
                for u in range(3):
                    if j == 0:
                        unit_loaded(pe, u)
                    w = ring[u].rearrange("p (k n) -> p k n", n=256)
                    b = M.claim(pe, ("qkv", j, u))
                    for k in range(KD):
                        mm = nc.tensor.matmul(b[0:n, 0:256], zT[:, k, META + P * j:META + P * j + n], w[:, k, :],
                                              start=(k == 0), stop=(k == KD - 1))
                    mm.then_inc(M.f_full(("qkv", j, u)), 1)

            def chan(u, c, name, rhs, kk):
                unit_loaded(pe, u)
                w = ring[u % RING].rearrange("p (k n) -> p k n", n=256)
                b = M.claim(pe, name)
                o = (c % 2) * P
                n = rhs(0).shape[-1]
                for k in range(kk):
                    mm = nc.tensor.matmul(b[:, 0:n], w[:, k, o:o + P], rhs(k), start=(k == 0), stop=(k == kk - 1))
                mm.then_inc(M.f_full(name), 1)

            for c in range(KD):
                chan(U_XR + c // 2, c, ("xr", c), lambda k: zT[:, k, 0:NALL], KD)

            pe.wait_ge(roped, 3)
            for j in range(3):
                n = OUT_ROWS[j]
                b = M.claim(pe, ("QT", j))
                for c in range(4):
                    mm = nc.tensor.transpose(b[:, c * P:c * P + n], qkv[0:n, j, c * P:c * P + P], ident[0:n, 0:n])
                mm.then_inc(M.f_full(("QT", j)), 1)
            b = M.claim(pe, "KT")
            for j in range(3):
                n = TILE_ROWS[j]
                mm = nc.tensor.transpose(b[:, P * j:P * j + n], qkv[0:n, j, NH * HD:NH * HD + P], ident[0:n, 0:n])
            mm.then_inc(M.f_full("KT"), 1)
            pe.wait_ge(side_keys, 2)
            pe.wait_ge(cache_in, 64)
            b = M.claim(pe, "KS")
            nc.tensor.transpose(b[:, 0:P], kW, ident)
            nc.tensor.transpose(b[:, P:P + DEC + META], kS[0:DEC + META, :], ident[0:DEC + META, 0:DEC + META])\
                .then_inc(M.f_full("KS"), 1)

            unit_loaded(pe, U_RG)
            wrg = ring[U_RG % RING].rearrange("p (w n e) -> p w n e", w=2, e=P)
            for c in range(KD):
                pe.wait_ge(conv_made, c + 1)
                for w, kind in enumerate("ri"):
                    b = M.claim(pe, (kind, c))
                    nc.tensor.matmul(b[:, 0:TW], wrg[:, w, c, :], xc[:, c, :], start=True, stop=True)\
                        .then_inc(M.f_full((kind, c)), 1)

            def scores(c):
                for g in range(4):
                    kv, half = divmod(g, 2)
                    hp = slice(HD * kv, HD * kv + HD)
                    b = S.claim(pe, ("S", c, g))
                    q = qT[hp, c, P * half:P * half + P]
                    if c < 4:
                        lo, hi, _ = chunk_keys(c)
                        nc.tensor.matmul(b[:, 0:hi - lo], q, kT[hp, lo:hi], start=True, stop=True)
                        mm = nc.tensor.matmul(b[:, hi - lo:hi - lo + META], q, kT[hp, NTOK:NALL], start=True, stop=True)
                    else:
                        mm = nc.tensor.matmul(b[:, 0:WIN + DEC + META], q, kTs[hp, :], start=True, stop=True)
                    mm.then_inc(S.f_full(("S", c, g)), 1)

            def attend(c):
                blocks = chunk_blocks(c)
                pe.wait_ge(prob_ready, c + 1)
                for i, (at, n) in enumerate(blocks):
                    b = M.claim(pe, ("PT", c, i))
                    for g in range(4):
                        mm = nc.tensor.transpose(b[0:n, g * P:g * P + P], prob[c % 2][:, g, at:at + n], ident)
                    mm.then_inc(M.f_full(("PT", c, i)), 1)
                b = M.claim(pe, ("PV", c))
                for i in range(len(blocks)):
                    M.emptied(pe, ("PT", c, i))
                if c == 0:
                    pe.wait_ge(vm_in, 16)
                for kv in range(NKV):
                    for half in range(2):
                        g = 2 * kv + half
                        for i, (at, n) in enumerate(blocks):
                            if c == 4:
                                v = (vW if i == 0 else vS)[0:n, HD * kv:HD * kv + HD]
                            elif i == len(blocks) - 1:
                                v = vM[0:n, HD * kv:HD * kv + HD]
                            else:
                                v = qkv[0:n, i, QKV - P + HD * kv:QKV - P + HD * kv + HD]
                            mm = nc.tensor.matmul(b[HD * kv:HD * kv + HD, half * P:half * P + P], v,
                                                  pT[0:n, i, g * P:g * P + P],
                                                  start=(i == 0), stop=(i == len(blocks) - 1))
                mm.then_inc(M.f_full(("PV", c)), 1)

            for name in (("QT", 0), ("QT", 1), ("QT", 2), "KT", "KS"):
                M.emptied(pe, name)
            gr = iter(range(KD))
            for c in range(CHUNKS + 1):
                if c < CHUNKS:
                    scores(c)
                if c >= 1:
                    attend(c - 1)
                for _ in range(GR_AFTER[c]):
                    cc = next(gr)
                    chan(U_GR + cc // 2, cc, ("gr", cc), lambda k: zT[:, k, META:NALL], KD)

            for m in range(KD):
                u = U_MERGE + 4 * (m // 2)
                fills = ((0, "ga", lambda k: zT[:, k, META:NALL], KD), (1, "gr_gate", lambda k: zT[:, k, META:NALL], KD),
                         (2, "pa", lambda k: attnT[:, k, :], 4), (3, "pr", lambda k: rnnT[:, k, :], KD))
                for o, name, rhs, kk in fills:
                    if m == 0 and o == 2:
                        M.emptied(pe, ("PV", CHUNKS - 1))
                    if m == 0 and o == 3:
                        pe.wait_ge(rnn_made, 4)
                    chan(u + o, m, (name, m), rhs, kk)

            pe.wait_ge(tail_staged, 1)
            b = S.claim(pe, "tail")
            nc.tensor.transpose(b[0:64, 0:P], stage, ident).then_inc(S.f_full("tail"), 1)

            pe.wait_ge(merge_made, KD)
            for kind, j in OUT_ORDER:
                n = OUT_ROWS[j]
                if kind == "z1T":
                    pe.wait_ge(rows_ready, 3 + j + 1)
                    transpose_rows("z1T", j, n)
                    continue
                for h in range(2):
                    b = S.claim(pe, ("out", j, h))
                    for q in range(2):
                        u = U_OUT + 2 * h + q
                        unit_loaded(pe, u)
                        w = ring[u % RING].rearrange("p (k n) -> p k n", n=256)
                        for k in range(KD):
                            mm = nc.tensor.matmul(b[0:n, 256 * q:256 * q + 256], merged[:, k, P * j:P * j + n], w[:, k, :],
                                                  start=(k == 0), stop=(k == KD - 1))
                    mm.then_inc(S.f_full(("out", j, h)), 1)
            pe.wait_ge(router_in, 64)
            b = S.claim(pe, "logits")
            for j in range(3):
                n = OUT_ROWS[j]
                for h in range(2):
                    S.emptied(pe, ("z1T", j, h))
                for k in range(KD):
                    nc.tensor.matmul(b[0:n, 20 * j:20 * j + 20], z1T[:, k, P * j:P * j + n], wr[:, k, :],
                                     start=(k == 0), stop=False)
                mm = nc.tensor.matmul(b[0:n, 20 * j:20 * j + 20], ones[0:1, 0:n], br[:, :], start=False, stop=True)
            mm.then_inc(S.f_full("logits"), 1)
            pe.wait_ge(chosen, 1)
            b = S.claim(pe, "ranks")
            for j in range(3):
                for i in range(j):
                    nc.tensor.matmul(b[:, NE * j:NE * j + NE], ones, e_sum[:, i, :], start=(i == 0), stop=False)
                nc.tensor.matmul(b[:, NE * j:NE * j + NE], before, e_sum[:, j, :], start=(j == 0), stop=True)
            for i in range(3):
                mm = nc.tensor.matmul(b[:, NE * 3:NE * 4], ones, e_sum[:, i, :], start=(i == 0), stop=(i == 2))
            mm.then_inc(S.f_full("ranks"), 1)
            pe.wait_ge(selected, 1)
            b = S.claim(pe, "index")
            for k in range(2):
                for j in range(3):
                    mm = nc.tensor.matmul(b[0:CAP, 0:NITEM], rank_hot[:, k, CAP * j:CAP * j + CAP], item_hot[:, k, NITEM * j:NITEM * j + NITEM],
                                          start=(k == 0 and j == 0), stop=(k == 1 and j == 2))
            mm.then_inc(S.f_full("index"), 1)
            pe.wait_ge(route_done, 1)

            def turn(i, s, n):
                pe.wait_ge(xg_in[s], 16 * (n + 1))
                wait_past(pe, xt_half, 2 * i)
                for h in range(2):
                    for k in range(4):
                        mm = nc.tensor.transpose(TB[h][:, k * CAP:k * CAP + CAP], xg[s][0:CAP, P * (4 * h + k):P * (4 * h + k) + P],
                                                 ident[0:CAP, 0:CAP])
                mm.then_inc(xt_full, 1)

            def hidden(i, s, n):
                pe.wait_ge(xt_half, 2 * (i + 1))
                pe.wait_ge(g_in[s], 16 * (n + 1))
                pe.wait_ge(u_in[s], 16 * (n + 1))
                wait_past(pe, hid_made, KF * i)
                for m in range(KF):
                    for q, w in enumerate((w_gate[s], w_up[s])):
                        for k in range(KD):
                            mm = nc.tensor.matmul(HB[m][:, CAP * q:CAP * q + CAP], w[:, k, P * m:P * m + P], xT[s][:, k, :],
                                                  start=(k == 0), stop=(k == KD - 1))
                    mm.then_inc(hid_full, 1)

            def down(i, s, n):
                pe.wait_ge(d_in[s], 16 * (n + 1))
                wait_past(pe, y_made, 2 * i)
                for k in range(KF):
                    pe.wait_ge(hid_made, KF * i + k + 1)
                    for h in range(2):
                        mm = nc.tensor.matmul(YB[h][0:CAP, :], hT[s][:, k, :], w_down[s][:, k, 512 * h:512 * h + 512],
                                              start=(k == 0), stop=(k == KF - 1))
                mm.then_inc(y_full, 1)

            turn(0, 0, 0)
            def round_of(n):
                for s in range(3):
                    i = 3 * n + s
                    hidden(i, s, n)
                    turn(i + 1, (s + 1) % 3, n + (s + 1) // 3)
                    down(i, s, n)

            round_of(0)
            with pe.Fori(1, NE // 3) as n:
                round_of(n)
            hidden(NE - 1, 0, NE // 3)
            down(NE - 1, 0, NE // 3)
            pe.wait_ge(ctrl_done, 1)
            count = pe.value_load(ctrl_i[0:1, NOV:NOV + 1], min_val=0, max_val=NOV)
            with pe.If(count > 0):
                with pe.Fori(0, count) as v:
                    turn(v + NE, 1, v + NE // 3)
                    hidden(v + NE, 1, v + NE // 3)
                    down(v + NE, 1, v + NE // 3)

        @block.scalar
        def _(act):
            step = Steps(act, act_step)
            run = nc.scalar.activation

            def norm_rows_load(g, b):
                for i, name in enumerate((g, b)):
                    row = t[name] if len(t[name].shape) == 2 else t[name].rearrange("(o d) -> o d", o=1)
                    act.dma_start(gb[:, i, :], row.to_broadcast([P, D])).then_inc(norm_in, 16)

            def deviation(i, j, n):
                act.wait_ge(var_ready, 3 * i + j + 1)
                run(rstd[0:n, j:j + 1], mv[0:n, j, 1:2], ACT.Sqrt, bias=eps[0:n, :], scale=1.0).then_inc(std_ready, 1)

            norm_rows_load("ln_in_g", "ln_in_b")
            act.wait_ge(const_in, 16)
            for j in range(3):
                deviation(0, j, TILE_ROWS[j])
            for j in range(3):
                n = TILE_ROWS[j]
                for h in range(2):
                    b = S.arrived(act, ("zT", j, h)).rearrange("p (k n) -> p k n", n=P)
                    if j == 2:
                        nc.scalar.copy(zT[:, 4 * h:4 * h + 4, 0:META], b[:, :, DEC:DEC + META])
                    at = META + P * j
                    nc.scalar.copy(zT[:, 4 * h:4 * h + 4, at:at + n], b[:, :, 0:n]).then_inc(S.f_free(("zT", j, h)), 1)
            act.wait_ge(lam_ready, 1)
            run(sp_t[1], sp_t[0], ACT.Exp, scale=-1.0).then_inc(lam_exp, 1)
            for j in range(3):
                n = TILE_ROWS[j]
                for u in range(3):
                    b = M.arrived(act, ("qkv", j, u))
                    if u < NKV:
                        dst = qkv[0:n, j, 0:NH * HD].rearrange("p (c g d) -> p g c d", g=NKV, d=HD)[:, u]
                        src = b[0:n, 0:256].rearrange("p (c d) -> p c d", d=HD)
                    else:
                        dst, src = qkv[0:n, j, NH * HD:QKV], b[0:n, 0:256]
                    nc.scalar.copy(dst, src).then_inc(M.f_free(("qkv", j, u)), 1)
            for c in range(KD):
                b = M.arrived(act, ("xr", c))
                nc.scalar.copy(xpad[:, c, GAP:GAP + TP], b[:, 0:TP])
                nc.scalar.copy(xpad[:, c, TP + 2 * GAP:XPAD], b[:, TP:NALL]).then_inc(M.f_free(("xr", c)), 1)
            for j in range(3):
                n = OUT_ROWS[j]
                b = M.arrived(act, ("QT", j)).rearrange("p (c x q) -> p x c q", c=4, q=CHUNK)
                for x in range(n // CHUNK):
                    cp = nc.scalar.copy(qT[:, 2 * j + x, :].rearrange("p (c q) -> p c q", q=CHUNK), b[:, x])
                cp.then_inc(M.f_free(("QT", j)), 1)
            b = M.arrived(act, "KT")
            nc.scalar.copy(kT, b[:, 0:NALL]).then_inc(M.f_free("KT"), 1)
            b = M.arrived(act, "KS")
            nc.scalar.copy(kTs, b[:, 0:WIN + DEC + META]).then_inc(M.f_free("KS"), 1)
            act.wait_ge(cols_ready, 1)
            for c in range(KD):
                b = M.arrived(act, ("r", c))
                step(run(th_r[:, c % 2, :], b[:, 0:TW], ACT.Tanh, bias=hba[:, c:c + 1], scale=0.5))
                act.wait_ge(act_step, step.n)
                run(dec[:, c, :], th_r[:, c % 2, :], ACT.Exp, bias=nsp4[:, c:c + 1], scale=nsp4[:, c:c + 1])\
                    .then_inc(M.f_free(("r", c)), 1)
                run(inp[:, c, :], th_r[:, c % 2, :], ACT.Tanh, bias=sp4[:, c:c + 1], scale=sp4[:, c:c + 1])
                b = M.arrived(act, ("i", c))
                run(gate_i[:, c, :], b[:, 0:TW], ACT.Tanh, bias=hbx[:, c:c + 1], scale=0.5)\
                    .then_inc(M.f_free(("i", c)), 1)

            def exps(c):
                act.wait_ge(max_ready, c + 1)
                n = sum(k for _, k in chunk_blocks(c))
                off = chunk_keys(c)[2] if c < 4 else 0
                for g in range(4):
                    b = S.arrived(act, ("S", c, g))
                    run(prob[c % 2][:, g, off:n], b[:, 0:n - off], ACT.Exp, bias=nm[:, c % 2, g:g + 1], scale=HD ** -0.5,
                        accum_out=rs[:, c % 2, g:g + 1]).then_inc(S.f_free(("S", c, g)), 1)
                run(es[:, c % 2, :], m_c[:, c % 2, :], ACT.Exp).then_inc(exp_made, 1)

            gr = iter(range(KD))
            for c in range(CHUNKS + 1):
                if c < CHUNKS:
                    exps(c)
                if c >= 1:
                    for i, (_, n) in enumerate(chunk_blocks(c - 1)):
                        b = M.arrived(act, ("PT", c - 1, i))
                        if i == 0 and c >= 2:
                            M.arrived(act, ("PV", c - 2))
                        nc.scalar.copy(pT[0:n, i, :], b[0:n, :]).then_inc(M.f_free(("PT", c - 1, i)), 1)
                for _ in range(GR_AFTER[c]):
                    cc = next(gr)
                    b = M.arrived(act, ("gr", cc))
                    if cc >= 2:
                        M.emptied(act, ("gr", cc - 2))
                    run(gel[cc % 2], b[:, 0:NTOK], ACT.Square, scale=0.044715 ** 0.5).then_inc(gelu_sq, 1)
                    act.wait_ge(gelu_cube, cc + 1)
                    run(gel[cc % 2], gel[cc % 2], ACT.Tanh, scale=(2.0 / np.pi) ** 0.5).then_inc(gelu_tanh, 1)
            act.wait_ge(gate_prod, 4)
            run(inp[:, :, :], inp[:, :, :], ACT.Sqrt, scale=0.5).then_inc(sqrt_made, 1)

            for m in range(KD):
                if m == 0:
                    act.wait_ge(rows_ready, 3)
                if m >= 2:
                    act.wait_ge(merge_made, m - 1)
                for w, name in enumerate(("ga", "gr_gate")):
                    b = M.arrived(act, (name, m))
                    run(mtmp[m % 2][w], b[:, 0:NTOK], ACT.Tanh, bias=hbg[:, KD * w + m:KD * w + m + 1], scale=0.5)\
                        .then_inc(M.f_free((name, m)), 1)
            act.wait_ge(merge_made, KD)
            norm_rows_load("ln1_g", "ln1_b")

            def turned(j):
                act.wait_ge(rows_ready, 3 + j + 1)
                n = OUT_ROWS[j]
                act.dma_start(z1_dram[P * j:P * j + n, :], rows[0:n, j, :]).then_inc(z1_out, 16)
                for h in range(2):
                    b = S.arrived(act, ("z1T", j, h)).rearrange("p (k n) -> p k n", n=P)
                    nc.scalar.copy(z1T[:, 4 * h:4 * h + 4, P * j:P * j + n], b[:, :, 0:n])\
                        .then_inc(S.f_free(("z1T", j, h)), 1)

            deviation(1, 0, P)
            deviation(1, 1, P)
            turned(0)
            deviation(1, 2, DEC)
            turned(1)
            turned(2)
            norm_rows_load("ln2_g", "ln2_b")
            act.wait_ge(lg_exp_in, 1)
            run(exo, exi, ACT.Exp).then_inc(lg_exp, 1)

            def item(i, s, n):
                for m in range(KF):
                    act.wait_ge(hid_full, KF * i + (m + 1))
                    run(htmp[m], HB[m][:, 0:CAP], ACT.Tanh, scale=0.5).then_inc(hid_tanh, 1)
                act.wait_ge(y_full, i + 1)
                wait_past(act, y_out[s], 16 * n)
                for h in range(2):
                    nc.scalar.copy(yo[s][0:CAP, 512 * h:512 * h + 512], YB[h][0:CAP, :]).then_inc(y_made, 1)
                act.wait_ge(y_made, 2 * i + 2)
                dst = y_dram[i * CAP:(i + 1) * CAP, :] if isinstance(i, int) else y_dram[bass.ds(i * CAP, CAP), :]
                act.dma_start(dst, yo[s][0:CAP, :]).then_inc(y_out[s], 16)

            act.wait_ge(route_done, 1)
            for s in range(3):
                item(s, s, 0)
            with act.Fori(1, NE // 3) as n:
                for s in range(3):
                    item(3 * n + s, s, n)
            item(NE - 1, 0, NE // 3)
            act.wait_ge(ctrl_done, 1)
            count = act.value_load(ctrl_i[0:1, NOV:NOV + 1], min_val=0, max_val=NOV)
            with act.If(count > 0):
                with act.Fori(0, count) as v:
                    item(v + NE, 1, v + NE // 3)
            for j in range(3):
                deviation(2, j, OUT_ROWS[j])

        @block.vector
        def _(dve):
            step = Steps(dve, dve_step)
            V = nc.vector
            tt, stt, ts = V.tensor_tensor, V.scalar_tensor_tensor, V.tensor_scalar

            def alone(inst):
                step(inst)
                step.settle()

            def moments(j, n):
                for h in range(2):
                    step(V.bn_stats(stats[0:n, j, 6 * h:6 * h + 6], rows[0:n, j, 512 * h:512 * h + 512]))
                step.settle()
                V.bn_aggr(mv[0:n, j, :], stats[0:n, j, :]).then_inc(var_ready, 1)

            def normed(i, j, n):
                dve.wait_ge(std_ready, 3 * i + j + 1)
                alone(V.reciprocal(rstd[0:n, j:j + 1], rstd[0:n, j:j + 1]))
                dve.wait_ge(var_ready, 3 * i + j + 1)
                alone(ts(rows[0:n, j, :], rows[0:n, j, :], mv[0:n, j, 0:1], rstd[0:n, j:j + 1], ALU.subtract, ALU.mult))
                if j == 0:
                    dve.wait_ge(norm_in, 32 * (i + 1))
                alone(tt(rows[0:n, j, :], rows[0:n, j, :], gb[0:n, 0, :], ALU.mult))
                tt(rows[0:n, j, :], rows[0:n, j, :], gb[0:n, 1, :], ALU.add).then_inc(rows_ready, 1)

            for j in range(3):
                dve.wait_ge(x_in[j], 16 if j < 2 else 32)
                moments(j, TILE_ROWS[j])
            for j in range(3):
                normed(0, j, TILE_ROWS[j])

            b = S.arrived(dve, "vec")
            V.tensor_copy(vcol, b[:, 0:NVEC]).then_inc(S.f_free("vec"), 1)
            S.emptied(dve, "vec")
            alone(ts(sp_t[1], vc("lam", 0, KD), -1.0, None, ALU.mult))
            tt(sp_t[0], sp_t[1], vc("lam", 0, KD), ALU.max).then_inc(lam_ready, 1)
            step(ts(hba, vc("b_a", 0, KD), 0.5, None, ALU.mult))
            step(ts(hbx, vc("b_x", 0, KD), 0.5, None, ALU.mult))
            step(ts(hbg, vc("b_gate", 0, 2 * KD), 0.5, None, ALU.mult))
            step(V.memset(xpad[:, :, 0:GAP], 0.0))
            states = vc("state_conv", 0, GAP * KD).rearrange("p (j c) -> p c j", c=KD)
            step(V.tensor_copy(xpad[:, :, TP + GAP:TP + 2 * GAP], states))
            dve.wait_ge(lam_exp, 1)
            alone(ts(sp_t[2], sp_t[1], 2.0, None, ALU.add))
            alone(V.reciprocal(sp_t[2], sp_t[2]))
            alone(tt(sp_t[2], sp_t[2], sp_t[1], ALU.mult))
            alone(tt(sp_t[3], sp_t[2], sp_t[2], ALU.mult))
            alone(ts(sp_t[4], sp_t[3], 1.0 / 17, None, ALU.mult))
            for k in (15, 13, 11, 9, 7, 5, 3):
                alone(stt(sp_t[4], sp_t[4], 1.0 / k, sp_t[3], ALU.add, ALU.mult))
            alone(stt(sp_t[4], sp_t[4], 1.0, sp_t[2], ALU.add, ALU.mult))
            alone(ts(sp_t[5], vc("lam", 0, KD), -1.0, 0.0, ALU.mult, ALU.max))
            alone(stt(sp_t[5], sp_t[4], 2.0, sp_t[5], ALU.mult, ALU.add))
            alone(ts(sp4, sp_t[5], 0.5 * LRU_C, None, ALU.mult))
            ts(nsp4, sp_t[5], -0.5 * LRU_C, None, ALU.mult).then_inc(cols_ready, 1)

            rot = [gel[0][:, 80 * i:80 * i + 80].rearrange("p (h d) -> p h d", d=HALF) for i in range(4)]
            for j in range(3):
                n = TILE_ROWS[j]
                for u in range(3):
                    M.emptied(dve, ("qkv", j, u))
                heads = qkv[0:n, j, 0:(NH + NKV) * HD].rearrange("p (h d) -> p h d", d=HD)
                x1, x2 = heads[:, :, 0:HALF], heads[:, :, HALF:ROT]
                cos = cst("cos")[0:n, HALF * j:HALF * j + HALF].unsqueeze(1).to_broadcast([n, NH + NKV, HALF])
                sin = cst("sin")[0:n, HALF * j:HALF * j + HALF].unsqueeze(1).to_broadcast([n, NH + NKV, HALF])
                for out, a, b in ((0, x1, cos), (1, x2, sin), (2, x2, cos), (3, x1, sin)):
                    step(tt(rot[out][0:n], a, b, ALU.mult))
                step.settle()
                step(tt(x1, rot[0][0:n], rot[1][0:n], ALU.subtract))
                step.settle()
                tt(x2, rot[2][0:n], rot[3][0:n], ALU.add).then_inc(roped, 1)
                dve.wait_ge(roped, j + 1)

            for c in range(0, KD, 2):
                for q in (c, c + 1):
                    M.emptied(dve, ("xr", q))
                    step(ts(xc[:, q, :], xpad[:, q, 0:TW], vc("conv_w", q), vc("conv_b", q), ALU.mult, ALU.add))
                for j in range(1, CONVW):
                    for q in (c, c + 1):
                        dve.wait_ge(dve_step, step.n if j == CONVW - 1 and q > c else step.n - 1)
                        inst = stt(xc[:, q, :], xpad[:, q, j:j + TW], vc("conv_w", KD * j + q), xc[:, q, :], ALU.mult, ALU.add)
                        if j < CONVW - 1:
                            step(inst)
                        else:
                            inst.then_inc(conv_made, 1)

            for c in range(0, KD, 2):
                for q in (c, c + 1):
                    M.emptied(dve, ("i", q))
                two = slice(c, c + 2)
                alone(ts(den[:, :, :], inp[:, two, :], 1.0, None, ALU.add))
                step(V.reciprocal(den[:, :, :], den[:, :, :]))
                step(stt(gate_i[:, two, :], gate_i[:, two, :], 1.0, xc[:, two, :], ALU.add, ALU.mult))
                step.settle()
                tt(inp[:, two, :], inp[:, two, :], den[:, :, :], ALU.mult).then_inc(gate_prod, 1)
                dve.wait_ge(gate_prod, c // 2 + 1)

            def softmax_max(c):
                if c == 3:
                    M.arrived(dve, ("PT", 1, 0))
                    step(V.memset(prob[1][:, :, 0:chunk_keys(3)[2]], 0.0))
                n = sum(k for _, k in chunk_blocks(c)) - (chunk_keys(c)[2] if c < 4 else 0)
                k = c % 2
                for g in range(4):
                    b = S.arrived(dve, ("S", c, g))
                    step(V.tensor_reduce(mx[:, k, g:g + 1], b[:, 0:n], AX_X, ALU.max))
                step.settle()
                alone(stt(m_c[:, k, :], mx[:, k, :], HD ** -0.5, sink, ALU.mult, ALU.max))
                alone(ts(nm[:, k, :], m_c[:, k, :], -1.0, None, ALU.mult))
                tt(m_c[:, k, :], sink, m_c[:, k, :], ALU.subtract).then_inc(max_ready, 1)

            def softmax_norm(c):
                k = c % 2
                dve.wait_ge(exp_made, c + 1)
                for g in range(4):
                    S.emptied(dve, ("S", c, g))
                alone(tt(dn[:, k, :], rs[:, k, :], es[:, k, :], ALU.add))
                alone(V.reciprocal(rd[:, k, :], dn[:, k, :]))
                n = sum(w for _, w in chunk_blocks(c))
                for g in range(4):
                    inst = ts(prob[k][:, g, 0:n], prob[k][:, g, 0:n], rd[:, k, g:g + 1], None, ALU.mult)
                inst.then_inc(prob_ready, 1)

            dve.wait_ge(sink_in, 32)
            gr = iter(range(KD))
            for c in range(CHUNKS + 1):
                if c < CHUNKS:
                    softmax_max(c)
                    softmax_norm(c)
                if c >= 1:
                    b = M.arrived(dve, ("PV", c - 1))
                    V.tensor_copy(attnT[:, :, CHUNK * (c - 1):CHUNK * c], b[:, 0:256].rearrange("p (h q) -> p h q", q=CHUNK))\
                        .then_inc(M.f_free(("PV", c - 1)), 1)
                for _ in range(GR_AFTER[c]):
                    cc = next(gr)
                    b = M.arrived(dve, ("gr", cc))
                    dve.wait_ge(gelu_sq, cc + 1)
                    stt(gel[cc % 2], gel[cc % 2], 1.0, b[:, 0:NTOK], ALU.add, ALU.mult).then_inc(gelu_cube, 1)
                    dve.wait_ge(gelu_tanh, cc + 1)
                    stt(rnnT[:, cc, :], gel[cc % 2], 1.0, b[:, 0:NTOK], ALU.add, ALU.mult).then_inc(M.f_free(("gr", cc)), 1)

            dve.wait_ge(sqrt_made, 1)
            for c in range(0, KD, 2):
                two = slice(c, c + 2)
                alone(tt(inp[:, two, :], inp[:, two, :], gate_i[:, two, :], ALU.mult))
                last = TP + GAP - 1
                step(V.memset(dec[:, two, last:last + 1], 0.0))
                step(V.tensor_copy(inp[:, two, last:last + 1], vc("state_h", c, 2).unsqueeze(2)))
                step.settle()
                for q in (c, c + 1):
                    step(V.tensor_tensor_scan(gate_i[:, q, :], dec[:, q, :], inp[:, q, :], 0.0, ALU.mult, ALU.add))
                step.settle()
                step(stt(rnnT[:, two, 0:SEQ], gate_i[:, two, META:TP], 0.5, rnnT[:, two, 0:SEQ], ALU.mult, ALU.mult))
                stt(rnnT[:, two, SEQ:NTOK], gate_i[:, two, TP + GAP:TW], 0.5, rnnT[:, two, SEQ:NTOK], ALU.mult, ALU.mult)\
                    .then_inc(rnn_made, 1)
            for k, at in ((0, TP), (1, XPAD - GAP)):
                V.tensor_copy(stage[:, 24 * k:24 * k + 24].rearrange("p (j c) -> p c j", c=KD), xpad[:, :, at:at + GAP])
            V.tensor_copy(stage[:, 48:56], gate_i[:, :, TP - 1])
            V.tensor_copy(stage[:, 56:64], gate_i[:, :, TW - 1]).then_inc(tail_staged, 1)

            dve.wait_ge(zero_out, 16 * -(-NOV * CAP // 112))
            for m in range(KD):
                for w, (gate, proj) in enumerate((("ga", "pa"), ("gr_gate", "pr"))):
                    M.emptied(dve, (gate, m))
                    b = M.arrived(dve, (proj, m))
                    stt(mtmp[m % 2][w], mtmp[m % 2][w], 1.0, b[:, 0:NTOK], ALU.add, ALU.mult)\
                        .then_inc(M.f_free((proj, m)), 1)
                for proj in ("pa", "pr"):
                    M.emptied(dve, (proj, m))
                tt(merged[:, m, :], mtmp[m % 2][0], mtmp[m % 2][1], ALU.add).then_inc(merge_made, 1)
            b = S.arrived(dve, "tail")
            V.tensor_copy(stage_rows[0:64, :], b[0:64, 0:P]).then_inc(S.f_free("tail"), 1)
            dve.wait_ge(scaled, 3)
            for j in range(3):
                n = OUT_ROWS[j]
                for h in range(2):
                    half = rows[0:n, j, 512 * h:512 * h + 512]
                    b = S.arrived(dve, ("out", j, h))
                    stt(half, b[0:n, :], 0.5, half, ALU.mult, ALU.add).then_inc(S.f_free(("out", j, h)), 1)
                    S.emptied(dve, ("out", j, h))
                moments(j, n)
                normed(1, j, n)

            def bc(ap, *shape):
                return ap.to_broadcast([P, *shape])

            def first_max(src, top, hot):
                alone(V.tensor_reduce(top, src, AX_X, ALU.max))
                alone(tt(hot, src, bc(top.unsqueeze(2), 3, 4), ALU.is_equal))
                alone(tt(hot, hot, bc(cst("tie").unsqueeze(1), 3, 4), ALU.mult))
                alone(V.tensor_reduce(tie_top, hot, AX_X, ALU.max))
                alone(tt(hot, hot, bc(tie_top.unsqueeze(2), 3, 4), ALU.is_equal))

            alone(V.memset(logit, 0.0))
            b = S.arrived(dve, "logits")
            step(V.tensor_copy(logit[:, 0:2, :], b[:, 0:40].rearrange("p (j e) -> p j e", e=20)))
            V.tensor_copy(logit[0:DEC, 2, :], b[0:DEC, 40:60]).then_inc(S.f_free("logits"), 1)
            step.settle()
            S.emptied(dve, "logits")
            glog, elog = logit[:, :, 0:NG], logit[:, :, NG:20].rearrange("p j (g e) -> p j g e", e=EPG)
            first_max(glog, g_top, g_hot)
            exi3 = exi[:, 0:12].rearrange("p (j g) -> p j g", g=NG)
            step(tt(exi3, glog, bc(g_top.unsqueeze(2), 3, 4), ALU.subtract))
            for j in range(3):
                step(tt(cross[:, j].rearrange("p g e -> p g e"), elog[:, j], bc(g_hot[:, j, :].unsqueeze(2), 4, 4), ALU.mult))
            step.settle()
            for j in range(3):
                step(V.tensor_reduce(e_sel[:, j, :], cross[:, j].rearrange("p g e -> p e g"), AX_X, ALU.add))
            step.settle()
            first_max(e_sel, top[0], hot[0])
            alone(stt(e_sel, hot[0], -1e30, e_sel, ALU.mult, ALU.add))
            first_max(e_sel, top[1], hot[1])
            tt(exi[:, 12:15], top[1], top[0], ALU.subtract).then_inc(lg_exp_in, 1)
            for k in range(2):
                for j in range(3):
                    step(tt(e_hot[k][:, j].rearrange("p (g e) -> p g e", e=EPG), bc(g_hot[:, j, :].unsqueeze(2), 4, 4),
                            bc(hot[k][:, j, :].unsqueeze(1), 4, 4), ALU.mult))
            step.settle()
            alone(tt(e_sum, e_hot[0], e_hot[1], ALU.add))
            tt(e_sum, e_sum, bc(cst("valid").unsqueeze(2), 3, NE), ALU.mult).then_inc(chosen, 1)
            dve.wait_ge(lg_exp, 1)
            step(V.tensor_reduce(g_top, exo[:, 0:12].rearrange("p (j g) -> p j g", g=NG), AX_X, ALU.add))
            step(ts(tie_top, exo[:, 12:15], 1.0, None, ALU.add))
            step.settle()
            alone(tt(g_top, g_top, tie_top, ALU.mult))
            alone(V.reciprocal(weight[0], g_top))
            alone(tt(weight[1], weight[0], exo[:, 12:15], ALU.mult))
            b = S.arrived(dve, "ranks")
            step(V.tensor_copy(rank, b[:, 0:3 * NE].rearrange("p (j e) -> p j e", e=NE)))
            V.tensor_copy(count_e, b[:, 3 * NE:4 * NE]).then_inc(S.f_free("ranks"), 1)
            step.settle()
            S.emptied(dve, "ranks")
            alone(ts(ov, count_e, float(CAP), None, ALU.is_gt))
            for m in range(2, LEVELS + 1):
                alone(stt(ov, count_e, float(CAP * m), ov, ALU.is_gt, ALU.add))
            alone(V.tensor_tensor_scan(ov_end, ones[:, 0:NE], ov, 0.0, ALU.mult, ALU.add))
            alone(tt(base, ov_end, ov, ALU.subtract))
            alone(tt(base, base, cst("expert"), ALU.subtract))
            alone(ts(level, rank, float(CAP), None, ALU.is_ge))
            for m in range(2, LEVELS + 1):
                alone(stt(level, rank, float(CAP * m), level, ALU.is_ge, ALU.add))
            alone(stt(rank, level, -float(CAP), rank, ALU.mult, ALU.add))
            alone(tt(where, level, bc(base.unsqueeze(1), 3, NE), ALU.add))
            alone(ts(level, level, 1.0, None, ALU.min))
            alone(stt(where, where, float(NE - 1), level, ALU.add, ALU.mult))
            alone(tt(where, where, bc(cst("expert").unsqueeze(1), 3, NE), ALU.add))
            for k in range(2):
                alone(tt(e_sum2, e_hot[k], where, ALU.mult))
                alone(V.tensor_reduce(item_of[k], e_sum2, AX_X, ALU.add))
                alone(tt(e_sum2, e_hot[k], rank, ALU.mult))
                alone(V.tensor_reduce(rank_of[k], e_sum2, AX_X, ALU.add))
                alone(stt(slot_f, item_of[k], float(CAP), rank_of[k], ALU.mult, ALU.add))
                step(V.tensor_copy(slot_i[:, k, :], slot_f))
                rh = rank_hot[:, k, :].rearrange("p (j c) -> p j c", c=CAP)
                ih = item_hot[:, k, :].rearrange("p (j i) -> p j i", i=NITEM)
                step(tt(rh, bc(cst("iota_cap").unsqueeze(1), 3, CAP), bc(rank_of[k].unsqueeze(2), 3, CAP), ALU.is_equal))
                alone(tt(ih, bc(cst("iota_item").unsqueeze(1), 3, NITEM), bc(item_of[k].unsqueeze(2), 3, NITEM), ALU.is_equal))
                inst = tt(ih, ih, bc(cst("token").unsqueeze(2), 3, NITEM), ALU.mult)
                if k == 0:
                    alone(inst)
            inst.then_inc(selected, 1)
            alone(tt(ov_cmp, bc(ov_end.unsqueeze(1), NOV, NE), bc(cst("iota_ov").unsqueeze(2), NOV, NE), ALU.is_le))
            alone(V.tensor_reduce(ov_exp, ov_cmp, AX_X, ALU.add))
            alone(ts(ov_exp, ov_exp, float(NE - 1), None, ALU.min))
            step(V.tensor_copy(ctrl_i[:, 0:NOV], ov_exp))
            V.tensor_copy(ctrl_i[:, NOV:NOV + 1], ov_end[:, NE - 1:NE]).then_inc(ctrl_done, 1)
            dve.wait_ge(ctrl_done, 1)
            b = S.arrived(dve, "index")
            V.tensor_copy(index_i[0:CAP, :], b[0:CAP, 0:NITEM]).then_inc(route_done, 1)
            dve.wait_ge(route_done, 1)

            def item(i, s):
                dve.wait_ge(xt_full, i + 1)
                for h in range(2):
                    V.tensor_copy(xT[s][:, 4 * h:4 * h + 4, :], TB[h][:, 0:4 * CAP].rearrange("p (k c) -> p k c", c=CAP))\
                        .then_inc(xt_half, 1)
                for m in range(KF):
                    dve.wait_ge(hid_tanh, KF * i + (m + 1))
                    stt(htmp[m], htmp[m], 1.0, HB[m][:, 0:CAP], ALU.add, ALU.mult).then_inc(hid_mul, 1)
                    dve.wait_ge(hid_mul, KF * i + (m + 1))
                    stt(hT[s][:, m, :], htmp[m], 0.5, HB[m][:, CAP:2 * CAP], ALU.mult, ALU.mult).then_inc(hid_made, 1)

            with dve.Fori(0, NE // 3) as n:
                for s in range(3):
                    item(3 * n + s, s)
            item(NE - 1, 0)
            count = dve.value_load(ctrl_i[0:1, NOV:NOV + 1], min_val=0, max_val=NOV)
            with dve.If(count > 0):
                with dve.Fori(0, count) as v:
                    item(v + NE, 1)

            dve.wait_ge(rows_scaled2, 3)
            for j in range(3):
                n = OUT_ROWS[j]
                dve.wait_ge(yg_in[j], 32)
                for k in range(2):
                    alone(stt(rows[0:n, j, :], yg[j][k][0:n, :], weight[k][0:n, j:j + 1], rows[0:n, j, :], ALU.mult, ALU.add))
                moments(j, n)
                normed(2, j, n)


INPUTS = ["x_prompt", "x_sample", "cache_meta_k", "cache_meta_v", "cache_win_k", "cache_win_v", "state_conv", "state_h",
          "meta_tokens", "ln_in_g", "ln_in_b", "w_in", "b_gate", "attn_sinks", "conv_w", "conv_b", "w_rg_a", "b_rg_a",
          "w_rg_x", "b_rg_x", "lru_lambda", "w_branch_attn", "w_branch_rnn", "w_out", "ln1_g", "ln1_b", "w_group",
          "b_group", "w_router", "b_router", "w_gate", "w_up", "w_down", "ln2_g", "ln2_b"]
OUTPUTS = [(1, SEQ, D), (1, DEC, D), (1, 1, META, NKV, HD), (1, 1, META, NKV, HD), (1, 1, WIN, NKV, HD),
           (1, 1, WIN, NKV, HD), (1, 1, GAP, D), (1, 1, D), (1, 1, DEC, NKV, HD), (1, 1, DEC, NKV, HD),
           (1, 1, GAP, D), (1, 1, D)]


def kernel(**inputs):
    import concourse.bacc as bacc
    from concourse.bass_utils import run_bass_kernel_spmd

    nc = bacc.Bacc("TRN2", target_bir_lowering=False, num_devices=1)
    arrays, aps = {}, {}
    for name in INPUTS:
        arrays[f"in_{name}"] = np.ascontiguousarray(inputs[name])
    arrays["in_const"] = constants()
    for key, a in arrays.items():
        aps[key[3:]] = nc.dram_tensor(key, a.shape, F32, kind="ExternalInput").ap()
    outs = [nc.dram_tensor(f"out_{i}", shape, F32, kind="ExternalOutput").ap() for i, shape in enumerate(OUTPUTS)]
    build(nc, aps, outs)
    r = run_bass_kernel_spmd(nc, [arrays], core_ids=[0])
    return tuple(r.results[0][f"out_{i}"] for i in range(len(OUTPUTS)))
```

```python
from contextlib import ExitStack

import numpy as np

import concourse.bass as bass
from concourse import mybir

F32 = mybir.dt.float32
I32 = mybir.dt.int32
ALU = mybir.AluOpType
ACT = mybir.ActivationFunctionType
AX_X = mybir.AxisListType.X

P = 128
D = 1024
KD = D // P
SEQ, DEC, META = 256, 64, 16
NTOK = SEQ + DEC
NALL = NTOK + META
CHUNK, WIN = 64, 128
NH, NKV, HD = 8, 2, 64
HPK = NH // NKV
ROT = HD // 4
HALF = ROT // 2
THETA = 500000.0
LRU_C = 8.0
PAST = 512
CONVW = 4
QKV = (NH + 2 * NKV) * HD
ALPHA = 2.0 ** 0.25
EPS = 1e-5
NG, EPG = 4, 4
NE = NG * EPG
FE = 512
KF = FE // P
TILE_ROWS = (128, 128, DEC + META)
OUT_ROWS = (128, 128, DEC)
TP = META + SEQ
GAP = CONVW - 1
TW = TP + GAP + DEC
XPAD = TW + GAP
FIRST, REST = 64, 32
CAP = FIRST + REST
LEVELS = NTOK // CAP
NOV = 2 * NTOK // (CAP + 1)
NITEM = NE + NOV
W_COUNT, W_REST, W_BEFORE, W_TOTAL = NOV, NOV + 1, NOV + 1 + NE, NOV + 1 + 2 * NE
NWORD = W_TOTAL + 1
UNIT = KD * 256
RING = 6
U_QKV, U_XR, U_RG, U_GR, U_MERGE, U_OUT = 0, 3, 7, 8, 12, 28
NUNIT = 32
C_XR = QKV
C_GR = C_XR + D
C_GL = C_GR + D


def const_layout():
    cols, at = {}, 0
    for name, n in (("ident", P), ("before", P), ("ones", P), ("cos", 3 * HALF), ("sin", 3 * HALF),
                    ("iota_cap", CAP), ("iota_item", NITEM), ("iota_ov", NOV), ("expert", NE),
                    ("level", LEVELS), ("tie", 4), ("token", 3), ("valid", 3), ("eps", 1)):
        cols[name] = (at, at + n)
        at += n
    return cols, at


CC, NCONST = const_layout()


def constants():
    c = np.zeros((P, NCONST), np.float32)

    def put(name, v):
        c[:, CC[name][0]:CC[name][1]] = v

    row = np.arange(P)
    put("ident", np.eye(P))
    put("before", (row[:, None] < row[None, :]).astype(np.float32))
    put("ones", 1.0)
    pos = np.zeros((P, 3), np.float32)
    pos[:, 0] = META + row
    pos[:, 1] = META + P + row
    pos[:DEC, 2] = META + PAST + row[:DEC]
    pos[DEC:DEC + META, 2] = row[:META]
    inv = np.float32(THETA) ** (-np.arange(HALF, dtype=np.float32) / np.float32(HALF))
    ang = pos[:, :, None] * inv.astype(np.float32)[None, None, :]
    put("cos", np.cos(ang).reshape(P, -1))
    put("sin", np.sin(ang).reshape(P, -1))
    put("iota_cap", np.arange(CAP))
    put("iota_item", np.arange(NITEM))
    put("iota_ov", np.arange(NOV))
    put("expert", np.arange(NE))
    put("level", CAP * (1 + np.arange(LEVELS)))
    put("tie", [4, 3, 2, 1])
    valid = np.array([[float(p < OUT_ROWS[j]) for j in range(3)] for p in range(P)])
    put("valid", valid)
    put("token", valid * (row[:, None] + P * np.arange(3)[None, :]))
    put("eps", EPS)
    return c


VEC = {}
_at = 0
for _n, _k in (("conv_w", CONVW * KD), ("conv_b", KD), ("b_a", KD), ("b_x", KD), ("lam", KD),
               ("state_h", KD), ("state_conv", GAP * KD), ("b_gate", 2 * KD)):
    VEC[_n] = (_at, _at + _k)
    _at += _k
NVEC = _at


class Ring:

    def __init__(self, banks, full, free, names):
        self.banks, self.full, self.free = banks, full, free
        self.index = {n: i for i, n in enumerate(names)}

    def bank(self, name):
        return self.banks[self.index[name] % len(self.banks)]

    def sems(self, name):
        i = self.index[name]
        n = len(self.banks)
        return self.full[i % n], self.free[i % n], i // n

    def claim(self, eng, name):
        _, free, n = self.sems(name)
        if n >= 1:
            eng.wait_ge(free, n)
        return self.bank(name)

    def arrived(self, eng, name):
        full, _, n = self.sems(name)
        eng.wait_ge(full, n + 1)
        return self.bank(name)

    def emptied(self, eng, name):
        _, free, n = self.sems(name)
        eng.wait_ge(free, n + 1)

    def f_full(self, name):
        return self.sems(name)[0]

    def f_free(self, name):
        return self.sems(name)[1]


class Steps:

    def __init__(self, eng, sem):
        self.eng, self.sem, self.n = eng, sem, 0

    def __call__(self, inst):
        inst.then_inc(self.sem, 1)
        self.n += 1
        return self.n

    def settle(self):
        self.eng.wait_ge(self.sem, self.n)


def wait_past(eng, sem, n):
    if not (isinstance(n, int) and n == 0):
        eng.wait_ge(sem, n)


CHUNKS = 5


def chunk_keys(c):
    lo = max(0, (c - 2) * CHUNK)
    hi = (c + 1) * CHUNK
    return lo, hi, lo % P


def chunk_blocks(c):
    if c == 4:
        return [(0, P), (P, DEC + META)]
    lo, hi, off = chunk_keys(c)
    out, at, end = [], 0, off + hi - lo
    while at < end:
        out.append((at, min(P, end - at)))
        at += P
    return out + [(end, META)]


def pe_fills():
    m, s = [], []
    for j in range(3):
        s += [("zT", j, h) for h in range(2)]
        m += [("qkv", j, u) for u in range(3)]
    s.append("vec")
    m += [("xr", c) for c in range(KD)]
    m += [("QT", j) for j in range(3)] + ["KT", "KS"]
    for c in range(KD):
        m += [("r", c), ("i", c)]
    gr = iter(range(KD))
    for c in range(CHUNKS + 1):
        if c < CHUNKS:
            s += [("S", c, g) for g in range(4)]
        if c >= 1:
            m += [("PT", c - 1, b) for b in range(len(chunk_blocks(c - 1)))] + [("PV", c - 1)]
        for _ in range(GR_AFTER[c]):
            m.append(("gr", next(gr)))
    for mm in range(KD):
        m += [("ga", mm), ("gr_gate", mm), ("pa", mm), ("pr", mm)]
    s.append("tail")
    for kind, j in OUT_ORDER:
        s += [(kind, j, h) for h in range(2)]
    s += ["logits", "ranks", "index"]
    return m, s


OUT_ORDER = (("out", 0), ("out", 1), ("z1T", 0), ("out", 2), ("z1T", 1), ("z1T", 2))
GR_AFTER = [4, 1, 1, 1, 1, 0]
GELU_AT = [c for c in range(CHUNKS) if sum(GR_AFTER[:c]) < 4 <= sum(GR_AFTER[:c + 1])]


def build(nc, t, outs):
    (y_prompt, y_sample, meta_k, meta_v, win_k, win_v, conv_p, h_p, new_k, new_v, conv_s, h_s) = outs
    with ExitStack() as ctx:
        def sb(name, shape, dt=F32):
            return ctx.enter_context(nc.sbuf_tensor(name, shape, dt))

        def sem(name):
            return ctx.enter_context(nc.semaphore(name))

        EXP = KD * FE + KD * FE + KF * D
        slots = sb("expert_slots", [P, 3 * EXP])
        NWORK = 3 * D + KD * (NALL + META) + 2 * KD * NTOK + 4 * NTOK + 160
        work = sb("work", [P, NWORK])
        const = sb("const", [P, NCONST])
        small = sb("small", [P, 900])
        index_i = sb("index_i", [P, NITEM], I32)
        slot_i = sb("slot_i", [P, 2, 3], I32)
        ctrl_i = sb("ctrl_i", [P, NWORD], I32)

        class Area:
            def __init__(self, tensor, base, end):
                self.t, self.at, self.end = tensor, base, end

            def take(self, *dims):
                n = int(np.prod(dims))
                ap = self.t[:, self.at:self.at + n]
                self.at += n
                assert self.at <= self.end, (self.at, self.end)
                if len(dims) == 2:
                    ap = ap.rearrange("p (a b) -> p a b", b=dims[1])
                if len(dims) == 3:
                    ap = ap.rearrange("p (a b c) -> p a b c", b=dims[1], c=dims[2])
                return ap

        def cst(name):
            return const[:, CC[name][0]:CC[name][1]]

        ident, before, ones = cst("ident"), cst("before"), cst("ones")

        scr = Area(slots, 0, 2 * EXP)
        qkv = scr.take(3, QKV)
        qT = scr.take(CHUNKS, 4 * CHUNK)
        kT = scr.take(NALL)
        kTs = scr.take(WIN + DEC + META)
        vM, vS, vW = scr.take(P), scr.take(P), scr.take(P)
        kW, kS = scr.take(P), scr.take(P)
        prob = [scr.take(4, 272), scr.take(4, 272)]
        pT = scr.take(3, 512)
        xpad = scr.take(KD, XPAD)
        xc = scr.take(KD, TW)
        dec = scr.take(KD, TW)
        inp = scr.take(KD, TW)
        gate_i = scr.take(KD, TW)
        gel_at = scr.at
        th_r = scr.take(2, TW)
        asq = scr.take(2, TW)
        rot_t = scr.take(4, 80)
        gel = slots[:, gel_at:gel_at + 4 * NTOK].rearrange("p (c n) -> p c n", n=NTOK)
        ring = [slots[:, 2 * EXP + i * UNIT:2 * EXP + (i + 1) * UNIT] for i in range(RING)]
        w_gate = [slots[:, i * EXP:i * EXP + KD * FE].rearrange("p (k f) -> p k f", f=FE) for i in range(3)]
        w_up = [slots[:, i * EXP + KD * FE:i * EXP + 2 * KD * FE].rearrange("p (k f) -> p k f", f=FE)
                for i in range(3)]
        w_down = [slots[:, i * EXP + 2 * KD * FE:(i + 1) * EXP].rearrange("p (k f) -> p k f", f=D)
                  for i in range(3)]

        area = Area(work, 0, NWORK)
        rows = area.take(3, D)
        zT = area.take(KD, NALL + META)
        rnnT = area.take(KD, NTOK)
        attnT = area.take(4, NTOK)
        merged = area.take(KD, NTOK)
        z1T = rnnT
        ea = Area(work, 3 * D, NWORK)
        xg = [ea.take(D) for _ in range(3)]
        xT = [ea.take(KD, CAP) for _ in range(3)]
        yo = [ea.take(512) for _ in range(3)]
        th_a, hid_a, hT_a = ea.take(256), ea.take(256), ea.take(256)
        th_b, hid_b, hT_b, yo_b = ea.take(P), ea.take(P), ea.take(P), ea.take(256)
        gb = sb("norm_rows", [P, 2, D])
        mtmp = [[gb[:, i, NTOK * w:NTOK * w + NTOK] for w in range(2)] for i in range(2)]
        fin = Area(slots, 0, 3 * EXP)
        yg = [[fin.take(D) for _ in range(2)] for _ in range(3)]

        sm = Area(small, 0, 900)
        vrow = sm.take(P)
        vcol = sm.take(NVEC)
        stage = sm.take(64)
        stage_rows = sm.take(P)
        sink = sm.take(4)
        stats = sm.take(3, 12)
        mv = sm.take(3, 2)
        rstd = sm.take(3)
        hba, hbx = sm.take(KD), sm.take(KD)
        hbg = sm.take(2 * KD)
        sp4, nsp4 = sm.take(KD), sm.take(KD)
        sp_t = [sm.take(KD) for _ in range(6)]
        mx, m_c, nm, es, rs, dn, rd = [sm.take(2, 4) for _ in range(7)]
        wr = sb("router", [P, KD, 20])
        br = sb("router_bias", [1, 20])
        rt = Area(work, 3 * D + KD * (NALL + META) + KD * NTOK + 4 * NTOK, NWORK)
        logit = rt.take(3, 20)
        e_sum = rt.take(3, NE)
        rank_hot = rt.take(2, 3 * CAP)
        item_hot = rt.take(2, 3 * NITEM)
        weight = [sm.take(3) for _ in range(2)]
        exi, exo = rt.take(15), rt.take(15)
        g_top, tie_top, slot_f = rt.take(3), rt.take(3), rt.take(3)
        top, item_of, rank_of = ([rt.take(3) for _ in range(2)] for _ in range(3))
        g_hot, e_sel = rt.take(3, 4), rt.take(3, 4)
        hot = [rt.take(3, 4) for _ in range(2)]
        cross = rt.take(3, 4, 4)
        e_hot = [rt.take(3, NE) for _ in range(2)]
        e_sum2, rank, level, where = (rt.take(3, NE) for _ in range(4))
        count_e, ov, ov_end, base = (rt.take(NE) for _ in range(4))
        ov_cmp, ov_exp = rt.take(NOV, NE), rt.take(NOV)
        eps = cst("eps")

        def vc(name, i, n=1):
            return vcol[:, VEC[name][0] + i:VEC[name][0] + i + n]

        banks = [ctx.enter_context(nc.psum_tensor(f"bank{i}", [P, 512], F32)) for i in range(8)]
        names_m, names_s = pe_fills()
        M = Ring(banks[0:4], [sem(f"m_full{i}") for i in range(4)], [sem(f"m_free{i}") for i in range(4)], names_m)
        S = Ring(banks[4:8], [sem(f"s_full{i}") for i in range(4)], [sem(f"s_free{i}") for i in range(4)], names_s)

        TB, HB, TH, YB, BB = banks[0:2], banks[2:5], banks[5], banks[6], banks[7]
        z1_dram = nc.dram_tensor("z1_rows", [NTOK, D], F32, kind="Internal")
        y_dram = nc.dram_tensor("expert_rows", [NITEM * CAP, D], F32, kind="Internal")

        const_in = sem("const_in")
        lam_ready, lam_exp, cols_ready = sem("lam_ready"), sem("lam_exp"), sem("cols_ready")
        x_in = [sem(f"x_in{j}") for j in range(3)]
        norm_in = sem("norm_in")
        vec_in = sem("vec_in")
        sink_in = sem("sink_in")
        cache_in = sem("cache_in")
        vm_in = sem("vm_in")
        router_in = sem("router_in")
        unit_in = [sem(f"unit_in{i}") for i in range(RING)]
        dve_step, act_step, pool_step = sem("dve_step"), sem("act_step"), sem("pool_step")
        var_ready = sem("var_ready")
        std_ready = sem("std_ready")
        rows_ready = sem("rows_ready")
        scaled = sem("scaled")
        roped = sem("roped")
        side_keys = sem("side_keys")
        conv_made = sem("conv_made")
        asq_made, gate_prod = sem("asq_made"), sem("gate_prod")
        sqrt_made = sem("sqrt_made")
        max_ready = sem("max_ready")
        exp_made = sem("exp_made")
        prob_ready = sem("prob_ready")
        gelu_sq, gelu_cube, gelu_tanh, gelu_done = [sem(f"gelu_{n}") for n in ("sq", "cube", "tanh", "done")]
        rnn_made = sem("rnn_made")
        tail_staged = sem("tail_staged")
        merge_made = sem("merge_made")
        kv_out = sem("kv_out")
        tail_out = sem("tail_out")
        z1_out = sem("z1_out")
        lg_exp_in, lg_exp = sem("lg_exp_in"), sem("lg_exp")
        chosen = sem("chosen")
        selected = sem("selected")
        route_done = sem("route_done")
        zeroed, zero_out = sem("zeroed"), sem("zero_out")
        ctrl_done = sem("ctrl_done")
        rows_scaled2 = sem("rows_scaled2")
        g_in = [sem(f"gate_in{i}") for i in range(3)]
        u_in = [sem(f"up_in{i}") for i in range(3)]
        d_in = [sem(f"down_in{i}") for i in range(3)]
        xg_in = [sem(f"xg_in{i}") for i in range(3)]
        xt_full, xt_made = sem("xt_full"), sem("xt_made")
        ha_full, ha_tanh, ha_half, ha_made = [sem(f"ha_{n}") for n in ("full", "tanh", "half", "made")]
        hta_full, hta_made = sem("hta_full"), sem("hta_made")
        ya_full, ya_made = sem("ya_full"), sem("ya_made")
        y_out = [sem(f"y_out{i}") for i in range(3)]
        hb_full, hb_tanh, hb_half, hb_made = [sem(f"hb_{n}") for n in ("full", "tanh", "half", "made")]
        htb_full, htb_made = sem("htb_full"), sem("htb_made")
        yb_full, yb_made, yb_out = sem("yb_full"), sem("yb_made"), sem("yb_out")
        y_written = sem("y_written")
        yg_in = [sem(f"yg_in{j}") for j in range(3)]
        out_done = sem("out_done")

        def word(eng, at, most):
            return eng.value_load(ctrl_i[0:1, at:at + 1] if isinstance(at, int) else ctrl_i[0:1, bass.ds(at, 1)],
                                  min_val=0, max_val=most)

        def rest_words(eng, i):
            return word(eng, i + W_REST, 1), word(eng, i + W_BEFORE, NE)

        def overflow_words(eng):
            return word(eng, W_COUNT, NOV), word(eng, W_TOTAL, NE)

        def unit_consumed(eng, u):
            if u < U_XR:
                M.arrived(eng, ("qkv", 2, u))
            elif u < U_RG:
                M.arrived(eng, ("xr", 2 * (u - U_XR) + 1))
            elif u == U_RG:
                M.arrived(eng, ("i", KD - 1))
            elif u < U_MERGE:
                M.arrived(eng, ("gr", 2 * (u - U_GR) + 1))
            elif u < U_OUT:
                M.arrived(eng, (("ga", "gr_gate", "pa", "pr")[(u - U_MERGE) % 4], 2 * ((u - U_MERGE) // 4) + 1))
            else:
                S.arrived(eng, ("out", 2, (u - U_OUT) // 2))

        def unit_loaded(eng, u):
            n = 0
            for v in range(u % RING, u + 1, RING):
                n += 32 if v == U_RG or (U_MERGE <= v < U_OUT and (v - U_MERGE) % 4 == 2) else 16
            eng.wait_ge(unit_in[u % RING], n)

        block = ctx.enter_context(nc.Block())

        @block.sync
        def _(sp):
            w_in = t["w_in"][0].rearrange("(k p) n -> p k n", p=P)
            w_pa, w_pr, w_o = t["w_branch_attn"][0], t["w_branch_rnn"][0], t["w_out"][0]
            xp, xs = t["x_prompt"][0], t["x_sample"][0]
            sp.dma_start(rows[:, 0, :], xp[0:P, :]).then_inc(x_in[0], 16)
            sp.dma_start(const[:], t["const"]).then_inc(const_in, 16)
            sp.dma_start(rows[:, 1, :], xp[P:2 * P, :]).then_inc(x_in[1], 16)
            sp.dma_start(rows[0:DEC, 2, :], xs).then_inc(x_in[2], 16)
            sp.dma_start(rows[DEC:DEC + META, 2, :], t["meta_tokens"]).then_inc(x_in[2], 16)

            def unit(u):
                if u >= RING:
                    unit_consumed(sp, u - RING)
                dst, done = ring[u % RING], unit_in[u % RING]
                wide = dst.rearrange("p (k n) -> p k n", n=256)
                if u == U_RG:
                    half = dst.rearrange("p (w n e) -> p w n e", w=2, e=P)
                    sp.dma_start(half[:, 0], t["w_rg_a"][0].rearrange("n c e -> c n e")).then_inc(done, 16)
                    sp.dma_start(half[:, 1], t["w_rg_x"][0].rearrange("n c e -> c n e")).then_inc(done, 16)
                elif u < U_MERGE:
                    col = 256 * u if u < U_RG else C_GR + 256 * (u - U_GR)
                    sp.dma_start(wide, w_in[:, :, col:col + 256]).then_inc(done, 16)
                elif u < U_OUT:
                    mp, kind = divmod(u - U_MERGE, 4)
                    cols = slice(256 * mp, 256 * mp + 256)
                    if kind < 2:
                        col = C_GL + D * kind + 256 * mp
                        sp.dma_start(wide, w_in[:, :, col:col + 256]).then_inc(done, 16)
                    elif kind == 2:
                        for g in range(NKV):
                            src = w_pa[256 * g:256 * g + 256, cols].rearrange("(c d) n -> d c n", d=HD)
                            sp.dma_start(wide[HD * g:HD * g + HD, 0:4], src).then_inc(done, 16)
                    else:
                        sp.dma_start(wide, w_pr[:, cols].rearrange("(k p) n -> p k n", p=P)).then_inc(done, 16)
                else:
                    c = 256 * (u - U_OUT)
                    sp.dma_start(wide, w_o[:, c:c + 256].rearrange("(k p) n -> p k n", p=P)).then_inc(done, 16)

            def load_hidden(e, s):
                src = (t["w_gate"][0, e:e + 1], t["w_up"][0, e:e + 1]) if isinstance(e, int) else \
                    (t["w_gate"][0, bass.ds(e, 1)], t["w_up"][0, bass.ds(e, 1)])
                sp.dma_start(w_gate[s], src[0].rearrange("o (k p) f -> p (o k) f", p=P)).then_inc(g_in[s], 16)
                sp.dma_start(w_up[s], src[1].rearrange("o (k p) f -> p (o k) f", p=P)).then_inc(u_in[s], 16)

            def load_down(e, s):
                src = t["w_down"][0, e:e + 1] if isinstance(e, int) else t["w_down"][0, bass.ds(e, 1)]
                sp.dma_start(w_down[s], src.rearrange("o (k p) f -> p (o k) f", p=P)).then_inc(d_in[s], 16)

            def expert(e, s):
                load_hidden(e, s)
                load_down(e, s)

            for u in range(U_MERGE + 8):
                unit(u)
            sp.wait_ge(rnn_made, 2)
            M.emptied(sp, ("PV", CHUNKS - 1))
            sp.wait_ge(tail_staged, 1)
            sp.wait_ge(kv_out, 16 * 6)
            expert(0, 0)
            for u in range(U_MERGE + 8, U_MERGE + 12):
                unit(u)
            expert(1, 1)
            for u in range(U_MERGE + 12, NUNIT):
                unit(u)
            for u in range(NUNIT - RING, NUNIT):
                unit_consumed(sp, u)
            expert(2, 2)
            with sp.Fori(1, NE // 3) as n:
                for s in range(3):
                    i = 3 * n + s
                    sp.wait_ge(hta_full, i - 2)
                    load_hidden(i, s)
                    sp.wait_ge(ya_full, i - 2)
                    load_down(i, s)
            sp.wait_ge(hta_full, NE - 3)
            load_hidden(NE - 1, 0)
            sp.wait_ge(ya_full, NE - 3)
            load_down(NE - 1, 0)
            sp.wait_ge(ctrl_done, 1)
            count = sp.value_load(ctrl_i[0:1, W_COUNT:W_COUNT + 1], min_val=0, max_val=NOV)
            with sp.If(count > 0):
                with sp.Fori(0, count) as v:
                    sp.wait_ge(ya_full, v + NE)
                    e = sp.value_load(ctrl_i[0:1, bass.ds(v, 1)], min_val=0, max_val=NE - 1)
                    expert(e, 1)
            for j, dst in enumerate((y_prompt[0, 0:P, :], y_prompt[0, P:SEQ, :], y_sample[0])):
                sp.wait_ge(rows_ready, 7 + j)
                sp.dma_start(dst, rows[0:OUT_ROWS[j], j, :]).then_inc(out_done, 16)
            sp.wait_ge(out_done, 48)
            sp.wait_ge(kv_out, 96)
            sp.wait_ge(tail_out, 64)

        @block.gpsimd
        def _(pool):
            for name, key, spec in (("conv_w", "conv_w", "j (c p) -> (j c) p"), ("state_conv", "state_conv", "j (c p) -> (j c) p")):
                a, b = VEC[name]
                src = t[key][0] if name == "conv_w" else t[key][0, 0]
                pool.dma_start(vrow[a:b, :], src.rearrange(spec, p=P)).then_inc(vec_in, 16)
            for name, key in (("conv_b", "conv_b"), ("b_a", "b_rg_a"), ("b_x", "b_rg_x"), ("lam", "lru_lambda"),
                              ("b_gate", "b_gate")):
                a, b = VEC[name]
                pool.dma_start(vrow[a:b, :], t[key][0].rearrange("(c p) -> c p", p=P)).then_inc(vec_in, 16)
            a, b = VEC["state_h"]
            pool.dma_start(vrow[a:b, :], t["state_h"][0, 0].rearrange("(c p) -> c p", p=P)).then_inc(vec_in, 16)
            for h in range(2):
                src = t["attn_sinks"][0].rearrange("(c h) -> h c", h=2)[h:h + 1, :].to_broadcast([HD, 4])
                pool.dma_start(sink[HD * h:HD * h + HD, :], src, allow_slow_non_contiguous=True).then_inc(sink_in, 16)
            flat = "r h d -> r (h d)"
            pool.dma_start(kW, t["cache_win_k"][0, 0].rearrange(flat)).then_inc(cache_in, 16)
            pool.dma_start(vW, t["cache_win_v"][0, 0].rearrange(flat)).then_inc(cache_in, 16)
            pool.dma_start(kS[DEC:DEC + META, :], t["cache_meta_k"][0, 0].rearrange(flat)).then_inc(cache_in, 16)
            pool.dma_start(vS[DEC:DEC + META, :], t["cache_meta_v"][0, 0].rearrange(flat)).then_inc(cache_in, 16)
            nc.gpsimd.memset(merged[:, 0:4, :].rearrange("p k n -> p (k n)")[:, 0:D], 0.0).then_inc(zeroed, 1)
            pool.wait_ge(zeroed, 1)
            zeros = merged[0:REST, 0:4, :].rearrange("p k n -> p (k n)")[:, 0:D]
            for i in range(NE):
                pool.dma_start(y_dram[CAP * i + FIRST:CAP * (i + 1), :], zeros).then_inc(zero_out, 16)
            zeros = merged[0:CAP, 0:4, :].rearrange("p k n -> p (k n)")[:, 0:D]
            for i in range(NE, NITEM - 1):
                pool.dma_start(y_dram[CAP * i:CAP * (i + 1), :], zeros).then_inc(zero_out, 16)
            for j in range(3):
                for h in range(2):
                    S.emptied(pool, ("zT", j, h))
            for j in range(3):
                n = TILE_ROWS[j]
                nc.gpsimd.tensor_scalar(rows[0:n, j, :], rows[0:n, j, :], ALPHA, None, ALU.mult).then_inc(scaled, 1)
            M.emptied(pool, ("qkv", 2, 2))
            pool.dma_start(vM[0:META, :], qkv[DEC:DEC + META, 2, QKV - P:QKV]).then_inc(vm_in, 16)
            pool.wait_ge(roped, 3)
            nc.gpsimd.tensor_copy(kS[0:DEC, :], qkv[0:DEC, 2, NH * HD:NH * HD + P]).then_inc(side_keys, 1)
            nc.gpsimd.tensor_copy(vS[0:DEC, :], qkv[0:DEC, 2, QKV - P:QKV]).then_inc(side_keys, 1)
            for ko, vo, j, lo, n in ((meta_k, meta_v, 2, DEC, META), (win_k, win_v, 1, 0, P), (new_k, new_v, 2, 0, DEC)):
                pool.dma_start(ko[0, 0].rearrange(flat), qkv[lo:lo + n, j, NH * HD:NH * HD + P]).then_inc(kv_out, 16)
                pool.dma_start(vo[0, 0].rearrange(flat), qkv[lo:lo + n, j, QKV - P:QKV]).then_inc(kv_out, 16)
            pool.dma_start(wr[:, :, 0:NG], t["w_group"][0].rearrange("(k p) g -> p k g", p=P),
                           allow_slow_non_contiguous=True).then_inc(router_in, 16)
            pool.dma_start(wr[:, :, NG:20], t["w_router"][0].rearrange("(k p) g e -> p k (g e)", p=P),
                           allow_slow_non_contiguous=True).then_inc(router_in, 16)
            pool.dma_start(br[:, 0:NG], t["b_group"]).then_inc(router_in, 16)
            pool.dma_start(br[:, NG:20], t["b_router"].rearrange("a g e -> a (g e)")).then_inc(router_in, 16)
            S.emptied(pool, "tail")
            pool.dma_start(conv_p[0, 0].rearrange("j (c p) -> (j c) p", p=P), stage_rows[0:24, :]).then_inc(tail_out, 16)
            pool.dma_start(conv_s[0, 0].rearrange("j (c p) -> (j c) p", p=P), stage_rows[24:48, :]).then_inc(tail_out, 16)
            pool.dma_start(h_p[0, 0].rearrange("(c p) -> c p", p=P), stage_rows[48:56, :]).then_inc(tail_out, 16)
            pool.dma_start(h_s[0, 0].rearrange("(c p) -> c p", p=P), stage_rows[56:64, :]).then_inc(tail_out, 16)
            for j in range(3):
                for h in range(2):
                    S.emptied(pool, ("z1T", j, h))
            pool.wait_ge(z1_out, 48)
            for j in range(3):
                n = OUT_ROWS[j]
                nc.gpsimd.tensor_scalar(rows[0:n, j, :], rows[0:n, j, :], ALPHA, None, ALU.mult).then_inc(rows_scaled2, 1)

            def gather(i, s):
                nc.gpsimd.indirect_dma_start(
                    out=xg[s][0:CAP, :], out_offset=None, in_=z1_dram[:, :],
                    in_offset=bass.IndirectOffsetOnAxis(ap=index_i[0:CAP, i:i + 1], axis=0)).then_inc(xg_in[s], 16)

            pool.wait_ge(route_done, 1)
            for i in range(NE):
                if i >= 3:
                    pool.wait_ge(xt_full, i - 2)
                gather(i, i % 3)
            pool.wait_ge(ctrl_done, 1)
            count = pool.value_load(ctrl_i[0:1, W_COUNT:W_COUNT + 1], min_val=0, max_val=NOV)
            for v in range(NOV):
                with pool.If(count > v):
                    pool.wait_ge(xt_full, NE + v)
                    gather(NE + v, 1)
            pool.wait_ge(y_written, 1)
            for j in range(3):
                for k in range(2):
                    nc.gpsimd.indirect_dma_start(
                        out=yg[j][k][0:OUT_ROWS[j], :], out_offset=None, in_=y_dram[:, :],
                        in_offset=bass.IndirectOffsetOnAxis(ap=slot_i[0:OUT_ROWS[j], k, j:j + 1], axis=0))\
                        .then_inc(yg_in[j], 16)

        @block.tensor
        def _(pe):
            pe.wait_ge(const_in, 16)
            def transpose_rows(kind, j, n):
                for h in range(2):
                    b = S.claim(pe, (kind, j, h))
                    for k in range(4):
                        kk = 4 * h + k
                        mm = nc.tensor.transpose(b[:, k * P:k * P + n], rows[0:n, j, kk * P:kk * P + P], ident[0:n, 0:n])
                    mm.then_inc(S.f_full((kind, j, h)), 1)

            for j in range(3):
                n = TILE_ROWS[j]
                pe.wait_ge(rows_ready, j + 1)
                transpose_rows("zT", j, n)
            for j in range(3):
                n = TILE_ROWS[j]
                for h in range(2):
                    S.emptied(pe, ("zT", j, h))
                for u in range(3):
                    if j == 0:
                        unit_loaded(pe, u)
                    w = ring[u].rearrange("p (k n) -> p k n", n=256)
                    b = M.claim(pe, ("qkv", j, u))
                    for k in range(KD):
                        mm = nc.tensor.matmul(b[0:n, 0:256], zT[:, k, META + P * j:META + P * j + n], w[:, k, :],
                                              start=(k == 0), stop=(k == KD - 1))
                    mm.then_inc(M.f_full(("qkv", j, u)), 1)

            pe.wait_ge(vec_in, 128)
            b = S.claim(pe, "vec")
            nc.tensor.transpose(b[:, 0:NVEC], vrow[0:NVEC, :], ident[0:NVEC, 0:NVEC]).then_inc(S.f_full("vec"), 1)

            def chan(u, c, name, rhs, kk):
                unit_loaded(pe, u)
                w = ring[u % RING].rearrange("p (k n) -> p k n", n=256)
                b = M.claim(pe, name)
                o = (c % 2) * P
                n = rhs(0).shape[-1]
                for k in range(kk):
                    mm = nc.tensor.matmul(b[:, 0:n], w[:, k, o:o + P], rhs(k), start=(k == 0), stop=(k == kk - 1))
                mm.then_inc(M.f_full(name), 1)

            for c in range(KD):
                chan(U_XR + c // 2, c, ("xr", c), lambda k: zT[:, k, 0:NALL], KD)

            pe.wait_ge(roped, 3)
            for j in range(3):
                n = OUT_ROWS[j]
                b = M.claim(pe, ("QT", j))
                for c in range(4):
                    mm = nc.tensor.transpose(b[:, c * P:c * P + n], qkv[0:n, j, c * P:c * P + P], ident[0:n, 0:n])
                mm.then_inc(M.f_full(("QT", j)), 1)
            b = M.claim(pe, "KT")
            for j in range(3):
                n = TILE_ROWS[j]
                mm = nc.tensor.transpose(b[:, P * j:P * j + n], qkv[0:n, j, NH * HD:NH * HD + P], ident[0:n, 0:n])
            mm.then_inc(M.f_full("KT"), 1)
            pe.wait_ge(side_keys, 2)
            pe.wait_ge(cache_in, 64)
            b = M.claim(pe, "KS")
            nc.tensor.transpose(b[:, 0:P], kW, ident)
            nc.tensor.transpose(b[:, P:P + DEC + META], kS[0:DEC + META, :], ident[0:DEC + META, 0:DEC + META])\
                .then_inc(M.f_full("KS"), 1)

            unit_loaded(pe, U_RG)
            wrg = ring[U_RG % RING].rearrange("p (w n e) -> p w n e", w=2, e=P)
            for c in range(KD):
                pe.wait_ge(conv_made, c + 1)
                for w, kind in enumerate("ri"):
                    b = M.claim(pe, (kind, c))
                    nc.tensor.matmul(b[:, 0:TW], wrg[:, w, c, :], xc[:, c, :], start=True, stop=True)\
                        .then_inc(M.f_full((kind, c)), 1)

            def scores(c):
                for g in range(4):
                    kv, half = divmod(g, 2)
                    hp = slice(HD * kv, HD * kv + HD)
                    b = S.claim(pe, ("S", c, g))
                    q = qT[hp, c, P * half:P * half + P]
                    if c < 4:
                        lo, hi, _ = chunk_keys(c)
                        nc.tensor.matmul(b[:, 0:hi - lo], q, kT[hp, lo:hi], start=True, stop=True)
                        mm = nc.tensor.matmul(b[:, hi - lo:hi - lo + META], q, kT[hp, NTOK:NALL], start=True, stop=True)
                    else:
                        mm = nc.tensor.matmul(b[:, 0:WIN + DEC + META], q, kTs[hp, :], start=True, stop=True)
                    mm.then_inc(S.f_full(("S", c, g)), 1)

            def attend(c):
                blocks = chunk_blocks(c)
                pe.wait_ge(prob_ready, c + 1)
                for i, (at, n) in enumerate(blocks):
                    b = M.claim(pe, ("PT", c, i))
                    for g in range(4):
                        mm = nc.tensor.transpose(b[0:n, g * P:g * P + P], prob[c % 2][:, g, at:at + n], ident)
                    mm.then_inc(M.f_full(("PT", c, i)), 1)
                b = M.claim(pe, ("PV", c))
                for i in range(len(blocks)):
                    M.emptied(pe, ("PT", c, i))
                if c == 0:
                    pe.wait_ge(vm_in, 16)
                for kv in range(NKV):
                    for half in range(2):
                        g = 2 * kv + half
                        for i, (at, n) in enumerate(blocks):
                            if c == 4:
                                v = (vW if i == 0 else vS)[0:n, HD * kv:HD * kv + HD]
                            elif i == len(blocks) - 1:
                                v = vM[0:n, HD * kv:HD * kv + HD]
                            else:
                                v = qkv[0:n, i, QKV - P + HD * kv:QKV - P + HD * kv + HD]
                            mm = nc.tensor.matmul(b[HD * kv:HD * kv + HD, half * P:half * P + P], v,
                                                  pT[0:n, i, g * P:g * P + P],
                                                  start=(i == 0), stop=(i == len(blocks) - 1))
                mm.then_inc(M.f_full(("PV", c)), 1)

            for name in (("QT", 0), ("QT", 1), ("QT", 2), "KT", "KS"):
                M.emptied(pe, name)
            gr = iter(range(KD))
            for c in range(CHUNKS + 1):
                if c < CHUNKS:
                    scores(c)
                if c >= 1:
                    attend(c - 1)
                for _ in range(GR_AFTER[c]):
                    cc = next(gr)
                    chan(U_GR + cc // 2, cc, ("gr", cc), lambda k: zT[:, k, META:NALL], KD)

            for m in range(KD):
                u = U_MERGE + 4 * (m // 2)
                fills = ((0, "ga", lambda k: zT[:, k, META:NALL], KD), (1, "gr_gate", lambda k: zT[:, k, META:NALL], KD),
                         (2, "pa", lambda k: attnT[:, k, :], 4), (3, "pr", lambda k: rnnT[:, k, :], KD))
                for o, name, rhs, kk in fills:
                    if m == 0 and o == 2:
                        M.emptied(pe, ("PV", CHUNKS - 1))
                    if m == 0 and o == 3:
                        pe.wait_ge(rnn_made, 2)
                    chan(u + o, m, (name, m), rhs, kk)

            pe.wait_ge(tail_staged, 1)
            b = S.claim(pe, "tail")
            nc.tensor.transpose(b[0:64, 0:P], stage, ident).then_inc(S.f_full("tail"), 1)

            pe.wait_ge(merge_made, KD)
            for kind, j in OUT_ORDER:
                n = OUT_ROWS[j]
                if kind == "z1T":
                    pe.wait_ge(rows_ready, 3 + j + 1)
                    transpose_rows("z1T", j, n)
                    continue
                for h in range(2):
                    b = S.claim(pe, ("out", j, h))
                    for q in range(2):
                        u = U_OUT + 2 * h + q
                        unit_loaded(pe, u)
                        w = ring[u % RING].rearrange("p (k n) -> p k n", n=256)
                        for k in range(KD):
                            mm = nc.tensor.matmul(b[0:n, 256 * q:256 * q + 256], merged[:, k, P * j:P * j + n], w[:, k, :],
                                                  start=(k == 0), stop=(k == KD - 1))
                    mm.then_inc(S.f_full(("out", j, h)), 1)
            pe.wait_ge(router_in, 64)
            b = S.claim(pe, "logits")
            for j in range(3):
                n = OUT_ROWS[j]
                for h in range(2):
                    S.emptied(pe, ("z1T", j, h))
                for k in range(KD):
                    nc.tensor.matmul(b[0:n, 20 * j:20 * j + 20], z1T[:, k, P * j:P * j + n], wr[:, k, :],
                                     start=(k == 0), stop=False)
                mm = nc.tensor.matmul(b[0:n, 20 * j:20 * j + 20], ones[0:1, 0:n], br[:, :], start=False, stop=True)
            mm.then_inc(S.f_full("logits"), 1)
            pe.wait_ge(chosen, 1)
            b = S.claim(pe, "ranks")
            for j in range(3):
                for i in range(j):
                    nc.tensor.matmul(b[:, NE * j:NE * j + NE], ones, e_sum[:, i, :], start=(i == 0), stop=False)
                nc.tensor.matmul(b[:, NE * j:NE * j + NE], before, e_sum[:, j, :], start=(j == 0), stop=True)
            for i in range(3):
                mm = nc.tensor.matmul(b[:, NE * 3:NE * 4], ones, e_sum[:, i, :], start=(i == 0), stop=(i == 2))
            mm.then_inc(S.f_full("ranks"), 1)
            pe.wait_ge(selected, 1)
            b = S.claim(pe, "index")
            for k in range(2):
                for j in range(3):
                    mm = nc.tensor.matmul(b[0:CAP, 0:NITEM], rank_hot[:, k, CAP * j:CAP * j + CAP], item_hot[:, k, NITEM * j:NITEM * j + NITEM],
                                          start=(k == 0 and j == 0), stop=(k == 1 and j == 2))
            mm.then_inc(S.f_full("index"), 1)
            pe.wait_ge(route_done, 1)

            def turn(i, s, n):
                pe.wait_ge(xg_in[s], 16 * (n + 1))
                wait_past(pe, xt_made, i)
                for h in range(2):
                    for k in range(4):
                        mm = nc.tensor.transpose(TB[h][:, k * CAP:k * CAP + CAP], xg[s][0:CAP, P * (4 * h + k):P * (4 * h + k) + P],
                                                 ident[0:CAP, 0:CAP])
                mm.then_inc(xt_full, 1)

            def tiles(bank, cols, lhsT, rhs, kk, m):
                for k in range(kk):
                    for j in range(P // m):
                        mm = nc.tensor.matmul(bank[m * j:m * j + m, cols], lhsT(k), rhs(k, j), start=(k == 0), stop=(k == kk - 1))
                return mm

            def hidden(i, s, n):
                pe.wait_ge(xt_made, i + 1)
                pe.wait_ge(g_in[s], 16 * (n + 1))
                tiles(HB[s], slice(0, 256), lambda k: xT[s][:, k, 0:FIRST],
                      lambda k, j: w_gate[s][:, k, 256 * j:256 * j + 256], KD, FIRST)
                pe.wait_ge(u_in[s], 16 * (n + 1))
                tiles(HB[s], slice(256, 512), lambda k: xT[s][:, k, 0:FIRST],
                      lambda k, j: w_up[s][:, k, 256 * j:256 * j + 256], KD, FIRST).then_inc(ha_full, 1)

            def down(i, s, n):
                pe.wait_ge(d_in[s], 16 * (n + 1))
                pe.wait_ge(hta_made, i + 1)
                wait_past(pe, ya_made, i)
                tiles(YB, slice(0, 512), lambda k: hT_a[:, P * (k % 2) + FIRST * (k // 2):P * (k % 2) + FIRST * (k // 2) + FIRST],
                      lambda k, j: w_down[s][:, k, 512 * j:512 * j + 512], KF, FIRST).then_inc(ya_full, 1)

            def turn_hidden(i):
                pe.wait_ge(ha_made, i + 1)
                for h in range(2):
                    mm = nc.tensor.transpose(TH[:, P * h:P * h + P], hid_a[:, P * h:P * h + P], ident)
                mm.then_inc(hta_full, 1)

            def rest(s, n, b):
                pe.wait_ge(yb_made, b + 1)
                tiles(BB, slice(0, P), lambda k: xT[s][:, k, FIRST:CAP], lambda k, j: w_gate[s][:, k, P * j:P * j + P], KD, REST)
                tiles(BB, slice(P, 2 * P), lambda k: xT[s][:, k, FIRST:CAP], lambda k, j: w_up[s][:, k, P * j:P * j + P], KD, REST)\
                    .then_inc(hb_full, 1)
                pe.wait_ge(hb_made, b + 1)
                nc.tensor.transpose(BB[:, 2 * P:3 * P], hid_b, ident).then_inc(htb_full, 1)
                pe.wait_ge(d_in[s], 16 * (n + 1))
                pe.wait_ge(htb_made, b + 1)
                tiles(BB, slice(0, 256), lambda k: hT_b[:, REST * k:REST * k + REST],
                      lambda k, j: w_down[s][:, k, 256 * j:256 * j + 256], KF, REST).then_inc(yb_full, 1)

            def maybe_rest(i, s, n):
                has, b = rest_words(pe, i)
                with pe.If(has > 0):
                    rest(s, n, b)

            pe.wait_ge(ctrl_done, 1)

            def round_of(n, first):
                for s in range(3):
                    i = 3 * n + s
                    hidden(i, s, n)
                    if not (first and s == 0):
                        down(i - 1, (s - 1) % 3, n if s else n - 1)
                    turn(i + 1, (s + 1) % 3, n + (s + 1) // 3)
                    maybe_rest(i, s, n)
                    turn_hidden(i)

            turn(0, 0, 0)
            round_of(0, True)
            with pe.Fori(1, NE // 3) as n:
                round_of(n, False)
            down(NE - 2, 2, NE // 3 - 1)
            hidden(NE - 1, 0, NE // 3)
            maybe_rest(NE - 1, 0, NE // 3)
            turn_hidden(NE - 1)
            down(NE - 1, 0, NE // 3)
            count, total = overflow_words(pe)
            with pe.If(count > 0):
                with pe.Fori(0, count) as v:
                    turn(v + NE, 1, v + NE // 3)
                    hidden(v + NE, 1, v + NE // 3)
                    rest(1, v + NE // 3, total + v)
                    turn_hidden(v + NE)
                    down(v + NE, 1, v + NE // 3)

        @block.scalar
        def _(act):
            step = Steps(act, act_step)
            run = nc.scalar.activation

            def norm_rows_load(g, b):
                for i, name in enumerate((g, b)):
                    row = t[name] if len(t[name].shape) == 2 else t[name].rearrange("(o d) -> o d", o=1)
                    act.dma_start(gb[:, i, :], row.to_broadcast([P, D])).then_inc(norm_in, 16)

            def deviation(i, j, n):
                act.wait_ge(var_ready, 3 * i + j + 1)
                run(rstd[0:n, j:j + 1], mv[0:n, j, 1:2], ACT.Sqrt, bias=eps[0:n, :], scale=1.0).then_inc(std_ready, 1)

            norm_rows_load("ln_in_g", "ln_in_b")
            act.wait_ge(const_in, 16)
            for j in range(3):
                deviation(0, j, TILE_ROWS[j])
            for j in range(3):
                n = TILE_ROWS[j]
                for h in range(2):
                    b = S.arrived(act, ("zT", j, h)).rearrange("p (k n) -> p k n", n=P)
                    if j == 2:
                        nc.scalar.copy(zT[:, 4 * h:4 * h + 4, 0:META], b[:, :, DEC:DEC + META])
                    at = META + P * j
                    nc.scalar.copy(zT[:, 4 * h:4 * h + 4, at:at + n], b[:, :, 0:n]).then_inc(S.f_free(("zT", j, h)), 1)
            for j in range(3):
                n = TILE_ROWS[j]
                for u in range(3):
                    b = M.arrived(act, ("qkv", j, u))
                    if u < NKV:
                        dst = qkv[0:n, j, 0:NH * HD].rearrange("p (c g d) -> p g c d", g=NKV, d=HD)[:, u]
                        src = b[0:n, 0:256].rearrange("p (c d) -> p c d", d=HD)
                    else:
                        dst, src = qkv[0:n, j, NH * HD:QKV], b[0:n, 0:256]
                    nc.scalar.copy(dst, src).then_inc(M.f_free(("qkv", j, u)), 1)
            act.wait_ge(zeroed, 1)
            act.dma_start(y_dram[CAP * (NITEM - 1):CAP * NITEM, :], merged[0:CAP, 0:4, :].rearrange("p k n -> p (k n)")[:, 0:D])\
                .then_inc(yb_out, 16)
            act.wait_ge(lam_ready, 1)
            run(sp_t[1], sp_t[0], ACT.Exp, scale=-1.0).then_inc(lam_exp, 1)
            for c in range(KD):
                b = M.arrived(act, ("xr", c))
                nc.scalar.copy(xpad[:, c, GAP:GAP + TP], b[:, 0:TP])
                nc.scalar.copy(xpad[:, c, TP + 2 * GAP:XPAD], b[:, TP:NALL]).then_inc(M.f_free(("xr", c)), 1)
            for j in range(3):
                n = OUT_ROWS[j]
                b = M.arrived(act, ("QT", j)).rearrange("p (c x q) -> p x c q", c=4, q=CHUNK)
                for x in range(n // CHUNK):
                    cp = nc.scalar.copy(qT[:, 2 * j + x, :].rearrange("p (c q) -> p c q", q=CHUNK), b[:, x])
                cp.then_inc(M.f_free(("QT", j)), 1)
            b = M.arrived(act, "KT")
            nc.scalar.copy(kT, b[:, 0:NALL]).then_inc(M.f_free("KT"), 1)
            b = M.arrived(act, "KS")
            nc.scalar.copy(kTs, b[:, 0:WIN + DEC + META]).then_inc(M.f_free("KS"), 1)
            act.wait_ge(cols_ready, 1)
            for c in range(KD):
                b = M.arrived(act, ("r", c))
                step(run(th_r[:, c % 2, :], b[:, 0:TW], ACT.Tanh, bias=hba[:, c:c + 1], scale=0.5))
                act.wait_ge(act_step, step.n)
                run(dec[:, c, :], th_r[:, c % 2, :], ACT.Exp, bias=nsp4[:, c:c + 1], scale=nsp4[:, c:c + 1])\
                    .then_inc(M.f_free(("r", c)), 1)
                run(inp[:, c, :], th_r[:, c % 2, :], ACT.Tanh, bias=sp4[:, c:c + 1], scale=sp4[:, c:c + 1])
                b = M.arrived(act, ("i", c))
                run(gate_i[:, c, :], b[:, 0:TW], ACT.Tanh, bias=hbx[:, c:c + 1], scale=0.5)\
                    .then_inc(M.f_free(("i", c)), 1)
                if c % 2:
                    if c > 1:
                        act.wait_ge(gate_prod, c // 2)
                    M.emptied(act, ("r", c))
                    run(asq[:, :, :], dec[:, c - 1:c + 1, :], ACT.Square).then_inc(asq_made, 1)

            def exps(c):
                act.wait_ge(max_ready, c + 1)
                n = sum(k for _, k in chunk_blocks(c))
                off = chunk_keys(c)[2] if c < 4 else 0
                for g in range(4):
                    b = S.arrived(act, ("S", c, g))
                    run(prob[c % 2][:, g, off:n], b[:, 0:n - off], ACT.Exp, bias=nm[:, c % 2, g:g + 1], scale=HD ** -0.5,
                        accum_out=rs[:, c % 2, g:g + 1]).then_inc(S.f_free(("S", c, g)), 1)
                run(es[:, c % 2, :], m_c[:, c % 2, :], ACT.Exp).then_inc(exp_made, 1)

            def gelu_inner(h):
                act.wait_ge(gelu_cube, h + 1)
                run(gel, gel, ACT.Tanh, scale=(2.0 / np.pi) ** 0.5).then_inc(gelu_tanh, 1)

            gr = iter(range(KD))
            for c in range(CHUNKS + 1):
                if c < CHUNKS:
                    exps(c)
                if c >= 1:
                    for i, (_, n) in enumerate(chunk_blocks(c - 1)):
                        b = M.arrived(act, ("PT", c - 1, i))
                        if i == 0 and c >= 2:
                            M.arrived(act, ("PV", c - 2))
                        nc.scalar.copy(pT[0:n, i, :], b[0:n, :]).then_inc(M.f_free(("PT", c - 1, i)), 1)
                if c == 0:
                    act.wait_ge(gate_prod, 4)
                    run(inp[:, :, :], inp[:, :, :], ACT.Sqrt, scale=0.25).then_inc(sqrt_made, 1)
                if c == GELU_AT[0] + 1:
                    gelu_inner(0)
                for _ in range(GR_AFTER[c]):
                    cc = next(gr)
                    b = M.arrived(act, ("gr", cc))
                    nc.scalar.copy(rnnT[:, cc, :], b[:, 0:NTOK]).then_inc(M.f_free(("gr", cc)), 1)
                    if cc % 4 == 3:
                        M.emptied(act, ("gr", cc))
                        if cc > 3:
                            act.wait_ge(gelu_done, 1)
                        run(gel, rnnT[:, cc - 3:cc + 1, :], ACT.Square, scale=0.044715 ** 0.5).then_inc(gelu_sq, 1)
            gelu_inner(1)

            for m in range(KD):
                if m == 0:
                    act.wait_ge(rows_ready, 3)
                if m >= 2:
                    act.wait_ge(merge_made, m - 1)
                for w, name in enumerate(("ga", "gr_gate")):
                    b = M.arrived(act, (name, m))
                    run(mtmp[m % 2][w], b[:, 0:NTOK], ACT.Tanh, bias=hbg[:, KD * w + m:KD * w + m + 1], scale=0.5)\
                        .then_inc(M.f_free((name, m)), 1)
            act.wait_ge(merge_made, KD)
            norm_rows_load("ln1_g", "ln1_b")

            def turned(j):
                act.wait_ge(rows_ready, 3 + j + 1)
                n = OUT_ROWS[j]
                act.dma_start(z1_dram[P * j:P * j + n, :], rows[0:n, j, :]).then_inc(z1_out, 16)
                for h in range(2):
                    b = S.arrived(act, ("z1T", j, h)).rearrange("p (k n) -> p k n", n=P)
                    nc.scalar.copy(z1T[:, 4 * h:4 * h + 4, P * j:P * j + n], b[:, :, 0:n])\
                        .then_inc(S.f_free(("z1T", j, h)), 1)

            deviation(1, 0, P)
            deviation(1, 1, P)
            turned(0)
            deviation(1, 2, DEC)
            turned(1)
            turned(2)
            norm_rows_load("ln2_g", "ln2_b")
            act.wait_ge(lg_exp_in, 1)
            run(exo, exi, ACT.Exp).then_inc(lg_exp, 1)

            def gate_tanh(i, s):
                act.wait_ge(ha_full, i + 1)
                run(th_a, HB[s][:, 0:256], ACT.Tanh, scale=0.5).then_inc(ha_tanh, 1)

            def rows_out(i, s, n):
                act.wait_ge(ya_full, i + 1)
                wait_past(act, y_out[s], 32 * n)
                nc.scalar.copy(yo[s], YB[:, :]).then_inc(ya_made, 1)
                act.wait_ge(ya_made, i + 1)
                for h in range(2):
                    cols = slice(512 * h, 512 * h + 512)
                    dst = y_dram[i * CAP:i * CAP + FIRST, cols] if isinstance(i, int) else \
                        y_dram[bass.ds(i * CAP, FIRST), cols]
                    act.dma_start(dst, yo[s][FIRST * h:FIRST * h + FIRST, :]).then_inc(y_out[s], 16)

            def rest(i, b):
                act.wait_ge(hb_full, b + 1)
                run(th_b, BB[:, 0:P], ACT.Tanh, scale=0.5).then_inc(hb_tanh, 1)
                act.wait_ge(yb_full, b + 1)
                act.wait_ge(yb_out, 16 + 64 * b)
                nc.scalar.copy(yo_b, BB[:, 0:256]).then_inc(yb_made, 1)
                act.wait_ge(yb_made, b + 2)
                for j in range(4):
                    cols = slice(256 * j, 256 * j + 256)
                    dst = y_dram[i * CAP + FIRST:(i + 1) * CAP, cols] if isinstance(i, int) else \
                        y_dram[bass.ds(i * CAP + FIRST, REST), cols]
                    act.dma_start(dst, yo_b[REST * j:REST * j + REST, :]).then_inc(yb_out, 16)

            def maybe_rest(i):
                has, b = rest_words(act, i)
                with act.If(has > 0):
                    rest(i, b)

            act.wait_ge(route_done, 1)
            nc.scalar.copy(yo_b[:, 0:1], ident[:, 0:1]).then_inc(yb_made, 1)

            def round_of(n, first):
                for s in range(3):
                    i = 3 * n + s
                    gate_tanh(i, s)
                    if not (first and s == 0):
                        rows_out(i - 1, (s - 1) % 3, n if s else n - 1)
                    maybe_rest(i)

            round_of(0, True)
            with act.Fori(1, NE // 3) as n:
                round_of(n, False)
            rows_out(NE - 2, 2, NE // 3 - 1)
            gate_tanh(NE - 1, 0)
            maybe_rest(NE - 1)
            rows_out(NE - 1, 0, NE // 3)
            count, total = overflow_words(act)
            with act.If(count > 0):
                with act.Fori(0, count) as v:
                    gate_tanh(v + NE, 1)
                    rest(v + NE, total + v)
                    rows_out(v + NE, 1, v + NE // 3)
            act.wait_ge(y_out[0], 32 * (NE // 3 + 1))
            act.wait_ge(y_out[2], 32 * (NE // 3))
            act.wait_ge(y_out[1], 32 * (count + NE // 3))
            act.wait_ge(yb_out, 16 + 64 * (count + total))
            act.wait_ge(zero_out, 16 * (NITEM - 1))
            nc.scalar.copy(th_a[:, 0:1], ident[:, 0:1]).then_inc(y_written, 1)
            for j in range(3):
                deviation(2, j, OUT_ROWS[j])

        @block.vector
        def _(dve):
            step = Steps(dve, dve_step)
            V = nc.vector
            tt, stt, ts = V.tensor_tensor, V.scalar_tensor_tensor, V.tensor_scalar

            def alone(inst):
                step(inst)
                step.settle()

            def moments(j, n):
                for h in range(2):
                    step(V.bn_stats(stats[0:n, j, 6 * h:6 * h + 6], rows[0:n, j, 512 * h:512 * h + 512]))
                step.settle()
                V.bn_aggr(mv[0:n, j, :], stats[0:n, j, :]).then_inc(var_ready, 1)

            def normed(i, j, n):
                if j == 0:
                    dve.wait_ge(norm_in, 32 * (i + 1))
                dve.wait_ge(var_ready, 3 * i + j + 1)
                step(stt(rows[0:n, j, :], rows[0:n, j, :], mv[0:n, j, 0:1], gb[0:n, 0, :], ALU.subtract, ALU.mult))
                dve.wait_ge(std_ready, 3 * i + j + 1)
                alone(V.reciprocal(rstd[0:n, j:j + 1], rstd[0:n, j:j + 1]))
                stt(rows[0:n, j, :], rows[0:n, j, :], rstd[0:n, j:j + 1], gb[0:n, 1, :], ALU.mult, ALU.add)\
                    .then_inc(rows_ready, 1)

            for j in range(4):
                if j < 3:
                    dve.wait_ge(x_in[j], 16 if j < 2 else 32)
                    moments(j, TILE_ROWS[j])
                if j > 0:
                    normed(0, j - 1, TILE_ROWS[j - 1])

            b = S.arrived(dve, "vec")
            V.tensor_copy(vcol, b[:, 0:NVEC]).then_inc(S.f_free("vec"), 1)
            S.emptied(dve, "vec")
            alone(ts(sp_t[1], vc("lam", 0, KD), -1.0, None, ALU.mult))
            tt(sp_t[0], sp_t[1], vc("lam", 0, KD), ALU.max).then_inc(lam_ready, 1)
            step(ts(hba, vc("b_a", 0, KD), 0.5, None, ALU.mult))
            step(ts(hbx, vc("b_x", 0, KD), 0.5, None, ALU.mult))
            step(ts(hbg, vc("b_gate", 0, 2 * KD), 0.5, None, ALU.mult))
            step(V.memset(xpad[:, :, 0:GAP], 0.0))
            states = vc("state_conv", 0, GAP * KD).rearrange("p (j c) -> p c j", c=KD)
            step(V.tensor_copy(xpad[:, :, TP + GAP:TP + 2 * GAP], states))
            rot = [rot_t[:, i, :].rearrange("p (h d) -> p h d", d=HALF) for i in range(4)]
            for j in range(3):
                n = TILE_ROWS[j]
                for u in range(3):
                    M.emptied(dve, ("qkv", j, u))
                heads = qkv[0:n, j, 0:(NH + NKV) * HD].rearrange("p (h d) -> p h d", d=HD)
                x1, x2 = heads[:, :, 0:HALF], heads[:, :, HALF:ROT]
                cos = cst("cos")[0:n, HALF * j:HALF * j + HALF].unsqueeze(1).to_broadcast([n, NH + NKV, HALF])
                sin = cst("sin")[0:n, HALF * j:HALF * j + HALF].unsqueeze(1).to_broadcast([n, NH + NKV, HALF])
                for out, a, b in ((0, x1, cos), (1, x2, sin), (2, x2, cos), (3, x1, sin)):
                    step(tt(rot[out][0:n], a, b, ALU.mult))
                step.settle()
                step(tt(x1, rot[0][0:n], rot[1][0:n], ALU.subtract))
                step.settle()
                tt(x2, rot[2][0:n], rot[3][0:n], ALU.add).then_inc(roped, 1)
                dve.wait_ge(roped, j + 1)

            dve.wait_ge(lam_exp, 1)
            alone(ts(sp_t[2], sp_t[1], 2.0, None, ALU.add))
            alone(V.reciprocal(sp_t[2], sp_t[2]))
            alone(tt(sp_t[2], sp_t[2], sp_t[1], ALU.mult))
            alone(tt(sp_t[3], sp_t[2], sp_t[2], ALU.mult))
            alone(ts(sp_t[4], sp_t[3], 1.0 / 17, None, ALU.mult))
            for k in (15, 13, 11, 9, 7, 5, 3):
                alone(stt(sp_t[4], sp_t[4], 1.0 / k, sp_t[3], ALU.add, ALU.mult))
            alone(stt(sp_t[4], sp_t[4], 1.0, sp_t[2], ALU.add, ALU.mult))
            alone(ts(sp_t[5], vc("lam", 0, KD), -1.0, 0.0, ALU.mult, ALU.max))
            alone(stt(sp_t[5], sp_t[4], 2.0, sp_t[5], ALU.mult, ALU.add))
            alone(ts(sp4, sp_t[5], 0.5 * LRU_C, None, ALU.mult))
            ts(nsp4, sp_t[5], -0.5 * LRU_C, None, ALU.mult).then_inc(cols_ready, 1)

            for c in range(0, KD, 2):
                for q in (c, c + 1):
                    M.emptied(dve, ("xr", q))
                    step(ts(xc[:, q, :], xpad[:, q, 0:TW], vc("conv_w", q), vc("conv_b", q), ALU.mult, ALU.add))
                for j in range(1, CONVW):
                    for q in (c, c + 1):
                        dve.wait_ge(dve_step, step.n if j == CONVW - 1 and q > c else step.n - 1)
                        inst = stt(xc[:, q, :], xpad[:, q, j:j + TW], vc("conv_w", KD * j + q), xc[:, q, :], ALU.mult, ALU.add)
                        if j < CONVW - 1:
                            step(inst)
                        else:
                            inst.then_inc(conv_made, 1)

            for c in range(0, KD, 2):
                for q in (c, c + 1):
                    M.emptied(dve, ("i", q))
                two = slice(c, c + 2)
                step(stt(gate_i[:, two, :], gate_i[:, two, :], 1.0, xc[:, two, :], ALU.add, ALU.mult))
                dve.wait_ge(asq_made, c // 2 + 1)
                stt(inp[:, two, :], asq[:, :, :], 1.0, inp[:, two, :], ALU.add, ALU.mult).then_inc(gate_prod, 1)

            def softmax_max(c):
                if c == 3:
                    M.arrived(dve, ("PT", 1, 0))
                    step(V.memset(prob[1][:, :, 0:chunk_keys(3)[2]], 0.0))
                n = sum(k for _, k in chunk_blocks(c)) - (chunk_keys(c)[2] if c < 4 else 0)
                k = c % 2
                for g in range(4):
                    b = S.arrived(dve, ("S", c, g))
                    step(V.tensor_reduce(mx[:, k, g:g + 1], b[:, 0:n], AX_X, ALU.max))
                step.settle()
                alone(stt(m_c[:, k, :], mx[:, k, :], HD ** -0.5, sink, ALU.mult, ALU.max))
                alone(ts(nm[:, k, :], m_c[:, k, :], -1.0, None, ALU.mult))
                tt(m_c[:, k, :], sink, m_c[:, k, :], ALU.subtract).then_inc(max_ready, 1)

            def softmax_norm(c):
                k = c % 2
                dve.wait_ge(exp_made, c + 1)
                for g in range(4):
                    S.emptied(dve, ("S", c, g))
                alone(tt(dn[:, k, :], rs[:, k, :], es[:, k, :], ALU.add))
                alone(V.reciprocal(rd[:, k, :], dn[:, k, :]))
                n = sum(w for _, w in chunk_blocks(c))
                for g in range(4):
                    inst = ts(prob[k][:, g, 0:n], prob[k][:, g, 0:n], rd[:, k, g:g + 1], None, ALU.mult)
                inst.then_inc(prob_ready, 1)

            def recurrence(c):
                if c == 0:
                    dve.wait_ge(sqrt_made, 1)
                two = slice(c, c + 2)
                last = TP + GAP - 1
                step(tt(inp[:, two, :], inp[:, two, :], gate_i[:, two, :], ALU.mult))
                step(V.memset(dec[:, two, last:last + 1], 0.0))
                step.settle()
                alone(V.tensor_copy(inp[:, two, last:last + 1], vc("state_h", c, 2).unsqueeze(2)))
                for q in (c, c + 1):
                    step(V.tensor_tensor_scan(gate_i[:, q, :], dec[:, q, :], inp[:, q, :], 0.0, ALU.mult, ALU.add))

            def gelu_cubes(h):
                dve.wait_ge(gelu_sq, h + 1)
                M.emptied(dve, ("gr", 4 * h + 3))
                stt(gel, gel, 1.0, rnnT[:, 4 * h:4 * h + 4, :], ALU.add, ALU.mult).then_inc(gelu_cube, 1)

            def branch(h):
                four = slice(4 * h, 4 * h + 4)
                dve.wait_ge(gelu_tanh, h + 1)
                stt(rnnT[:, four, :], gel, 1.0, rnnT[:, four, :], ALU.add, ALU.mult).then_inc(gelu_done, 1)
                dve.wait_ge(gelu_done, h + 1)
                step.settle()
                step(stt(rnnT[:, four, 0:SEQ], gate_i[:, four, META:TP], 0.5, rnnT[:, four, 0:SEQ], ALU.mult, ALU.mult))
                stt(rnnT[:, four, SEQ:NTOK], gate_i[:, four, TP + GAP:TW], 0.5, rnnT[:, four, SEQ:NTOK], ALU.mult, ALU.mult)\
                    .then_inc(rnn_made, 1)

            dve.wait_ge(sink_in, 32)
            for c in range(CHUNKS + 1):
                if c < CHUNKS:
                    softmax_max(c)
                    softmax_norm(c)
                if c >= 1:
                    b = M.arrived(dve, ("PV", c - 1))
                    V.tensor_copy(attnT[:, :, CHUNK * (c - 1):CHUNK * c], b[:, 0:256].rearrange("p (h q) -> p h q", q=CHUNK))\
                        .then_inc(M.f_free(("PV", c - 1)), 1)
                if c < 4:
                    recurrence(2 * c)
                if c == GELU_AT[0] + 1:
                    gelu_cubes(0)
                if c == GELU_AT[0] + 2:
                    branch(0)
            gelu_cubes(1)
            branch(1)
            for k, at in ((0, TP), (1, XPAD - GAP)):
                V.tensor_copy(stage[:, 24 * k:24 * k + 24].rearrange("p (j c) -> p c j", c=KD), xpad[:, :, at:at + GAP])
            V.tensor_copy(stage[:, 48:56], gate_i[:, :, TP - 1])
            V.tensor_copy(stage[:, 56:64], gate_i[:, :, TW - 1]).then_inc(tail_staged, 1)

            dve.wait_ge(zero_out, 16 * (NITEM - 1))
            dve.wait_ge(yb_out, 16)
            for m in range(KD):
                for w, (gate, proj) in enumerate((("ga", "pa"), ("gr_gate", "pr"))):
                    M.emptied(dve, (gate, m))
                    b = M.arrived(dve, (proj, m))
                    stt(mtmp[m % 2][w], mtmp[m % 2][w], 1.0, b[:, 0:NTOK], ALU.add, ALU.mult)\
                        .then_inc(M.f_free((proj, m)), 1)
                for proj in ("pa", "pr"):
                    M.emptied(dve, (proj, m))
                tt(merged[:, m, :], mtmp[m % 2][0], mtmp[m % 2][1], ALU.add).then_inc(merge_made, 1)
            b = S.arrived(dve, "tail")
            V.tensor_copy(stage_rows[0:64, :], b[0:64, 0:P]).then_inc(S.f_free("tail"), 1)
            dve.wait_ge(scaled, 3)
            for j in range(3):
                n = OUT_ROWS[j]
                for h in range(2):
                    half = rows[0:n, j, 512 * h:512 * h + 512]
                    b = S.arrived(dve, ("out", j, h))
                    stt(half, b[0:n, :], 0.5, half, ALU.mult, ALU.add).then_inc(S.f_free(("out", j, h)), 1)
                    S.emptied(dve, ("out", j, h))
                moments(j, n)
                normed(1, j, n)

            def bc(ap, *shape):
                return ap.to_broadcast([P, *shape])

            def first_max(src, top, hot):
                alone(V.tensor_reduce(top, src, AX_X, ALU.max))
                alone(tt(hot, src, bc(top.unsqueeze(2), 3, 4), ALU.is_equal))
                alone(tt(hot, hot, bc(cst("tie").unsqueeze(1), 3, 4), ALU.mult))
                alone(V.tensor_reduce(tie_top, hot, AX_X, ALU.max))
                alone(tt(hot, hot, bc(tie_top.unsqueeze(2), 3, 4), ALU.is_equal))

            alone(V.memset(logit, 0.0))
            b = S.arrived(dve, "logits")
            step(V.tensor_copy(logit[:, 0:2, :], b[:, 0:40].rearrange("p (j e) -> p j e", e=20)))
            V.tensor_copy(logit[0:DEC, 2, :], b[0:DEC, 40:60]).then_inc(S.f_free("logits"), 1)
            step.settle()
            S.emptied(dve, "logits")
            glog, elog = logit[:, :, 0:NG], logit[:, :, NG:20].rearrange("p j (g e) -> p j g e", e=EPG)
            first_max(glog, g_top, g_hot)
            exi3 = exi[:, 0:12].rearrange("p (j g) -> p j g", g=NG)
            step(tt(exi3, glog, bc(g_top.unsqueeze(2), 3, 4), ALU.subtract))
            for j in range(3):
                step(tt(cross[:, j].rearrange("p g e -> p g e"), elog[:, j], bc(g_hot[:, j, :].unsqueeze(2), 4, 4), ALU.mult))
            step.settle()
            for j in range(3):
                step(V.tensor_reduce(e_sel[:, j, :], cross[:, j].rearrange("p g e -> p e g"), AX_X, ALU.add))
            step.settle()
            first_max(e_sel, top[0], hot[0])
            alone(stt(e_sel, hot[0], -1e30, e_sel, ALU.mult, ALU.add))
            first_max(e_sel, top[1], hot[1])
            tt(exi[:, 12:15], top[1], top[0], ALU.subtract).then_inc(lg_exp_in, 1)
            for k in range(2):
                for j in range(3):
                    step(tt(e_hot[k][:, j].rearrange("p (g e) -> p g e", e=EPG), bc(g_hot[:, j, :].unsqueeze(2), 4, 4),
                            bc(hot[k][:, j, :].unsqueeze(1), 4, 4), ALU.mult))
            step.settle()
            alone(tt(e_sum, e_hot[0], e_hot[1], ALU.add))
            tt(e_sum, e_sum, bc(cst("valid").unsqueeze(2), 3, NE), ALU.mult).then_inc(chosen, 1)
            dve.wait_ge(lg_exp, 1)
            step(V.tensor_reduce(g_top, exo[:, 0:12].rearrange("p (j g) -> p j g", g=NG), AX_X, ALU.add))
            step(ts(tie_top, exo[:, 12:15], 1.0, None, ALU.add))
            step.settle()
            alone(tt(g_top, g_top, tie_top, ALU.mult))
            alone(V.reciprocal(weight[0], g_top))
            alone(tt(weight[1], weight[0], exo[:, 12:15], ALU.mult))
            b = S.arrived(dve, "ranks")
            step(V.tensor_copy(rank, b[:, 0:3 * NE].rearrange("p (j e) -> p j e", e=NE)))
            V.tensor_copy(count_e, b[:, 3 * NE:4 * NE]).then_inc(S.f_free("ranks"), 1)
            step.settle()
            S.emptied(dve, "ranks")
            alone(ts(ov, count_e, float(CAP), None, ALU.is_gt))
            for m in range(2, LEVELS + 1):
                alone(stt(ov, count_e, float(CAP * m), ov, ALU.is_gt, ALU.add))
            alone(V.tensor_tensor_scan(ov_end, ones[:, 0:NE], ov, 0.0, ALU.mult, ALU.add))
            alone(tt(base, ov_end, ov, ALU.subtract))
            alone(tt(base, base, cst("expert"), ALU.subtract))
            alone(ts(level, rank, float(CAP), None, ALU.is_ge))
            for m in range(2, LEVELS + 1):
                alone(stt(level, rank, float(CAP * m), level, ALU.is_ge, ALU.add))
            alone(stt(rank, level, -float(CAP), rank, ALU.mult, ALU.add))
            alone(tt(where, level, bc(base.unsqueeze(1), 3, NE), ALU.add))
            alone(ts(level, level, 1.0, None, ALU.min))
            alone(stt(where, where, float(NE - 1), level, ALU.add, ALU.mult))
            alone(tt(where, where, bc(cst("expert").unsqueeze(1), 3, NE), ALU.add))
            for k in range(2):
                alone(tt(e_sum2, e_hot[k], where, ALU.mult))
                alone(V.tensor_reduce(item_of[k], e_sum2, AX_X, ALU.add))
                alone(tt(e_sum2, e_hot[k], rank, ALU.mult))
                alone(V.tensor_reduce(rank_of[k], e_sum2, AX_X, ALU.add))
                alone(stt(slot_f, item_of[k], float(CAP), rank_of[k], ALU.mult, ALU.add))
                step(V.tensor_copy(slot_i[:, k, :], slot_f))
                rh = rank_hot[:, k, :].rearrange("p (j c) -> p j c", c=CAP)
                ih = item_hot[:, k, :].rearrange("p (j i) -> p j i", i=NITEM)
                step(tt(rh, bc(cst("iota_cap").unsqueeze(1), 3, CAP), bc(rank_of[k].unsqueeze(2), 3, CAP), ALU.is_equal))
                alone(tt(ih, bc(cst("iota_item").unsqueeze(1), 3, NITEM), bc(item_of[k].unsqueeze(2), 3, NITEM), ALU.is_equal))
                inst = tt(ih, ih, bc(cst("token").unsqueeze(2), 3, NITEM), ALU.mult)
                if k == 0:
                    alone(inst)
            inst.then_inc(selected, 1)
            alone(tt(ov_cmp, bc(ov_end.unsqueeze(1), NOV, NE), bc(cst("iota_ov").unsqueeze(2), NOV, NE), ALU.is_le))
            alone(V.tensor_reduce(ov_exp, ov_cmp, AX_X, ALU.add))
            alone(ts(ov_exp, ov_exp, float(NE - 1), None, ALU.min))
            step(V.tensor_copy(ctrl_i[:, 0:NOV], ov_exp))
            step(V.tensor_copy(ctrl_i[:, W_COUNT:W_REST], ov_end[:, NE - 1:NE]))
            alone(ts(ov, count_e, float(FIRST), None, ALU.is_gt))
            alone(V.tensor_tensor_scan(ov_end, ones[:, 0:NE], ov, 0.0, ALU.mult, ALU.add))
            step(V.tensor_copy(ctrl_i[:, W_REST:W_BEFORE], ov))
            step(V.tensor_copy(ctrl_i[:, W_TOTAL:NWORD], ov_end[:, NE - 1:NE]))
            tt(ctrl_i[:, W_BEFORE:W_TOTAL], ov_end, ov, ALU.subtract).then_inc(ctrl_done, 1)
            dve.wait_ge(ctrl_done, 1)
            b = S.arrived(dve, "index")
            V.tensor_copy(index_i[0:CAP, :], b[0:CAP, 0:NITEM]).then_inc(route_done, 1)
            dve.wait_ge(route_done, 1)

            def columns(i, s):
                dve.wait_ge(xt_full, i + 1)
                for h in range(2):
                    cp = V.tensor_copy(xT[s][:, 4 * h:4 * h + 4, :], TB[h][:, 0:4 * CAP].rearrange("p (k c) -> p k c", c=CAP))
                cp.then_inc(xt_made, 1)

            def silu(i, th, out, gate, up, tanh, half, made):
                dve.wait_ge(tanh, i + 1)
                stt(th, th, 1.0, gate, ALU.add, ALU.mult).then_inc(half, 1)
                dve.wait_ge(half, i + 1)
                stt(out, th, 0.5, up, ALU.mult, ALU.mult).then_inc(made, 1)

            def silu_first(i, s):
                silu(i, th_a, hid_a, HB[s][:, 0:256], HB[s][:, 256:512], ha_tanh, ha_half, ha_made)

            def hidden_columns(i):
                dve.wait_ge(hta_full, i + 1)
                V.tensor_copy(hT_a, TH[:, 0:256]).then_inc(hta_made, 1)

            def rest(b):
                silu(b, th_b, hid_b, BB[:, 0:P], BB[:, P:2 * P], hb_tanh, hb_half, hb_made)
                dve.wait_ge(htb_full, b + 1)
                V.tensor_copy(hT_b, BB[:, 2 * P:3 * P]).then_inc(htb_made, 1)

            def maybe_rest(i):
                has, b = rest_words(dve, i)
                with dve.If(has > 0):
                    rest(b)

            columns(0, 0)

            def round_of(n):
                for s in range(3):
                    i = 3 * n + s
                    silu_first(i, s)
                    columns(i + 1, (s + 1) % 3)
                    maybe_rest(i)
                    hidden_columns(i)

            with dve.Fori(0, NE // 3) as n:
                round_of(n)
            silu_first(NE - 1, 0)
            maybe_rest(NE - 1)
            hidden_columns(NE - 1)
            count, total = overflow_words(dve)
            with dve.If(count > 0):
                with dve.Fori(0, count) as v:
                    columns(v + NE, 1)
                    silu_first(v + NE, 1)
                    rest(total + v)
                    hidden_columns(v + NE)

            dve.wait_ge(rows_scaled2, 3)
            for j in range(4):
                if j < 3:
                    n = OUT_ROWS[j]
                    dve.wait_ge(yg_in[j], 32)
                    for k in range(2):
                        alone(stt(rows[0:n, j, :], yg[j][k][0:n, :], weight[k][0:n, j:j + 1], rows[0:n, j, :], ALU.mult, ALU.add))
                    moments(j, n)
                if j > 0:
                    normed(2, j - 1, OUT_ROWS[j - 1])


INPUTS = ["x_prompt", "x_sample", "cache_meta_k", "cache_meta_v", "cache_win_k", "cache_win_v", "state_conv", "state_h",
          "meta_tokens", "ln_in_g", "ln_in_b", "w_in", "b_gate", "attn_sinks", "conv_w", "conv_b", "w_rg_a", "b_rg_a",
          "w_rg_x", "b_rg_x", "lru_lambda", "w_branch_attn", "w_branch_rnn", "w_out", "ln1_g", "ln1_b", "w_group",
          "b_group", "w_router", "b_router", "w_gate", "w_up", "w_down", "ln2_g", "ln2_b"]
OUTPUTS = [(1, SEQ, D), (1, DEC, D), (1, 1, META, NKV, HD), (1, 1, META, NKV, HD), (1, 1, WIN, NKV, HD),
           (1, 1, WIN, NKV, HD), (1, 1, GAP, D), (1, 1, D), (1, 1, DEC, NKV, HD), (1, 1, DEC, NKV, HD),
           (1, 1, GAP, D), (1, 1, D)]


def kernel(**inputs):
    import concourse.bacc as bacc
    from concourse.bass_utils import run_bass_kernel_spmd

    nc = bacc.Bacc("TRN2", target_bir_lowering=False, num_devices=1)
    arrays, aps = {}, {}
    for name in INPUTS:
        arrays[f"in_{name}"] = np.ascontiguousarray(inputs[name])
    arrays["in_const"] = constants()
    for key, a in arrays.items():
        aps[key[3:]] = nc.dram_tensor(key, a.shape, F32, kind="ExternalInput").ap()
    outs = [nc.dram_tensor(f"out_{i}", shape, F32, kind="ExternalOutput").ap() for i, shape in enumerate(OUTPUTS)]
    build(nc, aps, outs)
    r = run_bass_kernel_spmd(nc, [arrays], core_ids=[0])
    return tuple(r.results[0][f"out_{i}"] for i in range(len(OUTPUTS)))
```

```python
from contextlib import ExitStack

import numpy as np

import concourse.bass as bass
from concourse import mybir

F32 = mybir.dt.float32
F32R = mybir.dt.float32r
I32 = mybir.dt.int32
ALU = mybir.AluOpType
ACT = mybir.ActivationFunctionType
AX_X = mybir.AxisListType.X

P = 128
D = 1024
KD = D // P
SEQ, DEC, META = 256, 64, 16
NTOK = SEQ + DEC
NALL = NTOK + META
CHUNK, WIN = 64, 128
NH, NKV, HD = 8, 2, 64
ROT = HD // 4
HALF = ROT // 2
THETA = 500000.0
LRU_C = 8.0
PAST = 512
CONVW = 4
QKV = (NH + 2 * NKV) * HD
ALPHA = 2.0 ** 0.25
EPS = 1e-5
NG, EPG = 4, 4
NE = NG * EPG
FE = 512
KF = FE // P
TILE_ROWS = (128, 128, DEC + META)
OUT_ROWS = (128, 128, DEC)
TP = META + SEQ
GAP = CONVW - 1
TW = TP + GAP + DEC
XPAD = TW + GAP
FIRST, REST = 64, 32
CAP = FIRST + REST
LEVELS = NTOK // CAP
NOV = 2 * NTOK // (CAP + 1)
NITEM = NE + NOV
W_COUNT, W_REST, W_BEFORE, W_TOTAL = NOV, NOV + 1, NOV + 1 + NE, NOV + 1 + 2 * NE
NWORD = W_TOTAL + 1
UNIT = KD * 256
RING = 3
U_QKV, U_XR, U_RG, U_GR, U_MERGE, U_OUT = 0, 3, 7, 8, 12, 28
NUNIT = 32
SPLIT = [*range(U_RG), *range(U_GR, U_MERGE)] + [u for u in range(U_MERGE, U_OUT) if (u - U_MERGE) % 4 < 2]
SPLIT_AT = ((9, 0), (10, 1), (11, 3))
C_XR = QKV
C_GR = C_XR + D
C_GL = C_GR + D


def const_layout():
    cols, at = {}, 0
    for name, n in (("ident", P), ("before", P), ("ones", P), ("cos", 3 * HALF), ("sin", 3 * HALF),
                    ("iota_cap", CAP), ("iota_item", NITEM), ("iota_ov", NOV), ("expert", NE),
                    ("tie", 4), ("token", 3), ("valid", 3), ("eps", 1)):
        cols[name] = (at, at + n)
        at += n
    return cols, at


CC, NCONST = const_layout()


def constants():
    c = np.zeros((P, NCONST), np.float32)

    def put(name, v):
        c[:, CC[name][0]:CC[name][1]] = v

    row = np.arange(P)
    put("ident", np.eye(P))
    put("before", (row[:, None] < row[None, :]).astype(np.float32))
    put("ones", 1.0)
    pos = np.zeros((P, 3), np.float32)
    pos[:, 0] = META + row
    pos[:, 1] = META + P + row
    pos[:DEC, 2] = META + PAST + row[:DEC]
    pos[DEC:DEC + META, 2] = row[:META]
    inv = np.float32(THETA) ** (-np.arange(HALF, dtype=np.float32) / np.float32(HALF))
    ang = pos[:, :, None] * inv.astype(np.float32)[None, None, :]
    put("cos", np.cos(ang).reshape(P, -1))
    put("sin", np.sin(ang).reshape(P, -1))
    put("iota_cap", np.arange(CAP))
    put("iota_item", np.arange(NITEM))
    put("iota_ov", np.arange(NOV))
    put("expert", np.arange(NE))
    put("tie", [4, 3, 2, 1])
    valid = np.array([[float(p < OUT_ROWS[j]) for j in range(3)] for p in range(P)])
    put("valid", valid)
    put("token", valid * (row[:, None] + P * np.arange(3)[None, :]))
    put("eps", EPS)
    return c


VEC = {}
_at = 0
for _n, _k in (("conv_w", CONVW * KD), ("conv_b", KD), ("b_a", KD), ("b_x", KD), ("lam", KD),
               ("state_h", KD), ("state_conv", GAP * KD), ("b_gate", 2 * KD)):
    VEC[_n] = (_at, _at + _k)
    _at += _k
NVEC = _at


class Ring:

    def __init__(self, banks, full, free, names):
        self.banks, self.full, self.free = banks, full, free
        self.index = {n: i for i, n in enumerate(names)}

    def bank(self, name):
        return self.banks[self.index[name] % len(self.banks)]

    def sems(self, name):
        i = self.index[name]
        n = len(self.banks)
        return self.full[i % n], self.free[i % n], i // n

    def claim(self, eng, name):
        _, free, n = self.sems(name)
        if n >= 1:
            eng.wait_ge(free, n)
        return self.bank(name)

    def arrived(self, eng, name):
        full, _, n = self.sems(name)
        eng.wait_ge(full, n + 1)
        return self.bank(name)

    def emptied(self, eng, name):
        _, free, n = self.sems(name)
        eng.wait_ge(free, n + 1)

    def f_full(self, name):
        return self.sems(name)[0]

    def f_free(self, name):
        return self.sems(name)[1]


class Steps:

    def __init__(self, eng, sem):
        self.eng, self.sem, self.n = eng, sem, 0

    def __call__(self, inst):
        inst.then_inc(self.sem, 1)
        self.n += 1
        return self.n

    def settle(self):
        self.eng.wait_ge(self.sem, self.n)


def wait_past(eng, sem, n):
    if not (isinstance(n, int) and n == 0):
        eng.wait_ge(sem, n)


CHUNKS = 5


def chunk_keys(c):
    lo = max(0, (c - 2) * CHUNK)
    hi = (c + 1) * CHUNK
    return lo, hi, lo % P


def chunk_blocks(c):
    if c == 4:
        return [(0, P), (P, DEC + META)]
    lo, hi, off = chunk_keys(c)
    out, at, end = [], 0, off + hi - lo
    while at < end:
        out.append((at, min(P, end - at)))
        at += P
    return out + [(end, META)]


def pe_fills():
    m, s = [], []
    for j in range(3):
        s += [("zT", j, h) for h in range(2)]
    m += [("qkv", j, u) for u in range(3) for j in range(3)]
    s.append("vec")
    m += [("xr", c) for c in range(KD)]
    m += [("QT", j) for j in range(3)] + ["KT", "KS"]
    for c in range(KD):
        m += [("r", c), ("i", c)]
    gr = iter(range(KD))
    for c in range(CHUNKS + 1):
        if c < CHUNKS:
            s += [("S", c, g) for g in range(4)]
        turned = [("PT", c - 1, b) for b in range(len(chunk_blocks(c - 1)))] if c >= 1 else []
        grs = [("gr", next(gr)) for _ in range(GR_AFTER[c])]
        m += turned + grs if c < CHUNKS else grs + turned + [("ga", 0)]
        if c >= 1:
            m.append(("PV", c - 1))
    for p in range(0, KD, 2):
        m += [(kind, mm) for kind in ("ga", "gr_gate", "pa", "pr") for mm in (p, p + 1) if (kind, mm) != ("ga", 0)]
    s.append("tail")
    for kind, j in OUT_ORDER:
        if (kind, j) == ("z1T", 2):
            s.append("logits")
        s += [(kind, j, h) for h in range(2)]
    s += ["ranks", "index"]
    return m, s


OUT_ORDER = (("out", 0), ("out", 1), ("z1T", 0), ("out", 2), ("z1T", 1), ("z1T", 2))
GR_AFTER = [3, 1, 1, 1, 1, 1]
HALF_GR = next(c for c in range(CHUNKS) if sum(GR_AFTER[:c + 1]) >= KD // 2)


def build(nc, t, outs):
    (y_prompt, y_sample, meta_k, meta_v, win_k, win_v, conv_p, h_p, new_k, new_v, conv_s, h_s) = outs
    with ExitStack() as ctx:
        def sb(name, shape, dt=F32):
            return ctx.enter_context(nc.sbuf_tensor(name, shape, dt))

        def sem(name):
            return ctx.enter_context(nc.semaphore(name))

        EXP = KD * FE + KD * FE + KF * D
        HALF_Z = KD // 2 * (NALL + META)
        with ExitStack() as under:
            def lower(name, n, dt=F32R):
                return under.enter_context(nc.sbuf_tensor(name, [P, n], dt))

            lower("under_slots", 2 * EXP - HALF_Z, F32)
            z_low_0 = lower("z_low_0", HALF_Z)
            low_t = lower("weights_low", RING * UNIT)
            high_t = lower("weights_high", 2 * UNIT)
            z_low_1 = lower("z_low_1", HALF_Z)
            lower("under_rest", EXP - (RING + 2) * UNIT - HALF_Z + 3 * D, F32)
            z_high = lower("z_high", 2 * HALF_Z)
        slots = sb("expert_slots", [P, 3 * EXP])
        NWORK = 3 * D + KD * (NALL + META) + 2 * KD * NTOK + 4 * NTOK + 160
        work = sb("work", [P, NWORK])
        const = sb("const", [P, NCONST])
        small = sb("small", [P, 900])
        index_i = sb("index_i", [P, NITEM], I32)
        slot_i = sb("slot_i", [P, 2, 3], I32)
        ctrl_i = sb("ctrl_i", [P, NWORD], I32)

        class Area:
            def __init__(self, tensor, base, end):
                self.t, self.at, self.end = tensor, base, end

            def take(self, *dims):
                n = int(np.prod(dims))
                ap = self.t[:, self.at:self.at + n]
                self.at += n
                assert self.at <= self.end, (self.at, self.end)
                if len(dims) == 2:
                    ap = ap.rearrange("p (a b) -> p a b", b=dims[1])
                if len(dims) == 3:
                    ap = ap.rearrange("p (a b c) -> p a b c", b=dims[1], c=dims[2])
                return ap

        def cst(name):
            return const[:, CC[name][0]:CC[name][1]]

        ident, before, ones = cst("ident"), cst("before"), cst("ones")

        scr = Area(slots, 0, 2 * EXP - HALF_Z)
        ring_end = 2 * EXP + (RING + 2) * UNIT + HALF_Z
        scr2 = Area(slots, ring_end, 3 * EXP)
        qkv = scr.take(3, QKV)
        qT = scr.take(CHUNKS, 4 * CHUNK)
        kT = scr.take(NALL)
        kTs = scr.take(WIN + DEC + META)
        vW = scr.take(P)
        kW, kS = scr.take(P), scr.take(P)
        prob = [scr.take(4, 272), scr.take(4, 272)]
        pT = scr.take(3, 512)
        xpad = scr.take(KD, XPAD)
        xc = scr.take(KD, TW)
        dec = scr.take(KD, TW)
        inp = scr.take(KD, TW)
        gate_i = scr.take(KD, TW)
        gel_at = scr.at
        th_r = scr.take(2, TW)
        asq = scr.take(2, TW)
        gel = slots[:, gel_at:gel_at + 4 * NTOK].rearrange("p (c n) -> p c n", n=NTOK)
        zl = [z[:, :].rearrange("p (k n) -> p k n", n=NALL + META) for z in (z_low_0, z_low_1)]
        rot_t = scr2.take(4, 80)
        vM, vS = scr2.take(P), scr2.take(P)
        ring = [slots[:, 2 * EXP + i * UNIT:2 * EXP + (i + 1) * UNIT] for i in range(RING + 1)]

        def at_ring(u):
            return RING if u == NUNIT - 1 else u % RING
        high = [high_t[:, i * UNIT:(i + 1) * UNIT] for i in range(2)]
        low = [low_t[:, i * UNIT:(i + 1) * UNIT] for i in range(RING)]
        w_gate = [slots[:, i * EXP:i * EXP + KD * FE].rearrange("p (k f) -> p k f", f=FE) for i in range(3)]
        w_up = [slots[:, i * EXP + KD * FE:i * EXP + 2 * KD * FE].rearrange("p (k f) -> p k f", f=FE)
                for i in range(3)]
        w_down = [slots[:, i * EXP + 2 * KD * FE:(i + 1) * EXP].rearrange("p (k f) -> p k f", f=D)
                  for i in range(3)]

        area = Area(work, 0, NWORK)
        rows = area.take(3, D)
        area.take(2 * HALF_Z)
        zh = z_high[:, :].rearrange("p (k n) -> p k n", n=NALL + META)
        rnnT = area.take(KD, NTOK)
        attnT = area.take(4, NTOK)
        merged = area.take(KD, NTOK)
        z1T = rnnT
        ea = Area(work, 3 * D, NWORK)
        xg = [ea.take(D) for _ in range(3)]
        xT = [ea.take(KD, CAP) for _ in range(3)]
        yo = [ea.take(512) for _ in range(3)]
        th_a, hid_a, hT_a = ea.take(256), ea.take(256), ea.take(256)
        th_b, hid_b, hT_b, yo_b = ea.take(P), ea.take(P), ea.take(P), ea.take(256)
        gb = sb("norm_rows", [P, 2, D])
        mtmp = [[gb[:, i, NTOK * w:NTOK * w + NTOK] for w in range(2)] for i in range(2)]
        fin = Area(slots, 0, 3 * EXP)
        yg = [[fin.take(D) for _ in range(2)] for _ in range(3)]

        sm = Area(small, 0, 900)
        vrow = sm.take(P)
        vcol = sm.take(NVEC)
        stage = sm.take(64)
        stage_rows = sm.take(P)
        sink = sm.take(4)
        stats = sm.take(3, 12)
        mv = sm.take(3, 2)
        rstd = sm.take(3)
        hba, hbx = sm.take(KD), sm.take(KD)
        hbg = sm.take(2 * KD)
        sp4, nsp4 = sm.take(KD), sm.take(KD)
        sp_t = [sm.take(KD) for _ in range(6)]
        mx, m_c, nm, es, rs, dn, rd = [sm.take(2, 4) for _ in range(7)]
        wr = sb("router", [P, KD, 20])
        br = sb("router_bias", [1, 20])
        rt = Area(work, 3 * D + KD * (NALL + META) + KD * NTOK + 4 * NTOK, NWORK)
        logit = rt.take(3, 20)
        e_sum = rt.take(3, NE)
        rank_hot = rt.take(2, 3 * CAP)
        item_hot = rt.take(2, 3 * NITEM)
        weight = [sm.take(3) for _ in range(2)]
        exi, exo = rt.take(15), rt.take(15)
        g_top, tie_top, slot_f = rt.take(3), rt.take(3), rt.take(6)
        top = [rt.take(3) for _ in range(2)]
        place = rt.take(12)
        g_hot, e_sel = rt.take(3, 4), rt.take(3, 4)
        hot = [rt.take(3, 4) for _ in range(2)]
        cross = rt.take(3, 4, 4)
        e_hot = [rt.take(3, NE) for _ in range(2)]
        rank, level, past = (rt.take(3, NE) for _ in range(3))
        spot = rt.take(2, 3 * NE).rearrange("p w (j e) -> p w j e", e=NE)
        e_pick = rt.take(2, 6 * NE).rearrange("p w (k j e) -> p w k j e", j=3, e=NE)
        count_e, ov, ov_end, base = (rt.take(NE) for _ in range(4))
        ov_cmp, ov_exp = rt.take(NOV, NE), rt.take(NOV)
        eps = cst("eps")

        def vc(name, i, n=1):
            return vcol[:, VEC[name][0] + i:VEC[name][0] + i + n]

        banks = [ctx.enter_context(nc.psum_tensor(f"bank{i}", [P, 512], F32)) for i in range(8)]
        names_m, names_s = pe_fills()
        M = Ring(banks[0:4], [sem(f"m_full{i}") for i in range(4)], [sem(f"m_free{i}") for i in range(4)], names_m)
        S = Ring(banks[4:8], [sem(f"s_full{i}") for i in range(4)], [sem(f"s_free{i}") for i in range(4)], names_s)

        TB, HB, TH, YB, BB = banks[0:2], banks[2:5], banks[5], banks[6], banks[7]
        z1_dram = nc.dram_tensor("z1_rows", [NTOK, D], F32, kind="Internal")
        y_dram = nc.dram_tensor("expert_rows", [NITEM * CAP, D], F32, kind="Internal")

        const_in = sem("const_in")
        lam_ready, lam_exp, cols_ready = sem("lam_ready"), sem("lam_exp"), sem("cols_ready")
        x_in = [sem(f"x_in{j}") for j in range(3)]
        norm_in = sem("norm_in")
        vec_in = sem("vec_in")
        sink_in = sem("sink_in")
        cache_in = sem("cache_in")
        vm_in = sem("vm_in")
        router_in = sem("router_in")
        unit_in = [sem(f"unit_in{i}") for i in range(RING + 1)]
        dve_step, act_step = sem("dve_step"), sem("act_step")
        var_ready = sem("var_ready")
        std_ready = sem("std_ready")
        rows_ready = sem("rows_ready")
        scaled = sem("scaled")
        roped = sem("roped")
        side_keys = sem("side_keys")
        conv_made = sem("conv_made")
        high_made, low_made, zh_made = sem("high_made"), sem("low_made"), sem("zh_made")
        gate_prod = sem("gate_prod")
        sqrt_made = sem("sqrt_made")
        max_ready = sem("max_ready")
        exp_made = sem("exp_made")
        prob_ready = sem("prob_ready")
        gelu_sq, gelu_cube, gelu_tanh, gelu_done = [sem(f"gelu_{n}") for n in ("sq", "cube", "tanh", "done")]
        rnn_made = sem("rnn_made")
        tail_staged = sem("tail_staged")
        merge_made = sem("merge_made")
        kv_out = sem("kv_out")
        tail_out = sem("tail_out")
        z1_out = sem("z1_out")
        lg_exp_in, lg_exp = sem("lg_exp_in"), sem("lg_exp")
        chosen = sem("chosen")
        selected = sem("selected")
        route_done = sem("route_done")
        zeroed, zero_out = sem("zeroed"), sem("zero_out")
        ctrl_done = sem("ctrl_done")
        rows_scaled2 = sem("rows_scaled2")
        g_in = [sem(f"gate_in{i}") for i in range(3)]
        u_in = [sem(f"up_in{i}") for i in range(3)]
        d_in = [sem(f"down_in{i}") for i in range(3)]
        xg_in = [sem(f"xg_in{i}") for i in range(3)]
        xt_full, xt_made = sem("xt_full"), sem("xt_made")
        ha_full, ha_tanh, ha_half, ha_made = [sem(f"ha_{n}") for n in ("full", "tanh", "half", "made")]
        hta_full, hta_made = sem("hta_full"), sem("hta_made")
        ya_full, ya_made = sem("ya_full"), sem("ya_made")
        y_out = [sem(f"y_out{i}") for i in range(3)]
        hb_full, hb_tanh, hb_half, hb_made = [sem(f"hb_{n}") for n in ("full", "tanh", "half", "made")]
        htb_full, htb_made = sem("htb_full"), sem("htb_made")
        yb_full, yb_made, yb_out = sem("yb_full"), sem("yb_made"), sem("yb_out")
        y_written = sem("y_written")
        yg_in = [sem(f"yg_in{j}") for j in range(3)]
        out_done = sem("out_done")

        def word(eng, at, most):
            return eng.value_load(ctrl_i[0:1, at:at + 1] if isinstance(at, int) else ctrl_i[0:1, bass.ds(at, 1)],
                                  min_val=0, max_val=most)

        def rest_words(eng, i):
            return word(eng, i + W_REST, 1), word(eng, i + W_BEFORE, NE)

        def overflow_words(eng):
            return word(eng, W_COUNT, NOV), word(eng, W_TOTAL, NE)

        def unit_consumed(eng, u):
            if u < U_XR:
                M.arrived(eng, ("qkv", 2, u))
            elif u < U_RG:
                M.arrived(eng, ("xr", 2 * (u - U_XR) + 1))
            elif u == U_RG:
                M.arrived(eng, ("i", KD - 1))
            elif u < U_MERGE:
                M.arrived(eng, ("gr", 2 * (u - U_GR) + 1))
            elif u < U_OUT:
                M.arrived(eng, (("ga", "gr_gate", "pa", "pr")[(u - U_MERGE) % 4], 2 * ((u - U_MERGE) // 4) + 1))
            else:
                S.arrived(eng, ("out", 2, (u - U_OUT) // 2))

        def split_order(u):
            return SPLIT.index(u)

        def high_of(eng, u):
            n = split_order(u)
            unit_loaded(eng, u)
            if n >= 2:
                unit_consumed(eng, SPLIT[n - 2])
            nc.scalar.copy(high[n % 2], ring[u % RING]).then_inc(high_made, 1)

        def low_of(eng, u, unit_engine=nc.vector):
            eng.wait_ge(high_made, split_order(u) + 1)
            unit_engine.tensor_tensor(low[u % RING], ring[u % RING], high[split_order(u) % 2], ALU.subtract)\
                .then_inc(low_made, 1)

        def unit_loaded(eng, u):
            n = 0
            for v in [v for v in range(u + 1) if at_ring(v) == at_ring(u)]:
                n += 32 if v == U_RG or (U_MERGE <= v < U_OUT and (v - U_MERGE) % 4 == 2) else 16
            eng.wait_ge(unit_in[at_ring(u)], n)

        block = ctx.enter_context(nc.Block())

        @block.sync
        def _(sp):
            w_in = t["w_in"][0].rearrange("(k p) n -> p k n", p=P)
            w_pa, w_pr, w_o = t["w_branch_attn"][0], t["w_branch_rnn"][0], t["w_out"][0]
            xp, xs = t["x_prompt"][0], t["x_sample"][0]
            sp.dma_start(rows[:, 0, :], xp[0:P, :]).then_inc(x_in[0], 16)
            sp.dma_start(const[:], t["const"]).then_inc(const_in, 16)
            sp.dma_start(rows[:, 1, :], xp[P:2 * P, :]).then_inc(x_in[1], 16)
            sp.dma_start(rows[0:DEC, 2, :], xs).then_inc(x_in[2], 16)
            sp.dma_start(rows[DEC:DEC + META, 2, :], t["meta_tokens"]).then_inc(x_in[2], 16)

            def unit(u):
                if u == NUNIT - 1:
                    unit_consumed(sp, SPLIT[-1])
                    unit_consumed(sp, SPLIT[-2])
                elif u >= RING:
                    unit_consumed(sp, u - RING)
                dst, done = ring[at_ring(u)], unit_in[at_ring(u)]
                wide = dst.rearrange("p (k n) -> p k n", n=256)
                if u == U_RG:
                    half = dst.rearrange("p (w n e) -> p w n e", w=2, e=P)
                    sp.dma_start(half[:, 0], t["w_rg_a"][0].rearrange("n c e -> c n e")).then_inc(done, 16)
                    sp.dma_start(half[:, 1], t["w_rg_x"][0].rearrange("n c e -> c n e")).then_inc(done, 16)
                elif u < U_MERGE:
                    col = 256 * u if u < U_RG else C_GR + 256 * (u - U_GR)
                    sp.dma_start(wide, w_in[:, :, col:col + 256]).then_inc(done, 16)
                elif u < U_OUT:
                    mp, kind = divmod(u - U_MERGE, 4)
                    cols = slice(256 * mp, 256 * mp + 256)
                    if kind < 2:
                        col = C_GL + D * kind + 256 * mp
                        sp.dma_start(wide, w_in[:, :, col:col + 256]).then_inc(done, 16)
                    elif kind == 2:
                        for g in range(NKV):
                            src = w_pa[256 * g:256 * g + 256, cols].rearrange("(c d) n -> d c n", d=HD)
                            sp.dma_start(wide[HD * g:HD * g + HD, 0:4], src).then_inc(done, 16)
                    else:
                        sp.dma_start(wide, w_pr[:, cols].rearrange("(k p) n -> p k n", p=P)).then_inc(done, 16)
                else:
                    c = 256 * (u - U_OUT)
                    sp.dma_start(wide, w_o[:, c:c + 256].rearrange("(k p) n -> p k n", p=P)).then_inc(done, 16)

            def load_hidden(e, s):
                src = (t["w_gate"][0, e:e + 1], t["w_up"][0, e:e + 1]) if isinstance(e, int) else \
                    (t["w_gate"][0, bass.ds(e, 1)], t["w_up"][0, bass.ds(e, 1)])
                sp.dma_start(w_gate[s], src[0].rearrange("o (k p) f -> p (o k) f", p=P)).then_inc(g_in[s], 16)
                sp.dma_start(w_up[s], src[1].rearrange("o (k p) f -> p (o k) f", p=P)).then_inc(u_in[s], 16)

            def load_down(e, s):
                src = t["w_down"][0, e:e + 1] if isinstance(e, int) else t["w_down"][0, bass.ds(e, 1)]
                sp.dma_start(w_down[s], src.rearrange("o (k p) f -> p (o k) f", p=P)).then_inc(d_in[s], 16)

            def expert(e, s):
                load_hidden(e, s)
                load_down(e, s)

            def expert_part(e, part):
                dst = (w_gate, w_up, w_down)[part][e]
                src = (t["w_gate"], t["w_up"], t["w_down"])[part][0, e].rearrange("(k p) f -> p k f", p=P)
                sp.dma_start(dst, src).then_inc((g_in, u_in, d_in)[part][e], 16)

            early = U_MERGE + 6
            for u in range(early):
                unit(u)
            sp.wait_ge(rnn_made, 2)
            M.emptied(sp, ("PV", CHUNKS - 1))
            sp.wait_ge(tail_staged, 1)
            sp.wait_ge(kv_out, 16 * 6)
            for u in range(early, NUNIT):
                unit(u)
                part, odd = divmod(u - early, 2)
                if not odd and part < 5:
                    expert_part(*divmod(part, 3))
                if u == U_OUT + 1:
                    expert_part(1, 2)
            for u in range(U_OUT, NUNIT):
                unit_consumed(sp, u)
            expert(2, 2)
            with sp.Fori(1, NE // 3) as n:
                for s in range(3):
                    i = 3 * n + s
                    sp.wait_ge(hta_full, i - 2)
                    load_hidden(i, s)
                    sp.wait_ge(ya_full, i - 2)
                    load_down(i, s)
            sp.wait_ge(hta_full, NE - 3)
            load_hidden(NE - 1, 0)
            sp.wait_ge(ya_full, NE - 3)
            load_down(NE - 1, 0)
            sp.wait_ge(ctrl_done, 1)
            count = sp.value_load(ctrl_i[0:1, W_COUNT:W_COUNT + 1], min_val=0, max_val=NOV)
            with sp.If(count > 0):
                with sp.Fori(0, count) as v:
                    sp.wait_ge(ya_full, v + NE)
                    e = sp.value_load(ctrl_i[0:1, bass.ds(v, 1)], min_val=0, max_val=NE - 1)
                    expert(e, 1)
            for j, dst in enumerate((y_prompt[0, 0:P, :], y_prompt[0, P:SEQ, :], y_sample[0])):
                sp.wait_ge(rows_ready, 7 + j)
                sp.dma_start(dst, rows[0:OUT_ROWS[j], j, :]).then_inc(out_done, 16)
            sp.wait_ge(out_done, 48)
            sp.wait_ge(kv_out, 96)
            sp.wait_ge(tail_out, 64)

        @block.gpsimd
        def _(pool):
            for name, key, spec in (("conv_w", "conv_w", "j (c p) -> (j c) p"), ("state_conv", "state_conv", "j (c p) -> (j c) p")):
                a, b = VEC[name]
                src = t[key][0] if name == "conv_w" else t[key][0, 0]
                pool.dma_start(vrow[a:b, :], src.rearrange(spec, p=P)).then_inc(vec_in, 16)
            for name, key in (("conv_b", "conv_b"), ("b_a", "b_rg_a"), ("b_x", "b_rg_x"), ("lam", "lru_lambda"),
                              ("b_gate", "b_gate")):
                a, b = VEC[name]
                pool.dma_start(vrow[a:b, :], t[key][0].rearrange("(c p) -> c p", p=P)).then_inc(vec_in, 16)
            a, b = VEC["state_h"]
            pool.dma_start(vrow[a:b, :], t["state_h"][0, 0].rearrange("(c p) -> c p", p=P)).then_inc(vec_in, 16)
            for h in range(2):
                src = t["attn_sinks"][0].rearrange("(c h) -> h c", h=2)[h:h + 1, :].to_broadcast([HD, 4])
                pool.dma_start(sink[HD * h:HD * h + HD, :], src, allow_slow_non_contiguous=True).then_inc(sink_in, 16)
            flat = "r h d -> r (h d)"
            pool.dma_start(kW, t["cache_win_k"][0, 0].rearrange(flat)).then_inc(cache_in, 16)
            pool.dma_start(vW, t["cache_win_v"][0, 0].rearrange(flat)).then_inc(cache_in, 16)
            pool.dma_start(kS[DEC:DEC + META, :], t["cache_meta_k"][0, 0].rearrange(flat)).then_inc(cache_in, 16)
            pool.dma_start(vS[DEC:DEC + META, :], t["cache_meta_v"][0, 0].rearrange(flat)).then_inc(cache_in, 16)
            low_of(pool, SPLIT[0], nc.gpsimd)
            nc.gpsimd.memset(merged[:, 0:4, :].rearrange("p k n -> p (k n)")[:, 0:D], 0.0).then_inc(zeroed, 1)
            pool.wait_ge(zeroed, 1)
            zeros = merged[0:REST, 0:4, :].rearrange("p k n -> p (k n)")[:, 0:D]
            for i in range(NE):
                pool.dma_start(y_dram[CAP * i + FIRST:CAP * (i + 1), :], zeros).then_inc(zero_out, 16)
            zeros = merged[0:CAP, 0:4, :].rearrange("p k n -> p (k n)")[:, 0:D]
            for i in range(NE, NITEM - 1):
                pool.dma_start(y_dram[CAP * i:CAP * (i + 1), :], zeros).then_inc(zero_out, 16)
            for j in range(3):
                for h in range(2):
                    S.emptied(pool, ("zT", j, h))
            for j in range(3):
                n = TILE_ROWS[j]
                nc.gpsimd.tensor_scalar(rows[0:n, j, :], rows[0:n, j, :], ALPHA, None, ALU.mult).then_inc(scaled, 1)
            M.emptied(pool, ("qkv", 2, 2))
            pool.dma_start(vM[0:META, :], qkv[DEC:DEC + META, 2, QKV - P:QKV]).then_inc(vm_in, 16)
            pool.wait_ge(roped, 1)
            nc.gpsimd.tensor_copy(kS[0:DEC, :], qkv[0:DEC, 2, NH * HD:NH * HD + P]).then_inc(side_keys, 1)
            nc.gpsimd.tensor_copy(vS[0:DEC, :], qkv[0:DEC, 2, QKV - P:QKV]).then_inc(side_keys, 1)
            pool.wait_ge(roped, 3)
            for ko, vo, j, lo, n in ((meta_k, meta_v, 2, DEC, META), (win_k, win_v, 1, 0, P), (new_k, new_v, 2, 0, DEC)):
                pool.dma_start(ko[0, 0].rearrange(flat), qkv[lo:lo + n, j, NH * HD:NH * HD + P]).then_inc(kv_out, 16)
                pool.dma_start(vo[0, 0].rearrange(flat), qkv[lo:lo + n, j, QKV - P:QKV]).then_inc(kv_out, 16)
            pool.dma_start(wr[:, :, 0:NG], t["w_group"][0].rearrange("(k p) g -> p k g", p=P),
                           allow_slow_non_contiguous=True).then_inc(router_in, 16)
            pool.dma_start(wr[:, :, NG:20], t["w_router"][0].rearrange("(k p) g e -> p k (g e)", p=P),
                           allow_slow_non_contiguous=True).then_inc(router_in, 16)
            pool.dma_start(br[:, 0:NG], t["b_group"]).then_inc(router_in, 16)
            pool.dma_start(br[:, NG:20], t["b_router"].rearrange("a g e -> a (g e)")).then_inc(router_in, 16)
            S.emptied(pool, "tail")
            pool.dma_start(conv_p[0, 0].rearrange("j (c p) -> (j c) p", p=P), stage_rows[0:24, :]).then_inc(tail_out, 16)
            pool.dma_start(conv_s[0, 0].rearrange("j (c p) -> (j c) p", p=P), stage_rows[24:48, :]).then_inc(tail_out, 16)
            pool.dma_start(h_p[0, 0].rearrange("(c p) -> c p", p=P), stage_rows[48:56, :]).then_inc(tail_out, 16)
            pool.dma_start(h_s[0, 0].rearrange("(c p) -> c p", p=P), stage_rows[56:64, :]).then_inc(tail_out, 16)
            def scale_residual():
                for j in range(3):
                    for h in range(2):
                        S.emptied(pool, ("z1T", j, h))
                for j in range(3):
                    n = OUT_ROWS[j]
                    nc.gpsimd.tensor_scalar(rows[0:n, j, :], rows[0:n, j, :], ALPHA, None, ALU.mult).then_inc(rows_scaled2, 1)

            def gather(i, s):
                nc.gpsimd.indirect_dma_start(
                    out=xg[s][0:CAP, :], out_offset=None, in_=z1_dram[:, :],
                    in_offset=bass.IndirectOffsetOnAxis(ap=index_i[0:CAP, i:i + 1], axis=0)).then_inc(xg_in[s], 16)

            pool.wait_ge(route_done, 1)
            pool.wait_ge(z1_out, 48)
            for i in range(NE):
                if i >= 3:
                    pool.wait_ge(xt_full, i - 2)
                gather(i, i % 3)
                if i == 2:
                    scale_residual()
            pool.wait_ge(ctrl_done, 1)
            count = pool.value_load(ctrl_i[0:1, W_COUNT:W_COUNT + 1], min_val=0, max_val=NOV)
            for v in range(NOV):
                with pool.If(count > v):
                    pool.wait_ge(xt_full, NE + v)
                    gather(NE + v, 1)
            pool.wait_ge(y_written, 1)
            for j in range(3):
                for k in range(2):
                    nc.gpsimd.indirect_dma_start(
                        out=yg[j][k][0:OUT_ROWS[j], :], out_offset=None, in_=y_dram[:, :],
                        in_offset=bass.IndirectOffsetOnAxis(ap=slot_i[0:OUT_ROWS[j], k, j:j + 1], axis=0))\
                        .then_inc(yg_in[j], 16)

        @block.tensor
        def _(pe):
            pe.wait_ge(const_in, 16)
            def transpose_rows(kind, j, n):
                for h in range(2):
                    b = S.claim(pe, (kind, j, h))
                    for k in range(4):
                        kk = 4 * h + k
                        mm = nc.tensor.transpose(b[:, k * P:k * P + n], rows[0:n, j, kk * P:kk * P + P], ident[0:n, 0:n])
                    mm.then_inc(S.f_full((kind, j, h)), 1)

            def parts(u):
                return [w.rearrange("p (k n) -> p k n", n=256) for w in (high[split_order(u) % 2], low[u % RING])]

            for j in range(3):
                n = TILE_ROWS[j]
                pe.wait_ge(rows_ready, j + 1)
                transpose_rows("zT", j, n)
            for u in range(3):
                pe.wait_ge(low_made, split_order(u) + 1)
                for j in range(3):
                    n = TILE_ROWS[j]
                    at = META + P * j
                    if u == 0:
                        for h in range(2):
                            S.emptied(pe, ("zT", j, h))
                    b = M.claim(pe, ("qkv", j, u))
                    wh, wl = parts(u)
                    for k in range(KD):
                        z = slice(at, at + n)
                        nc.tensor.matmul(b[0:n, 0:256], zh[:, k, z], wh[:, k, :], start=(k == 0), stop=False)
                        nc.tensor.matmul(b[0:n, 0:256], zh[:, k, z], wl[:, k, :], start=False, stop=False)
                        mm = nc.tensor.matmul(b[0:n, 0:256], zl[k // 4][:, k % 4, z], wh[:, k, :], start=False, stop=(k == KD - 1))
                    mm.then_inc(M.f_full(("qkv", j, u)), 1)

            pe.wait_ge(vec_in, 128)
            b = S.claim(pe, "vec")
            nc.tensor.transpose(b[:, 0:NVEC], vrow[0:NVEC, :], ident[0:NVEC, 0:NVEC]).then_inc(S.f_full("vec"), 1)

            def chan_split(u, c, name, lo):
                pe.wait_ge(low_made, split_order(u) + 1)
                wh, wl = parts(u)
                b = M.claim(pe, name)
                o = slice((c % 2) * P, (c % 2) * P + P)
                for k in range(KD):
                    nc.tensor.matmul(b[:, 0:NALL - lo], wh[:, k, o], zh[:, k, lo:NALL], start=(k == 0), stop=False)
                    nc.tensor.matmul(b[:, 0:NALL - lo], wh[:, k, o], zl[k // 4][:, k % 4, lo:NALL], start=False, stop=False)
                    mm = nc.tensor.matmul(b[:, 0:NALL - lo], wl[:, k, o], zh[:, k, lo:NALL], start=False, stop=(k == KD - 1))
                mm.then_inc(M.f_full(name), 1)

            def chan(u, c, name, rhs, kk):
                unit_loaded(pe, u)
                w = ring[u % RING].rearrange("p (k n) -> p k n", n=256)
                b = M.claim(pe, name)
                o = (c % 2) * P
                n = rhs(0).shape[-1]
                for k in range(kk):
                    mm = nc.tensor.matmul(b[:, 0:n], w[:, k, o:o + P], rhs(k), start=(k == 0), stop=(k == kk - 1))
                mm.then_inc(M.f_full(name), 1)

            for c in range(KD):
                chan_split(U_XR + c // 2, c, ("xr", c), 0)

            pe.wait_ge(roped, 3)
            for j in range(3):
                n = OUT_ROWS[j]
                b = M.claim(pe, ("QT", j))
                for c in range(4):
                    mm = nc.tensor.transpose(b[:, c * P:c * P + n], qkv[0:n, j, c * P:c * P + P], ident[0:n, 0:n])
                mm.then_inc(M.f_full(("QT", j)), 1)
            b = M.claim(pe, "KT")
            for j in range(3):
                n = TILE_ROWS[j]
                mm = nc.tensor.transpose(b[:, P * j:P * j + n], qkv[0:n, j, NH * HD:NH * HD + P], ident[0:n, 0:n])
            mm.then_inc(M.f_full("KT"), 1)
            pe.wait_ge(side_keys, 2)
            pe.wait_ge(cache_in, 64)
            b = M.claim(pe, "KS")
            nc.tensor.transpose(b[:, 0:P], kW, ident)
            nc.tensor.transpose(b[:, P:P + DEC + META], kS[0:DEC + META, :], ident[0:DEC + META, 0:DEC + META])\
                .then_inc(M.f_full("KS"), 1)

            unit_loaded(pe, U_RG)
            wrg = ring[U_RG % RING].rearrange("p (w n e) -> p w n e", w=2, e=P)
            for c in range(KD):
                pe.wait_ge(conv_made, c + 1)
                for w, kind in enumerate("ri"):
                    b = M.claim(pe, (kind, c))
                    nc.tensor.matmul(b[:, 0:TW], wrg[:, w, c, :], xc[:, c, :], start=True, stop=True)\
                        .then_inc(M.f_full((kind, c)), 1)

            def scores(c):
                for g in range(4):
                    kv, half = divmod(g, 2)
                    hp = slice(HD * kv, HD * kv + HD)
                    b = S.claim(pe, ("S", c, g))
                    q = qT[hp, c, P * half:P * half + P]
                    if c < 4:
                        lo, hi, _ = chunk_keys(c)
                        nc.tensor.matmul(b[:, 0:hi - lo], q, kT[hp, lo:hi], start=True, stop=True)
                        mm = nc.tensor.matmul(b[:, hi - lo:hi - lo + META], q, kT[hp, NTOK:NALL], start=True, stop=True)
                    else:
                        mm = nc.tensor.matmul(b[:, 0:WIN + DEC + META], q, kTs[hp, :], start=True, stop=True)
                    mm.then_inc(S.f_full(("S", c, g)), 1)

            def turn_probs(c):
                blocks = chunk_blocks(c)
                pe.wait_ge(prob_ready, c + 1)
                for i, (at, n) in enumerate(blocks):
                    b = M.claim(pe, ("PT", c, i))
                    for g in range(4):
                        mm = nc.tensor.transpose(b[0:n, g * P:g * P + P], prob[c % 2][:, g, at:at + n], ident)
                    mm.then_inc(M.f_full(("PT", c, i)), 1)

            def attend(c):
                blocks = chunk_blocks(c)
                b = M.claim(pe, ("PV", c))
                for i in range(len(blocks)):
                    M.emptied(pe, ("PT", c, i))
                if c == 0:
                    pe.wait_ge(vm_in, 16)
                for kv in range(NKV):
                    for half in range(2):
                        g = 2 * kv + half
                        for i, (at, n) in enumerate(blocks):
                            if c == 4:
                                v = (vW if i == 0 else vS)[0:n, HD * kv:HD * kv + HD]
                            elif i == len(blocks) - 1:
                                v = vM[0:n, HD * kv:HD * kv + HD]
                            else:
                                v = qkv[0:n, i, QKV - P + HD * kv:QKV - P + HD * kv + HD]
                            mm = nc.tensor.matmul(b[HD * kv:HD * kv + HD, half * P:half * P + P], v,
                                                  pT[0:n, i, g * P:g * P + P],
                                                  start=(i == 0), stop=(i == len(blocks) - 1))
                mm.then_inc(M.f_full(("PV", c)), 1)

            for name in (("QT", 0), ("QT", 1), ("QT", 2), "KT", "KS"):
                M.emptied(pe, name)
            gr = iter(range(KD))
            for c in range(CHUNKS + 1):
                if c < CHUNKS:
                    scores(c)
                if 1 <= c < CHUNKS:
                    turn_probs(c - 1)
                for _ in range(GR_AFTER[c]):
                    cc = next(gr)
                    chan_split(U_GR + cc // 2, cc, ("gr", cc), META)
                if c == CHUNKS:
                    turn_probs(c - 1)
                    chan_split(U_MERGE, 0, ("ga", 0), META)
                if c >= 1:
                    attend(c - 1)

            for p in range(0, KD, 2):
                u = U_MERGE + 2 * p
                for m in (p, p + 1):
                    if m > 0:
                        chan_split(u, m, ("ga", m), META)
                for m in (p, p + 1):
                    chan_split(u + 1, m, ("gr_gate", m), META)
                if p == 0:
                    M.emptied(pe, ("PV", CHUNKS - 1))
                for m in (p, p + 1):
                    chan(u + 2, m, ("pa", m), lambda k: attnT[:, k, :], 4)
                if p == 0:
                    pe.wait_ge(rnn_made, 2)
                for m in (p, p + 1):
                    chan(u + 3, m, ("pr", m), lambda k: rnnT[:, k, :], KD)

            pe.wait_ge(tail_staged, 1)
            b = S.claim(pe, "tail")
            nc.tensor.transpose(b[0:64, 0:P], stage, ident).then_inc(S.f_full("tail"), 1)

            pe.wait_ge(merge_made, KD)
            def logits(j):
                n = OUT_ROWS[j]
                b = S.bank("logits")
                for h in range(2):
                    S.emptied(pe, ("z1T", j, h))
                for k in range(KD):
                    nc.tensor.matmul(b[0:n, 20 * j:20 * j + 20], z1T[:, k, P * j:P * j + n], wr[:, k, :],
                                     start=(k == 0), stop=False)
                return nc.tensor.matmul(b[0:n, 20 * j:20 * j + 20], ones[0:1, 0:n], br[:, :], start=False, stop=True)

            for kind, j in OUT_ORDER:
                n = OUT_ROWS[j]
                if (kind, j) == ("z1T", 2):
                    pe.wait_ge(router_in, 64)
                    S.claim(pe, "logits")
                    logits(0)
                    logits(1)
                if kind == "z1T":
                    pe.wait_ge(rows_ready, 3 + j + 1)
                    transpose_rows("z1T", j, n)
                    continue
                for h in range(2):
                    b = S.claim(pe, ("out", j, h))
                    for q in range(2):
                        u = U_OUT + 2 * h + q
                        unit_loaded(pe, u)
                        w = ring[at_ring(u)].rearrange("p (k n) -> p k n", n=256)
                        for k in range(KD):
                            mm = nc.tensor.matmul(b[0:n, 256 * q:256 * q + 256], merged[:, k, P * j:P * j + n], w[:, k, :],
                                                  start=(k == 0), stop=(k == KD - 1))
                    mm.then_inc(S.f_full(("out", j, h)), 1)
            logits(2).then_inc(S.f_full("logits"), 1)
            pe.wait_ge(chosen, 1)
            b = S.claim(pe, "ranks")
            for j in range(3):
                for i in range(j):
                    nc.tensor.matmul(b[:, NE * j:NE * j + NE], ones, e_sum[:, i, :], start=(i == 0), stop=False)
                nc.tensor.matmul(b[:, NE * j:NE * j + NE], before, e_sum[:, j, :], start=(j == 0), stop=True)
            for i in range(3):
                mm = nc.tensor.matmul(b[:, NE * 3:NE * 4], ones, e_sum[:, i, :], start=(i == 0), stop=(i == 2))
            mm.then_inc(S.f_full("ranks"), 1)
            pe.wait_ge(selected, 1)
            b = S.claim(pe, "index")
            for k in range(2):
                for j in range(3):
                    mm = nc.tensor.matmul(b[0:CAP, 0:NITEM], rank_hot[:, k, CAP * j:CAP * j + CAP], item_hot[:, k, NITEM * j:NITEM * j + NITEM],
                                          start=(k == 0 and j == 0), stop=(k == 1 and j == 2))
            mm.then_inc(S.f_full("index"), 1)
            pe.wait_ge(route_done, 1)

            def turn(i, s, n):
                pe.wait_ge(xg_in[s], 16 * (n + 1))
                wait_past(pe, xt_made, i)
                for h in range(2):
                    for k in range(4):
                        mm = nc.tensor.transpose(TB[h][:, k * CAP:k * CAP + CAP], xg[s][0:CAP, P * (4 * h + k):P * (4 * h + k) + P],
                                                 ident[0:CAP, 0:CAP])
                mm.then_inc(xt_full, 1)

            def tiles(bank, cols, lhsT, rhs, kk, m):
                for k in range(kk):
                    for j in range(P // m):
                        mm = nc.tensor.matmul(bank[m * j:m * j + m, cols], lhsT(k), rhs(k, j), start=(k == 0), stop=(k == kk - 1))
                return mm

            def hidden(i, s, n):
                pe.wait_ge(xt_made, i + 1)
                pe.wait_ge(g_in[s], 16 * (n + 1))
                tiles(HB[s], slice(0, 256), lambda k: xT[s][:, k, 0:FIRST],
                      lambda k, j: w_gate[s][:, k, 256 * j:256 * j + 256], KD, FIRST)
                pe.wait_ge(u_in[s], 16 * (n + 1))
                tiles(HB[s], slice(256, 512), lambda k: xT[s][:, k, 0:FIRST],
                      lambda k, j: w_up[s][:, k, 256 * j:256 * j + 256], KD, FIRST).then_inc(ha_full, 1)

            def down(i, s, n):
                pe.wait_ge(d_in[s], 16 * (n + 1))
                pe.wait_ge(hta_made, i + 1)
                wait_past(pe, ya_made, i)
                tiles(YB, slice(0, 512), lambda k: hT_a[:, P * (k % 2) + FIRST * (k // 2):P * (k % 2) + FIRST * (k // 2) + FIRST],
                      lambda k, j: w_down[s][:, k, 512 * j:512 * j + 512], KF, FIRST).then_inc(ya_full, 1)

            def turn_hidden(i):
                pe.wait_ge(ha_made, i + 1)
                for h in range(2):
                    mm = nc.tensor.transpose(TH[:, P * h:P * h + P], hid_a[:, P * h:P * h + P], ident)
                mm.then_inc(hta_full, 1)

            def rest(s, n, b):
                pe.wait_ge(yb_made, b + 1)
                tiles(BB, slice(0, P), lambda k: xT[s][:, k, FIRST:CAP], lambda k, j: w_gate[s][:, k, P * j:P * j + P], KD, REST)
                tiles(BB, slice(P, 2 * P), lambda k: xT[s][:, k, FIRST:CAP], lambda k, j: w_up[s][:, k, P * j:P * j + P], KD, REST)\
                    .then_inc(hb_full, 1)
                pe.wait_ge(hb_made, b + 1)
                nc.tensor.transpose(BB[:, 2 * P:3 * P], hid_b, ident).then_inc(htb_full, 1)
                pe.wait_ge(d_in[s], 16 * (n + 1))
                pe.wait_ge(htb_made, b + 1)
                tiles(BB, slice(0, 256), lambda k: hT_b[:, REST * k:REST * k + REST],
                      lambda k, j: w_down[s][:, k, 256 * j:256 * j + 256], KF, REST).then_inc(yb_full, 1)

            def maybe_rest(i, s, n):
                has, b = rest_words(pe, i)
                with pe.If(has > 0):
                    rest(s, n, b)

            pe.wait_ge(ctrl_done, 1)

            def round_of(n, first):
                for s in range(3):
                    i = 3 * n + s
                    hidden(i, s, n)
                    if not (first and s == 0):
                        down(i - 1, (s - 1) % 3, n if s else n - 1)
                    turn(i + 1, (s + 1) % 3, n + (s + 1) // 3)
                    maybe_rest(i, s, n)
                    turn_hidden(i)

            turn(0, 0, 0)
            round_of(0, True)
            with pe.Fori(1, NE // 3) as n:
                round_of(n, False)
            down(NE - 2, 2, NE // 3 - 1)
            hidden(NE - 1, 0, NE // 3)
            maybe_rest(NE - 1, 0, NE // 3)
            turn_hidden(NE - 1)
            down(NE - 1, 0, NE // 3)
            count, total = overflow_words(pe)
            with pe.If(count > 0):
                with pe.Fori(0, count) as v:
                    turn(v + NE, 1, v + NE // 3)
                    hidden(v + NE, 1, v + NE // 3)
                    rest(1, v + NE // 3, total + v)
                    turn_hidden(v + NE)
                    down(v + NE, 1, v + NE // 3)

        @block.scalar
        def _(act):
            step = Steps(act, act_step)
            run = nc.scalar.activation

            def norm_rows_load(g, b):
                for i, name in enumerate((g, b)):
                    row = t[name] if len(t[name].shape) == 2 else t[name].rearrange("(o d) -> o d", o=1)
                    act.dma_start(gb[:, i, :], row.to_broadcast([P, D])).then_inc(norm_in, 16)

            def deviation(i, j, n):
                act.wait_ge(var_ready, 3 * i + j + 1)
                run(rstd[0:n, j:j + 1], mv[0:n, j, 1:2], ACT.Sqrt, bias=eps[0:n, :], scale=1.0).then_inc(std_ready, 1)

            norm_rows_load("ln_in_g", "ln_in_b")
            act.wait_ge(const_in, 16)
            def token_high(j):
                n = TILE_ROWS[j]
                at = META + P * j
                for h in range(2):
                    b = S.arrived(act, ("zT", j, h)).rearrange("p (k n) -> p k n", n=P)
                    if j == 2:
                        nc.scalar.copy(zh[:, 4 * h:4 * h + 4, 0:META], b[:, :, DEC:DEC + META])
                    nc.scalar.copy(zh[:, 4 * h:4 * h + 4, at:at + n], b[:, :, 0:n]).then_inc(zh_made, 1)

            for j in range(3):
                deviation(0, j, TILE_ROWS[j])
                if j == 1:
                    high_of(act, SPLIT[0])
            token_high(0)
            token_high(1)
            high_of(act, SPLIT[1])
            token_high(2)
            for u in range(3):
                if u > 0:
                    high_of(act, SPLIT[u + 1])
                for j in range(3):
                    n = TILE_ROWS[j]
                    b = M.arrived(act, ("qkv", j, u))
                    if u < NKV:
                        dst = qkv[0:n, j, 0:NH * HD].rearrange("p (c g d) -> p g c d", g=NKV, d=HD)[:, u]
                        src = b[0:n, 0:256].rearrange("p (c d) -> p c d", d=HD)
                    else:
                        dst, src = qkv[0:n, j, NH * HD:QKV], b[0:n, 0:256]
                    nc.scalar.copy(dst, src).then_inc(M.f_free(("qkv", j, u)), 1)
            act.wait_ge(zeroed, 1)
            act.dma_start(y_dram[CAP * (NITEM - 1):CAP * NITEM, :], merged[0:CAP, 0:4, :].rearrange("p k n -> p (k n)")[:, 0:D])\
                .then_inc(yb_out, 16)
            act.wait_ge(lam_ready, 1)
            run(sp_t[1], sp_t[0], ACT.Exp, scale=-1.0).then_inc(lam_exp, 1)
            for c in range(KD):
                if c % 2 == 0 and c < 6:
                    high_of(act, SPLIT[c // 2 + 4])
                b = M.arrived(act, ("xr", c))
                nc.scalar.copy(xpad[:, c, GAP:GAP + TP], b[:, 0:TP])
                nc.scalar.copy(xpad[:, c, TP + 2 * GAP:XPAD], b[:, TP:NALL]).then_inc(M.f_free(("xr", c)), 1)
            high_of(act, SPLIT[7])
            for j in range(3):
                n = OUT_ROWS[j]
                b = M.arrived(act, ("QT", j)).rearrange("p (c x q) -> p x c q", c=4, q=CHUNK)
                for x in range(n // CHUNK):
                    cp = nc.scalar.copy(qT[:, 2 * j + x, :].rearrange("p (c q) -> p c q", q=CHUNK), b[:, x])
                cp.then_inc(M.f_free(("QT", j)), 1)
            b = M.arrived(act, "KT")
            nc.scalar.copy(kT, b[:, 0:NALL]).then_inc(M.f_free("KT"), 1)
            b = M.arrived(act, "KS")
            nc.scalar.copy(kTs, b[:, 0:WIN + DEC + META]).then_inc(M.f_free("KS"), 1)
            high_of(act, SPLIT[8])
            act.wait_ge(cols_ready, 1)
            for c in range(KD):
                b = M.arrived(act, ("r", c))
                step(run(th_r[:, c % 2, :], b[:, 0:TW], ACT.Tanh, bias=hba[:, c:c + 1], scale=0.5))
                act.wait_ge(act_step, step.n)
                run(dec[:, c, :], th_r[:, c % 2, :], ACT.Exp, bias=nsp4[:, c:c + 1], scale=nsp4[:, c:c + 1])\
                    .then_inc(M.f_free(("r", c)), 1)
                run(inp[:, c, :], th_r[:, c % 2, :], ACT.Tanh, bias=sp4[:, c:c + 1], scale=sp4[:, c:c + 1])
                b = M.arrived(act, ("i", c))
                run(gate_i[:, c, :], b[:, 0:TW], ACT.Tanh, bias=hbx[:, c:c + 1], scale=0.5)\
                    .then_inc(M.f_free(("i", c)), 1)

            def exps(c):
                act.wait_ge(max_ready, c + 1)
                n = sum(k for _, k in chunk_blocks(c))
                off = chunk_keys(c)[2] if c < 4 else 0
                for g in range(4):
                    b = S.arrived(act, ("S", c, g))
                    run(prob[c % 2][:, g, off:n], b[:, 0:n - off], ACT.Exp, bias=nm[:, c % 2, g:g + 1], scale=HD ** -0.5,
                        accum_out=rs[:, c % 2, g:g + 1]).then_inc(S.f_free(("S", c, g)), 1)
                run(es[:, c % 2, :], m_c[:, c % 2, :], ACT.Exp).then_inc(exp_made, 1)

            def gelu_inner(h):
                act.wait_ge(gelu_cube, h + 1)
                run(gel, gel, ACT.Tanh, scale=(2.0 / np.pi) ** 0.5).then_inc(gelu_tanh, 1)

            def gelu_input(cc):
                b = M.arrived(act, ("gr", cc))
                nc.scalar.copy(rnnT[:, cc, :], b[:, 0:NTOK]).then_inc(M.f_free(("gr", cc)), 1)
                if cc % 4 == 3:
                    M.emptied(act, ("gr", cc))
                    if cc > 3:
                        act.wait_ge(gelu_done, 1)
                    run(gel, rnnT[:, cc - 3:cc + 1, :], ACT.Square, scale=0.044715 ** 0.5).then_inc(gelu_sq, 1)

            gr = iter(range(KD))
            for c in range(CHUNKS + 1):
                if c == CHUNKS:
                    gelu_input(KD - 1)
                if c >= 1:
                    for i, (_, n) in enumerate(chunk_blocks(c - 1)):
                        b = M.arrived(act, ("PT", c - 1, i))
                        if i == 0 and c >= 2:
                            M.arrived(act, ("PV", c - 2))
                        nc.scalar.copy(pT[0:n, i, :], b[0:n, :]).then_inc(M.f_free(("PT", c - 1, i)), 1)
                if c < CHUNKS:
                    exps(c)
                if c == 0:
                    act.wait_ge(gate_prod, 4)
                    run(inp[:, :, :], inp[:, :, :], ACT.Sqrt, scale=0.25).then_inc(sqrt_made, 1)
                if c < CHUNKS:
                    for _ in range(GR_AFTER[c]):
                        gelu_input(next(gr))
                for n, at in SPLIT_AT:
                    if c == at:
                        high_of(act, SPLIT[n])
                if c == HALF_GR + 1:
                    gelu_inner(0)
            high_of(act, SPLIT[12])
            gelu_inner(1)

            act.wait_ge(rows_ready, 3)
            for p in range(0, KD, 2):
                for w, name in enumerate(("ga", "gr_gate")):
                    for m in (p, p + 1):
                        if m >= 2:
                            act.wait_ge(merge_made, m - 1)
                        b = M.arrived(act, (name, m))
                        run(mtmp[m % 2][w], b[:, 0:NTOK], ACT.Tanh, bias=hbg[:, KD * w + m:KD * w + m + 1], scale=0.5)\
                            .then_inc(M.f_free((name, m)), 1)
                if p < KD - 2:
                    high_of(act, SPLIT[13 + p])
                    high_of(act, SPLIT[14 + p])
            act.wait_ge(merge_made, KD)
            norm_rows_load("ln1_g", "ln1_b")

            def turned(j):
                act.wait_ge(rows_ready, 3 + j + 1)
                n = OUT_ROWS[j]
                act.dma_start(z1_dram[P * j:P * j + n, :], rows[0:n, j, :]).then_inc(z1_out, 16)
                for h in range(2):
                    b = S.arrived(act, ("z1T", j, h)).rearrange("p (k n) -> p k n", n=P)
                    nc.scalar.copy(z1T[:, 4 * h:4 * h + 4, P * j:P * j + n], b[:, :, 0:n])\
                        .then_inc(S.f_free(("z1T", j, h)), 1)

            deviation(1, 0, P)
            deviation(1, 1, P)
            turned(0)
            deviation(1, 2, DEC)
            turned(1)
            turned(2)
            norm_rows_load("ln2_g", "ln2_b")
            act.wait_ge(lg_exp_in, 1)
            run(exo, exi, ACT.Exp).then_inc(lg_exp, 1)

            def gate_tanh(i, s):
                act.wait_ge(ha_full, i + 1)
                run(th_a, HB[s][:, 0:256], ACT.Tanh, scale=0.5).then_inc(ha_tanh, 1)

            def rows_out(i, s, n):
                act.wait_ge(ya_full, i + 1)
                wait_past(act, y_out[s], 32 * n)
                nc.scalar.copy(yo[s], YB[:, :]).then_inc(ya_made, 1)
                act.wait_ge(ya_made, i + 1)
                for h in range(2):
                    cols = slice(512 * h, 512 * h + 512)
                    dst = y_dram[i * CAP:i * CAP + FIRST, cols] if isinstance(i, int) else \
                        y_dram[bass.ds(i * CAP, FIRST), cols]
                    act.dma_start(dst, yo[s][FIRST * h:FIRST * h + FIRST, :]).then_inc(y_out[s], 16)

            def rest(i, b):
                act.wait_ge(hb_full, b + 1)
                run(th_b, BB[:, 0:P], ACT.Tanh, scale=0.5).then_inc(hb_tanh, 1)
                act.wait_ge(yb_full, b + 1)
                act.wait_ge(yb_out, 16 + 64 * b)
                nc.scalar.copy(yo_b, BB[:, 0:256]).then_inc(yb_made, 1)
                act.wait_ge(yb_made, b + 2)
                for j in range(4):
                    cols = slice(256 * j, 256 * j + 256)
                    dst = y_dram[i * CAP + FIRST:(i + 1) * CAP, cols] if isinstance(i, int) else \
                        y_dram[bass.ds(i * CAP + FIRST, REST), cols]
                    act.dma_start(dst, yo_b[REST * j:REST * j + REST, :]).then_inc(yb_out, 16)

            def maybe_rest(i):
                has, b = rest_words(act, i)
                with act.If(has > 0):
                    rest(i, b)

            act.wait_ge(route_done, 1)
            nc.scalar.copy(yo_b[:, 0:1], ident[:, 0:1]).then_inc(yb_made, 1)

            def round_of(n, first):
                for s in range(3):
                    i = 3 * n + s
                    gate_tanh(i, s)
                    if not (first and s == 0):
                        rows_out(i - 1, (s - 1) % 3, n if s else n - 1)
                    maybe_rest(i)

            round_of(0, True)
            with act.Fori(1, NE // 3) as n:
                round_of(n, False)
            rows_out(NE - 2, 2, NE // 3 - 1)
            gate_tanh(NE - 1, 0)
            maybe_rest(NE - 1)
            rows_out(NE - 1, 0, NE // 3)
            count, total = overflow_words(act)
            with act.If(count > 0):
                with act.Fori(0, count) as v:
                    gate_tanh(v + NE, 1)
                    rest(v + NE, total + v)
                    rows_out(v + NE, 1, v + NE // 3)
            act.wait_ge(y_out[0], 32 * (NE // 3 + 1))
            act.wait_ge(y_out[2], 32 * (NE // 3))
            act.wait_ge(y_out[1], 32 * (count + NE // 3))
            act.wait_ge(yb_out, 16 + 64 * (count + total))
            act.wait_ge(zero_out, 16 * (NITEM - 1))
            nc.scalar.copy(th_a[:, 0:1], ident[:, 0:1]).then_inc(y_written, 1)
            for j in range(3):
                deviation(2, j, OUT_ROWS[j])

        @block.vector
        def _(dve):
            step = Steps(dve, dve_step)
            V = nc.vector
            tt, stt, ts = V.tensor_tensor, V.scalar_tensor_tensor, V.tensor_scalar

            def alone(inst):
                step(inst)
                step.settle()

            def moments(j, n):
                for h in range(2):
                    step(V.bn_stats(stats[0:n, j, 6 * h:6 * h + 6], rows[0:n, j, 512 * h:512 * h + 512]))
                step.settle()
                V.bn_aggr(mv[0:n, j, :], stats[0:n, j, :]).then_inc(var_ready, 1)

            def normed(i, j, n):
                if j == 0:
                    dve.wait_ge(norm_in, 32 * (i + 1))
                dve.wait_ge(var_ready, 3 * i + j + 1)
                step(stt(rows[0:n, j, :], rows[0:n, j, :], mv[0:n, j, 0:1], gb[0:n, 0, :], ALU.subtract, ALU.mult))
                dve.wait_ge(std_ready, 3 * i + j + 1)
                alone(V.reciprocal(rstd[0:n, j:j + 1], rstd[0:n, j:j + 1]))
                stt(rows[0:n, j, :], rows[0:n, j, :], rstd[0:n, j:j + 1], gb[0:n, 1, :], ALU.mult, ALU.add)\
                    .then_inc(rows_ready, 1)

            def token_low(j):
                n = TILE_ROWS[j]
                at = META + P * j
                for h in range(2):
                    dve.wait_ge(zh_made, 2 * j + h + 1)
                    four = slice(4 * h, 4 * h + 4)
                    b = S.arrived(dve, ("zT", j, h)).rearrange("p (k n) -> p k n", n=P)
                    if j == 2:
                        tt(zl[h][:, :, 0:META], b[:, :, DEC:DEC + META], zh[:, four, 0:META], ALU.subtract)
                    tt(zl[h][:, :, at:at + n], b[:, :, 0:n], zh[:, four, at:at + n], ALU.subtract)\
                        .then_inc(S.f_free(("zT", j, h)), 1)

            for j in range(3):
                dve.wait_ge(x_in[j], 16 if j < 2 else 32)
                moments(j, TILE_ROWS[j])
                if j == 2:
                    token_low(0)
                normed(0, j, TILE_ROWS[j])
            token_low(1)
            token_low(2)
            dve.wait_ge(low_made, 1)
            low_of(dve, SPLIT[1])
            low_of(dve, SPLIT[2])
            low_of(dve, SPLIT[3])

            b = S.arrived(dve, "vec")
            V.tensor_copy(vcol, b[:, 0:NVEC]).then_inc(S.f_free("vec"), 1)
            S.emptied(dve, "vec")
            alone(ts(sp_t[1], vc("lam", 0, KD), -1.0, None, ALU.mult))
            tt(sp_t[0], sp_t[1], vc("lam", 0, KD), ALU.max).then_inc(lam_ready, 1)
            step(ts(hba, vc("b_a", 0, KD), 0.5, None, ALU.mult))
            step(ts(hbx, vc("b_x", 0, KD), 0.5, None, ALU.mult))
            step(ts(hbg, vc("b_gate", 0, 2 * KD), 0.5, None, ALU.mult))
            step(V.memset(xpad[:, :, 0:GAP], 0.0))
            states = vc("state_conv", 0, GAP * KD).rearrange("p (j c) -> p c j", c=KD)
            step(V.tensor_copy(xpad[:, :, TP + GAP:TP + 2 * GAP], states))
            low_of(dve, SPLIT[4])
            rot = [rot_t[:, i, :].rearrange("p (h d) -> p h d", d=HALF) for i in range(4)]
            for i, j in enumerate((2, 0, 1)):
                n = TILE_ROWS[j]
                for u in range(3):
                    M.emptied(dve, ("qkv", j, u))
                heads = qkv[0:n, j, 0:(NH + NKV) * HD].rearrange("p (h d) -> p h d", d=HD)
                x1, x2 = heads[:, :, 0:HALF], heads[:, :, HALF:ROT]
                cos = cst("cos")[0:n, HALF * j:HALF * j + HALF].unsqueeze(1).to_broadcast([n, NH + NKV, HALF])
                sin = cst("sin")[0:n, HALF * j:HALF * j + HALF].unsqueeze(1).to_broadcast([n, NH + NKV, HALF])
                for out, a, b in ((0, x1, cos), (1, x2, sin), (2, x2, cos), (3, x1, sin)):
                    step(tt(rot[out][0:n], a, b, ALU.mult))
                step.settle()
                step(tt(x1, rot[0][0:n], rot[1][0:n], ALU.subtract))
                step.settle()
                tt(x2, rot[2][0:n], rot[3][0:n], ALU.add).then_inc(roped, 1)
                dve.wait_ge(roped, i + 1)

            low_of(dve, SPLIT[5])
            dve.wait_ge(lam_exp, 1)
            alone(ts(sp_t[2], sp_t[1], 2.0, None, ALU.add))
            alone(V.reciprocal(sp_t[2], sp_t[2]))
            alone(tt(sp_t[2], sp_t[2], sp_t[1], ALU.mult))
            alone(tt(sp_t[3], sp_t[2], sp_t[2], ALU.mult))
            alone(ts(sp_t[4], sp_t[3], 1.0 / 17, None, ALU.mult))
            for k in (15, 13, 11, 9, 7, 5, 3):
                alone(stt(sp_t[4], sp_t[4], 1.0 / k, sp_t[3], ALU.add, ALU.mult))
            alone(stt(sp_t[4], sp_t[4], 1.0, sp_t[2], ALU.add, ALU.mult))
            alone(ts(sp_t[5], vc("lam", 0, KD), -1.0, 0.0, ALU.mult, ALU.max))
            alone(stt(sp_t[5], sp_t[4], 2.0, sp_t[5], ALU.mult, ALU.add))
            alone(ts(sp4, sp_t[5], 0.5 * LRU_C, None, ALU.mult))
            ts(nsp4, sp_t[5], -0.5 * LRU_C, None, ALU.mult).then_inc(cols_ready, 1)

            for c in range(0, KD, 2):
                if c == 2:
                    low_of(dve, SPLIT[6])
                for q in (c, c + 1):
                    M.emptied(dve, ("xr", q))
                    step(ts(xc[:, q, :], xpad[:, q, 0:TW], vc("conv_w", q), vc("conv_b", q), ALU.mult, ALU.add))
                for j in range(1, CONVW):
                    for q in (c, c + 1):
                        dve.wait_ge(dve_step, step.n if j == CONVW - 1 and q > c else step.n - 1)
                        inst = stt(xc[:, q, :], xpad[:, q, j:j + TW], vc("conv_w", KD * j + q), xc[:, q, :], ALU.mult, ALU.add)
                        if j < CONVW - 1:
                            step(inst)
                        else:
                            inst.then_inc(conv_made, 1)

            low_of(dve, SPLIT[7])
            low_of(dve, SPLIT[8])
            for c in range(0, KD, 2):
                for q in (c, c + 1):
                    M.emptied(dve, ("i", q))
                two = slice(c, c + 2)
                alone(tt(asq[:, :, :], dec[:, two, :], dec[:, two, :], ALU.mult))
                step(stt(gate_i[:, two, :], gate_i[:, two, :], 1.0, xc[:, two, :], ALU.add, ALU.mult))
                stt(inp[:, two, :], asq[:, :, :], 1.0, inp[:, two, :], ALU.add, ALU.mult).then_inc(gate_prod, 1)
                dve.wait_ge(gate_prod, c // 2 + 1)

            def softmax_max(c):
                if c == 3:
                    M.arrived(dve, ("PT", 1, 0))
                    step(V.memset(prob[1][:, :, 0:chunk_keys(3)[2]], 0.0))
                n = sum(k for _, k in chunk_blocks(c)) - (chunk_keys(c)[2] if c < 4 else 0)
                k = c % 2
                for g in range(4):
                    b = S.arrived(dve, ("S", c, g))
                    step(V.tensor_reduce(mx[:, k, g:g + 1], b[:, 0:n], AX_X, ALU.max))
                step.settle()
                alone(stt(m_c[:, k, :], mx[:, k, :], HD ** -0.5, sink, ALU.mult, ALU.max))
                alone(ts(nm[:, k, :], m_c[:, k, :], -1.0, None, ALU.mult))
                tt(m_c[:, k, :], sink, m_c[:, k, :], ALU.subtract).then_inc(max_ready, 1)

            def softmax_norm(c):
                k = c % 2
                dve.wait_ge(exp_made, c + 1)
                for g in range(4):
                    S.emptied(dve, ("S", c, g))
                alone(tt(dn[:, k, :], rs[:, k, :], es[:, k, :], ALU.add))
                alone(V.reciprocal(rd[:, k, :], dn[:, k, :]))
                n = sum(w for _, w in chunk_blocks(c))
                for g in range(4):
                    inst = ts(prob[k][:, g, 0:n], prob[k][:, g, 0:n], rd[:, k, g:g + 1], None, ALU.mult)
                inst.then_inc(prob_ready, 1)

            def recurrence(c):
                if c == 0:
                    dve.wait_ge(sqrt_made, 1)
                two = slice(c, c + 2)
                last = TP + GAP - 1
                step(tt(inp[:, two, :], inp[:, two, :], gate_i[:, two, :], ALU.mult))
                step(V.memset(dec[:, two, last:last + 1], 0.0))
                step.settle()
                alone(V.tensor_copy(inp[:, two, last:last + 1], vc("state_h", c, 2).unsqueeze(2)))
                for q in (c, c + 1):
                    step(V.tensor_tensor_scan(gate_i[:, q, :], dec[:, q, :], inp[:, q, :], 0.0, ALU.mult, ALU.add))

            def gelu_cubes(h):
                dve.wait_ge(gelu_sq, h + 1)
                M.emptied(dve, ("gr", 4 * h + 3))
                stt(gel, gel, 1.0, rnnT[:, 4 * h:4 * h + 4, :], ALU.add, ALU.mult).then_inc(gelu_cube, 1)

            def branch(h):
                four = slice(4 * h, 4 * h + 4)
                dve.wait_ge(gelu_tanh, h + 1)
                stt(rnnT[:, four, :], gel, 1.0, rnnT[:, four, :], ALU.add, ALU.mult).then_inc(gelu_done, 1)
                dve.wait_ge(gelu_done, h + 1)
                step.settle()
                step(stt(rnnT[:, four, 0:SEQ], gate_i[:, four, META:TP], 0.5, rnnT[:, four, 0:SEQ], ALU.mult, ALU.mult))
                stt(rnnT[:, four, SEQ:NTOK], gate_i[:, four, TP + GAP:TW], 0.5, rnnT[:, four, SEQ:NTOK], ALU.mult, ALU.mult)\
                    .then_inc(rnn_made, 1)

            dve.wait_ge(sink_in, 32)
            for c in range(CHUNKS + 1):
                if c < CHUNKS:
                    softmax_max(c)
                    softmax_norm(c)
                if c == HALF_GR + 1:
                    gelu_cubes(0)
                if c >= 1:
                    b = M.arrived(dve, ("PV", c - 1))
                    V.tensor_copy(attnT[:, :, CHUNK * (c - 1):CHUNK * c], b[:, 0:256].rearrange("p (h q) -> p h q", q=CHUNK))\
                        .then_inc(M.f_free(("PV", c - 1)), 1)
                if c < 4:
                    recurrence(2 * c)
                if c == HALF_GR + 2:
                    branch(0)
                for n, at in SPLIT_AT:
                    if c == at:
                        low_of(dve, SPLIT[n])
            gelu_cubes(1)
            low_of(dve, SPLIT[12])
            branch(1)
            for k, at in ((0, TP), (1, XPAD - GAP)):
                V.tensor_copy(stage[:, 24 * k:24 * k + 24].rearrange("p (j c) -> p c j", c=KD), xpad[:, :, at:at + GAP])
            V.tensor_copy(stage[:, 48:56], gate_i[:, :, TP - 1])
            V.tensor_copy(stage[:, 56:64], gate_i[:, :, TW - 1]).then_inc(tail_staged, 1)

            dve.wait_ge(zero_out, 16 * (NITEM - 1))
            dve.wait_ge(yb_out, 16)
            for p in range(0, KD, 2):
                for w, (gate, proj) in enumerate((("ga", "pa"), ("gr_gate", "pr"))):
                    for m in (p, p + 1):
                        M.emptied(dve, (gate, m))
                        b = M.arrived(dve, (proj, m))
                        stt(mtmp[m % 2][w], mtmp[m % 2][w], 1.0, b[:, 0:NTOK], ALU.add, ALU.mult)\
                            .then_inc(M.f_free((proj, m)), 1)
                    if p < KD - 2:
                        low_of(dve, SPLIT[13 + p + w])
                for m in (p, p + 1):
                    for proj in ("pa", "pr"):
                        M.emptied(dve, (proj, m))
                    tt(merged[:, m, :], mtmp[m % 2][0], mtmp[m % 2][1], ALU.add).then_inc(merge_made, 1)
            b = S.arrived(dve, "tail")
            V.tensor_copy(stage_rows[0:64, :], b[0:64, 0:P]).then_inc(S.f_free("tail"), 1)
            dve.wait_ge(scaled, 3)
            for j in range(3):
                n = OUT_ROWS[j]
                for h in range(2):
                    half = rows[0:n, j, 512 * h:512 * h + 512]
                    b = S.arrived(dve, ("out", j, h))
                    stt(half, b[0:n, :], 0.5, half, ALU.mult, ALU.add).then_inc(S.f_free(("out", j, h)), 1)
                    S.emptied(dve, ("out", j, h))
                moments(j, n)
                normed(1, j, n)

            def bc(ap, *shape):
                return ap.to_broadcast([P, *shape])

            def first_max(src, top, hot):
                alone(V.tensor_reduce(top, src, AX_X, ALU.max))
                alone(tt(hot, src, bc(top.unsqueeze(2), 3, 4), ALU.is_equal))
                alone(tt(hot, hot, bc(cst("tie").unsqueeze(1), 3, 4), ALU.mult))
                alone(V.tensor_reduce(tie_top, hot, AX_X, ALU.max))
                alone(tt(hot, hot, bc(tie_top.unsqueeze(2), 3, 4), ALU.is_equal))

            alone(V.memset(logit, 0.0))
            b = S.arrived(dve, "logits")
            step(V.tensor_copy(logit[:, 0:2, :], b[:, 0:40].rearrange("p (j e) -> p j e", e=20)))
            V.tensor_copy(logit[0:DEC, 2, :], b[0:DEC, 40:60]).then_inc(S.f_free("logits"), 1)
            step.settle()
            S.emptied(dve, "logits")
            glog, elog = logit[:, :, 0:NG], logit[:, :, NG:20].rearrange("p j (g e) -> p j g e", e=EPG)
            first_max(glog, g_top, g_hot)
            exi3 = exi[:, 0:12].rearrange("p (j g) -> p j g", g=NG)
            step(tt(exi3, glog, bc(g_top.unsqueeze(2), 3, 4), ALU.subtract))
            for j in range(3):
                step(tt(cross[:, j].rearrange("p g e -> p g e"), elog[:, j], bc(g_hot[:, j, :].unsqueeze(2), 4, 4), ALU.mult))
            step.settle()
            for j in range(3):
                step(V.tensor_reduce(e_sel[:, j, :], cross[:, j].rearrange("p g e -> p e g"), AX_X, ALU.add))
            step.settle()
            first_max(e_sel, top[0], hot[0])
            alone(stt(e_sel, hot[0], -1e30, e_sel, ALU.mult, ALU.add))
            first_max(e_sel, top[1], hot[1])
            tt(exi[:, 12:15], top[1], top[0], ALU.subtract).then_inc(lg_exp_in, 1)
            for k in range(2):
                for j in range(3):
                    step(tt(e_hot[k][:, j].rearrange("p (g e) -> p g e", e=EPG), bc(g_hot[:, j, :].unsqueeze(2), 4, 4),
                            bc(hot[k][:, j, :].unsqueeze(1), 4, 4), ALU.mult))
            step.settle()
            alone(tt(e_sum, e_hot[0], e_hot[1], ALU.add))
            tt(e_sum, e_sum, bc(cst("valid").unsqueeze(2), 3, NE), ALU.mult).then_inc(chosen, 1)
            dve.wait_ge(lg_exp, 1)
            step(V.tensor_reduce(g_top, exo[:, 0:12].rearrange("p (j g) -> p j g", g=NG), AX_X, ALU.add))
            step(ts(tie_top, exo[:, 12:15], 1.0, None, ALU.add))
            step.settle()
            alone(tt(g_top, g_top, tie_top, ALU.mult))
            alone(V.reciprocal(weight[0], g_top))
            alone(tt(weight[1], weight[0], exo[:, 12:15], ALU.mult))
            b = S.arrived(dve, "ranks")
            step(V.tensor_copy(rank, b[:, 0:3 * NE].rearrange("p (j e) -> p j e", e=NE)))
            V.tensor_copy(count_e, b[:, 3 * NE:4 * NE]).then_inc(S.f_free("ranks"), 1)
            step.settle()
            S.emptied(dve, "ranks")
            for m in range(1, LEVELS + 1):
                if m == 1:
                    step(ts(ov, count_e, float(CAP), None, ALU.is_gt))
                    step(ts(level, rank, float(CAP), None, ALU.is_ge))
                else:
                    step(stt(ov, count_e, float(CAP * m), ov, ALU.is_gt, ALU.add))
                    step(stt(level, rank, float(CAP * m), level, ALU.is_ge, ALU.add))
                step.settle()
            step(V.tensor_tensor_scan(ov_end, ones[:, 0:NE], ov, 0.0, ALU.mult, ALU.add))
            step(ts(past, level, 1.0, None, ALU.min))
            step(stt(spot[:, 1], level, -float(CAP), rank, ALU.mult, ALU.add))
            step.settle()
            alone(stt(base, ov_end, float(NE - 1), ov, ALU.add, ALU.subtract))
            alone(tt(base, base, cst("expert"), ALU.subtract))
            alone(tt(level, level, bc(base.unsqueeze(1), 3, NE), ALU.add))
            alone(tt(level, level, past, ALU.mult))
            alone(tt(spot[:, 0], level, bc(cst("expert").unsqueeze(1), 3, NE), ALU.add))
            for w in range(2):
                for k in range(2):
                    step(tt(e_pick[:, w, k], e_hot[k], spot[:, w], ALU.mult))
            step.settle()
            alone(V.tensor_reduce(place, e_pick.rearrange("p w k j e -> p (w k j) e"), AX_X, ALU.add))
            item_of, rank_of = place[:, 0:6], place[:, 6:12]
            rh = rank_hot.rearrange("p k (j c) -> p (k j) c", c=CAP)
            ih = item_hot.rearrange("p k (j i) -> p (k j) i", i=NITEM)
            step(tt(ih, bc(cst("iota_item").unsqueeze(1), 6, NITEM), bc(item_of.unsqueeze(2), 6, NITEM), ALU.is_equal))
            step(tt(rh, bc(cst("iota_cap").unsqueeze(1), 6, CAP), bc(rank_of.unsqueeze(2), 6, CAP), ALU.is_equal))
            step(stt(slot_f, item_of, float(CAP), rank_of, ALU.mult, ALU.add))
            step.settle()
            for k in range(2):
                inst = tt(ih[:, 3 * k:3 * k + 3], ih[:, 3 * k:3 * k + 3], bc(cst("token").unsqueeze(2), 3, NITEM), ALU.mult)
                if k == 0:
                    step(inst)
            inst.then_inc(selected, 1)
            step(V.tensor_copy(slot_i[:, :, :].rearrange("p k j -> p (k j)"), slot_f))
            alone(tt(ov_cmp, bc(ov_end.unsqueeze(1), NOV, NE), bc(cst("iota_ov").unsqueeze(2), NOV, NE), ALU.is_le))
            alone(V.tensor_reduce(ov_exp, ov_cmp, AX_X, ALU.add))
            alone(ts(ov_exp, ov_exp, float(NE - 1), None, ALU.min))
            step(V.tensor_copy(ctrl_i[:, 0:NOV], ov_exp))
            step(V.tensor_copy(ctrl_i[:, W_COUNT:W_REST], ov_end[:, NE - 1:NE]))
            alone(ts(ov, count_e, float(FIRST), None, ALU.is_gt))
            alone(V.tensor_tensor_scan(ov_end, ones[:, 0:NE], ov, 0.0, ALU.mult, ALU.add))
            step(V.tensor_copy(ctrl_i[:, W_REST:W_BEFORE], ov))
            step(V.tensor_copy(ctrl_i[:, W_TOTAL:NWORD], ov_end[:, NE - 1:NE]))
            tt(ctrl_i[:, W_BEFORE:W_TOTAL], ov_end, ov, ALU.subtract).then_inc(ctrl_done, 1)
            dve.wait_ge(ctrl_done, 1)
            b = S.arrived(dve, "index")
            V.tensor_copy(index_i[0:CAP, :], b[0:CAP, 0:NITEM]).then_inc(route_done, 1)
            dve.wait_ge(route_done, 1)

            def columns(i, s):
                dve.wait_ge(xt_full, i + 1)
                for h in range(2):
                    cp = V.tensor_copy(xT[s][:, 4 * h:4 * h + 4, :], TB[h][:, 0:4 * CAP].rearrange("p (k c) -> p k c", c=CAP))
                cp.then_inc(xt_made, 1)

            def silu(i, th, out, gate, up, tanh, half, made):
                dve.wait_ge(tanh, i + 1)
                stt(th, th, 1.0, gate, ALU.add, ALU.mult).then_inc(half, 1)
                dve.wait_ge(half, i + 1)
                stt(out, th, 0.5, up, ALU.mult, ALU.mult).then_inc(made, 1)

            def silu_first(i, s):
                silu(i, th_a, hid_a, HB[s][:, 0:256], HB[s][:, 256:512], ha_tanh, ha_half, ha_made)

            def hidden_columns(i):
                dve.wait_ge(hta_full, i + 1)
                V.tensor_copy(hT_a, TH[:, 0:256]).then_inc(hta_made, 1)

            def rest(b):
                silu(b, th_b, hid_b, BB[:, 0:P], BB[:, P:2 * P], hb_tanh, hb_half, hb_made)
                dve.wait_ge(htb_full, b + 1)
                V.tensor_copy(hT_b, BB[:, 2 * P:3 * P]).then_inc(htb_made, 1)

            def maybe_rest(i):
                has, b = rest_words(dve, i)
                with dve.If(has > 0):
                    rest(b)

            columns(0, 0)

            def round_of(n):
                for s in range(3):
                    i = 3 * n + s
                    silu_first(i, s)
                    columns(i + 1, (s + 1) % 3)
                    maybe_rest(i)
                    hidden_columns(i)

            with dve.Fori(0, NE // 3) as n:
                round_of(n)
            silu_first(NE - 1, 0)
            maybe_rest(NE - 1)
            hidden_columns(NE - 1)
            count, total = overflow_words(dve)
            with dve.If(count > 0):
                with dve.Fori(0, count) as v:
                    columns(v + NE, 1)
                    silu_first(v + NE, 1)
                    rest(total + v)
                    hidden_columns(v + NE)

            dve.wait_ge(rows_scaled2, 3)
            for j in range(4):
                if j < 3:
                    n = OUT_ROWS[j]
                    dve.wait_ge(yg_in[j], 32)
                    for k in range(2):
                        alone(stt(rows[0:n, j, :], yg[j][k][0:n, :], weight[k][0:n, j:j + 1], rows[0:n, j, :], ALU.mult, ALU.add))
                    moments(j, n)
                if j > 0:
                    normed(2, j - 1, OUT_ROWS[j - 1])


INPUTS = ["x_prompt", "x_sample", "cache_meta_k", "cache_meta_v", "cache_win_k", "cache_win_v", "state_conv", "state_h",
          "meta_tokens", "ln_in_g", "ln_in_b", "w_in", "b_gate", "attn_sinks", "conv_w", "conv_b", "w_rg_a", "b_rg_a",
          "w_rg_x", "b_rg_x", "lru_lambda", "w_branch_attn", "w_branch_rnn", "w_out", "ln1_g", "ln1_b", "w_group",
          "b_group", "w_router", "b_router", "w_gate", "w_up", "w_down", "ln2_g", "ln2_b"]
OUTPUTS = [(1, SEQ, D), (1, DEC, D), (1, 1, META, NKV, HD), (1, 1, META, NKV, HD), (1, 1, WIN, NKV, HD),
           (1, 1, WIN, NKV, HD), (1, 1, GAP, D), (1, 1, D), (1, 1, DEC, NKV, HD), (1, 1, DEC, NKV, HD),
           (1, 1, GAP, D), (1, 1, D)]


def kernel(**inputs):
    import concourse.bacc as bacc
    from concourse.bass_utils import run_bass_kernel_spmd

    nc = bacc.Bacc("TRN2", target_bir_lowering=False, num_devices=1)
    arrays, aps = {}, {}
    for name in INPUTS:
        arrays[f"in_{name}"] = np.ascontiguousarray(inputs[name])
    arrays["in_const"] = constants()
    for key, a in arrays.items():
        aps[key[3:]] = nc.dram_tensor(key, a.shape, F32, kind="ExternalInput").ap()
    outs = [nc.dram_tensor(f"out_{i}", shape, F32, kind="ExternalOutput").ap() for i, shape in enumerate(OUTPUTS)]
    build(nc, aps, outs)
    r = run_bass_kernel_spmd(nc, [arrays], core_ids=[0])
    return tuple(r.results[0][f"out_{i}"] for i in range(len(OUTPUTS)))
```
